# Optimizing a Trainium2 kernel written in Bass

```python
import math
import jax, jax.numpy as jnp
from jax import lax
import numpy as np

D_MODEL = 1024
BATCH = 1
SEQ = 1024
DEPTH = 2
DEC_BATCH = 8
DEC_SEQ = 16
PAST_LEN = 512

CHUNK = 64
QBLOCK = 128
EPS = 1e-6
NEG = -1e30

CONV_W = 256
CONV_K = 3
MLA_HEADS = 4
Q_LORA = 256
KV_LORA = 128
QK_NOPE = 128
QK_ROPE = 64
V_HEAD = 128
MLA_W = MLA_HEADS * V_HEAD
MLA_THETA = 10000.0
MLA_SCALE = (QK_NOPE + QK_ROPE) ** -0.5
SWA_HEADS = 4
SWA_KV_HEADS = 2
SWA_G = SWA_HEADS // SWA_KV_HEADS
SWA_HD = 64
SWA_W = SWA_HEADS * SWA_HD
WINDOW = 128
SWA_CACHE = WINDOW - CHUNK
SWA_THETA = 150000.0

D_MIX = CONV_W + MLA_W + SWA_W
IN_SIZES = (CONV_W, CONV_W, CONV_W, CONV_W,
            Q_LORA, KV_LORA, QK_ROPE, MLA_W,
            SWA_HEADS * SWA_HD, SWA_KV_HEADS * SWA_HD, SWA_KV_HEADS * SWA_HD, SWA_W)
D_IN = sum(IN_SIZES)

kernel_name = "hybrid_stream_conv_mla_swasink_step"

def _split_points():
    pts, acc = [], 0
    for s in IN_SIZES[:-1]:
        acc += s
        pts.append(acc)
    return pts

def rmsnorm(x, g):
    x32 = x.astype(jnp.float32)
    y = x32 * lax.rsqrt(jnp.mean(x32 * x32, axis=-1, keepdims=True) + EPS)
    return (y * g.astype(jnp.float32)).astype(x.dtype)

def rope(x, pos, theta):
    half = x.shape[-1] // 2
    inv = theta ** (-jnp.arange(half, dtype=jnp.float32) / half)
    ang = pos.astype(jnp.float32)[:, None] * inv[None, :]
    shape = (ang.shape[0],) + (1,) * (x.ndim - 3) + (half,)
    cos = jnp.cos(ang).reshape(shape)
    sin = jnp.sin(ang).reshape(shape)
    x1 = x[..., :half].astype(jnp.float32)
    x2 = x[..., half:].astype(jnp.float32)
    return jnp.concatenate([x1 * cos - x2 * sin, x1 * sin + x2 * cos], axis=-1).astype(x.dtype)

def causal_conv3(u, buf, w):
    T = u.shape[1]
    ua = jnp.concatenate([buf.astype(u.dtype), u], axis=1)
    y = w[0] * ua[:, 0:T] + w[1] * ua[:, 1:T + 1] + w[2] * ua[:, 2:T + 2]
    return y, ua[:, -(CONV_K - 1):]

def mla_attention(q_nope, q_rope, k_nope, k_rope, v, mask):
    s = (jnp.einsum('bqhd,bkhd->bhqk', q_nope, k_nope)
         + jnp.einsum('bqhd,bkd->bhqk', q_rope, k_rope)).astype(jnp.float32) * MLA_SCALE
    if mask is not None:
        s = jnp.where(mask[None, None], s, NEG)
    p = jax.nn.softmax(s, axis=-1)
    return jnp.einsum('bhqk,bkhd->bqhd', p.astype(v.dtype), v)

def sink_attention(q, k, v, sink, mask):
    s = jnp.einsum('bnqhgd,bnkhd->bnhgqk', q, k).astype(jnp.float32) * (q.shape[-1] ** -0.5)
    if mask is not None:
        s = jnp.where(mask[None, :, None, None], s, NEG)
    sk = sink.astype(jnp.float32).reshape(SWA_KV_HEADS, SWA_G)[None, None, :, :, None, None]
    m = jnp.maximum(jnp.max(s, axis=-1, keepdims=True), sk)
    p = jnp.exp(s - m)
    p = p / (jnp.sum(p, axis=-1, keepdims=True) + jnp.exp(sk - m))
    return jnp.einsum('bnhgqk,bnkhd->bnqhgd', p.astype(v.dtype), v)

def hybrid_layer(x, c, pos, norm_g, w_mod, b_mod, w_in, conv_w, q_norm_g, kv_norm_g,
                 w_uq, w_ukv, swa_sink, w_out, past):
    B, T, _ = x.shape
    mod = jax.nn.silu(c) @ w_mod + b_mod
    shift, scale, gate = jnp.split(mod, 3, axis=-1)
    h = rmsnorm(x, norm_g) * (1.0 + scale[:, None]) + shift[:, None]
    z = h @ w_in
    (cv_h, cv_b, cv_c, cv_g, m_q, m_kv, m_kr, m_g, s_q, s_k, s_v, s_g) = jnp.split(z, _split_points(), axis=-1)

    buf = jnp.zeros((B, CONV_K - 1, CONV_W), x.dtype) if past is None else past[0]
    cy, conv_state = causal_conv3(cv_c * cv_h, buf, conv_w)
    out_conv = cv_b * cy * jax.nn.silu(cv_g)

    cq = rmsnorm(m_q, q_norm_g)
    qm = (cq @ w_uq).reshape(B, T, MLA_HEADS, QK_NOPE + QK_ROPE)
    q_nope = qm[..., :QK_NOPE]
    q_rope = rope(qm[..., QK_NOPE:], pos, MLA_THETA)
    ckv = rmsnorm(m_kv, kv_norm_g)
    krope = rope(m_kr, pos, MLA_THETA)
    if past is None:
        ckv_all, kr_all = ckv, krope
    else:
        ckv_all = jnp.concatenate([past[1].astype(ckv.dtype), ckv], axis=1)
        kr_all = jnp.concatenate([past[2].astype(krope.dtype), krope], axis=1)
    kv = (ckv_all @ w_ukv).reshape(B, ckv_all.shape[1], MLA_HEADS, QK_NOPE + V_HEAD)
    k_nope, v_mla = kv[..., :QK_NOPE], kv[..., QK_NOPE:]
    if past is None:
        nb = T // QBLOCK
        qn_b = jnp.moveaxis(q_nope.reshape(B, nb, QBLOCK, MLA_HEADS, QK_NOPE), 1, 0)
        qr_b = jnp.moveaxis(q_rope.reshape(B, nb, QBLOCK, MLA_HEADS, QK_ROPE), 1, 0)
        key_chunk = jnp.arange(T) // CHUNK

        def one_block(args):
            qn, qr, i = args
            q_chunk = (i * QBLOCK + jnp.arange(QBLOCK)) // CHUNK
            mask = key_chunk[None, :] <= q_chunk[:, None]
            return mla_attention(qn, qr, k_nope, kr_all, v_mla, mask)

        o = lax.map(one_block, (qn_b, qr_b, jnp.arange(nb)))
        o_mla = jnp.moveaxis(o, 0, 1).reshape(B, T, MLA_W)
    else:
        o_mla = mla_attention(q_nope, q_rope, k_nope, kr_all, v_mla, None).reshape(B, T, MLA_W)
    out_mla = o_mla * jax.nn.silu(m_g)

    q = rope(s_q.reshape(B, T, SWA_HEADS, SWA_HD), pos, SWA_THETA)
    k = rope(s_k.reshape(B, T, SWA_KV_HEADS, SWA_HD), pos, SWA_THETA)
    v = s_v.reshape(B, T, SWA_KV_HEADS, SWA_HD)
    if past is None:
        nc = T // CHUNK
        qb = q.reshape(B, nc, CHUNK, SWA_KV_HEADS, SWA_G, SWA_HD)
        kc = k.reshape(B, nc, CHUNK, SWA_KV_HEADS, SWA_HD)
        vc = v.reshape(B, nc, CHUNK, SWA_KV_HEADS, SWA_HD)
        pad = ((0, 0), (1, 0), (0, 0), (0, 0), (0, 0))
        k_band = jnp.concatenate([jnp.pad(kc, pad)[:, :nc], kc], axis=2)
        v_band = jnp.concatenate([jnp.pad(vc, pad)[:, :nc], vc], axis=2)
        valid = (jnp.arange(nc)[:, None] > 0) | (jnp.arange(2 * CHUNK)[None, :] >= CHUNK)
        o_swa = sink_attention(qb, k_band, v_band, swa_sink, valid[:, None, :]).reshape(B, T, SWA_W)
        swa_k_state, swa_v_state = k[:, T - SWA_CACHE:], v[:, T - SWA_CACHE:]
    else:
        k_all = jnp.concatenate([past[3].astype(k.dtype), k], axis=1)[:, None]
        v_all = jnp.concatenate([past[4].astype(v.dtype), v], axis=1)[:, None]
        qb = q.reshape(B, 1, T, SWA_KV_HEADS, SWA_G, SWA_HD)
        o_swa = sink_attention(qb, k_all, v_all, swa_sink, None).reshape(B, T, SWA_W)
        swa_k_state, swa_v_state = k, v
    out_swa = o_swa * jax.nn.silu(s_g)

    out = jnp.concatenate([out_conv, out_mla, out_swa], axis=-1) @ w_out
    x = x + gate[:, None] * out
    return x, (conv_state, ckv, krope, swa_k_state, swa_v_state)

def setup_inputs(seed: int = 0) -> dict:
    key = jax.random.key(seed)
    ks = jax.random.split(key, 21)

    def nrm(k, shape, scale):
        return jax.random.normal(k, shape, jnp.float32) * scale

    return {
        "x_prompt": nrm(ks[0], (BATCH, SEQ, D_MODEL), 1.0),
        "x_sample": nrm(ks[1], (DEC_BATCH, DEC_SEQ, D_MODEL), 1.0),
        "c_prompt": nrm(ks[2], (BATCH, D_MODEL), 1.0),
        "c_sample": nrm(ks[3], (DEC_BATCH, D_MODEL), 1.0),
        "cache_conv": nrm(ks[4], (DEPTH, DEC_BATCH, CONV_K - 1, CONV_W), 1.0),
        "cache_mla_ckv": nrm(ks[5], (DEPTH, DEC_BATCH, PAST_LEN, KV_LORA), 1.0),
        "cache_mla_krope": nrm(ks[6], (DEPTH, DEC_BATCH, PAST_LEN, QK_ROPE), 1.0),
        "cache_swa_k": nrm(ks[7], (DEPTH, DEC_BATCH, SWA_CACHE, SWA_KV_HEADS, SWA_HD), 1.0),
        "cache_swa_v": nrm(ks[8], (DEPTH, DEC_BATCH, SWA_CACHE, SWA_KV_HEADS, SWA_HD), 1.0),
        "norm_g": 1.0 + nrm(ks[9], (DEPTH, D_MODEL), 0.05),
        "w_mod": nrm(ks[10], (DEPTH, D_MODEL, 3 * D_MODEL), D_MODEL ** -0.5),
        "b_mod": nrm(ks[11], (DEPTH, 3 * D_MODEL), 0.01),
        "w_in": nrm(ks[12], (DEPTH, D_MODEL, D_IN), D_MODEL ** -0.5),
        "conv_w": nrm(ks[13], (DEPTH, CONV_K, CONV_W), CONV_K ** -0.5),
        "q_norm_g": 1.0 + nrm(ks[14], (DEPTH, Q_LORA), 0.05),
        "kv_norm_g": 1.0 + nrm(ks[15], (DEPTH, KV_LORA), 0.05),
        "w_uq": nrm(ks[16], (DEPTH, Q_LORA, MLA_HEADS * (QK_NOPE + QK_ROPE)), Q_LORA ** -0.5),
        "w_ukv": nrm(ks[17], (DEPTH, KV_LORA, MLA_HEADS * (QK_NOPE + V_HEAD)), KV_LORA ** -0.5),
        "swa_sink": nrm(ks[18], (DEPTH, SWA_HEADS), 1.0),
        "w_out": nrm(ks[19], (DEPTH, D_MIX, D_MODEL), D_MIX ** -0.5),
        "final_norm_g": 1.0 + nrm(ks[20], (D_MODEL,), 0.05),
    }

def reference(x_prompt, x_sample, c_prompt, c_sample, cache_conv, cache_mla_ckv, cache_mla_krope,
              cache_swa_k, cache_swa_v, norm_g, w_mod, b_mod, w_in, conv_w, q_norm_g, kv_norm_g,
              w_uq, w_ukv, swa_sink, w_out, final_norm_g):
    past_len = cache_mla_ckv.shape[2]
    pos_p = jnp.arange(x_prompt.shape[1], dtype=jnp.int32)
    pos_s = past_len + jnp.arange(x_sample.shape[1], dtype=jnp.int32)

    xp, xs = x_prompt, x_sample
    st_p, st_s = [], []
    for i in range(DEPTH):
        xp, sp = hybrid_layer(xp, c_prompt, pos_p, norm_g[i], w_mod[i], b_mod[i], w_in[i], conv_w[i],
                              q_norm_g[i], kv_norm_g[i], w_uq[i], w_ukv[i], swa_sink[i], w_out[i], None)
        past = (cache_conv[i], cache_mla_ckv[i], cache_mla_krope[i], cache_swa_k[i], cache_swa_v[i])
        xs, ss = hybrid_layer(xs, c_sample, pos_s, norm_g[i], w_mod[i], b_mod[i], w_in[i], conv_w[i],
                              q_norm_g[i], kv_norm_g[i], w_uq[i], w_ukv[i], swa_sink[i], w_out[i], past)
        st_p.append(sp)
        st_s.append(ss)

    y_prompt = rmsnorm(xp, final_norm_g)
    y_sample = rmsnorm(xs, final_norm_g)
    conv_p = jnp.stack([s[0] for s in st_p])
    conv_s = jnp.stack([s[0] for s in st_s])
    ckv_p = jnp.stack([s[1] for s in st_p])
    ckv_s = jnp.stack([s[1] for s in st_s])
    kr_p = jnp.stack([s[2] for s in st_p])
    kr_s = jnp.stack([s[2] for s in st_s])
    sk_p = jnp.stack([s[3] for s in st_p])
    sk_s = jnp.stack([s[3] for s in st_s])
    sv_p = jnp.stack([s[4] for s in st_p])
    sv_s = jnp.stack([s[4] for s in st_s])
    return (y_prompt, y_sample, conv_p, conv_s, ckv_p, ckv_s, kr_p, kr_s, sk_p, sk_s, sv_p, sv_s)


_drawn_inputs = setup_inputs


def setup_inputs(seed=0):
    import zlib

    import numpy as np

    out = dict(_drawn_inputs(seed))
    spreads = {}
    factors = {'cache_mla_krope': 3.418, 'q_norm_g': 8.0, 'swa_sink': 8.0}
    for name, (base, spread) in spreads.items():
        noise = np.random.default_rng([zlib.crc32(name.encode()), seed]).standard_normal(out[name].shape)
        drawn = base * np.exp(spread * noise) if base else spread * noise
        out[name] = __import__('jax').numpy.asarray(drawn.astype(out[name].dtype))
    for name, factor in factors.items():
        out[name] = (out[name] * factor).astype(out[name].dtype)
    return out
```

```python
import numpy as np
import concourse.bass as bass
from concourse import mybir

F32 = mybir.dt.float32
F32R = mybir.dt.float32r
BF16 = mybir.dt.bfloat16
ACT = mybir.ActivationFunctionType
ALU = mybir.AluOpType
AX = mybir.AxisListType

P = 128
D = 1024
KD = D // P
DEPTH = 2
SEQ, NB, TS = 1024, 8, 16
NTOK = SEQ + NB * TS
TILES = NTOK // P
ST = TILES - 1
PAST = 512
BLK = 384
NBLK = NTOK // BLK
D_IN = 2752
EPS = 1e-6
NEG = -1e30
HEADS = 4
MLA_SCALE = (128 + 64) ** -0.5
SWA_SCALE = 64 ** -0.5
CH = 64
CONVW = 256

KV_KR, Q_LAT, SK_SV, S_Q, S_G, M_G0, M_G1, CV_H, CV_C, CV_B, CV_G = range(11)
PAIRS = [(1280, 192), (1024, 256), (2240, 256), (1984, 256), (2496, 256), (1472, 256), (1728, 256),
         (0, 256), (512, 256), (256, 256), (768, 256)]
NIN, NOUT = 2 * len(PAIRS), KD
NCHUNK = NIN + NOUT
ACT_CHUNKS = [c for c in range(NIN) if c // 2 in (KV_KR, Q_LAT, S_Q, S_G, M_G0, M_G1, CV_G) or c == 2 * SK_SV]
SPLIT_AFTER = S_G + 1

LOADS = ([("mod", i) for i in range(8)] + [("in", i) for i in range(len(PAIRS))]
         + [("mod", i) for i in range(8, 12)] + [("out", i) for i in range(NOUT // 2)])
LOAD_AT = {x: n for n, x in enumerate(LOADS)}

V_G, V_BMOD, V_QG, V_KVG, V_CONV, V_ROWS = 0, 8, 32, 34, 35, 41

SLOTS = 6


def plan_attention():
    groups, job, unit = [], 0, 0

    def add(kind, idx, jobs, keys):
        nonlocal job, unit
        units = 1 if kind == "mla_s" else len(keys)
        groups.append(dict(kind=kind, idx=idx, jobs=list(range(job, job + jobs)), keys=keys,
                           units=list(range(unit, unit + units))))
        job += jobs
        unit += units

    for t in range(ST):
        add("swa_p", t, 1, [t - 1, t] if t else [t])
    add("swa_s", ST, HEADS, list(range(5)))
    for t in range(ST):
        add("mla_p", t, HEADS, list(range(t + 1)))
    for b in range(NB):
        add("mla_s", b, 1, list(range(5)))
    return groups, job, unit


GROUPS, NJOBS, NUNITS = plan_attention()
GROUP_OF = {j: g for g in GROUPS for j in g["jobs"]}
LAST = len(GROUPS) - 1
N_SWA = sum(g["kind"][:3] == "swa" for g in GROUPS)
N_MLA = len(GROUPS) - N_SWA

N_STORES = 10
DVE_STEPS, ACT_STEPS = 207, 89


class Signal:

    def __init__(self, nc, name, per, first=0):
        self.sem, self.per, self.name, self.first = nc.alloc_semaphore(name), per, name, first

    def at(self, layer, k):
        return layer * self.per + k + self.first


class Lane:

    def __init__(self, eng, layer, own=None):
        self.eng, self.layer, self.own, self.count = eng, layer, own, {}

    def wait(self, sig, k):
        self.eng.wait_ge(sig.sem, sig.at(self.layer, k))

    def link(self, ins, sig=None):
        sig = sig or self.own
        ins.then_inc(sig.sem, 1)
        self.count[sig.name] = self.count.get(sig.name, 0) + 1
        self.wait(sig, self.count[sig.name])


def build(nc, io):
    H_AT, X_AT, G_AT, RAW_AT, SPL_AT, TAB_AT, ZT_AT, SM_AT = (
        0, 73728, 115200, 152064, 168448, 184832, 194048, 203424)

    base = -(-nc.sbuf_base // 32) * 32

    def at(name, off, shape, dt=F32):
        return nc.alloc_sbuf_tensor_at(name, shape, dt, offset=base + off)

    h_hi = at("h_hi", H_AT, [P, KD, NTOK], F32R)
    h_lo = at("h_lo", H_AT + 36864, [P, KD, NTOK], F32R)
    x = at("x", X_AT, [P, KD, NTOK])
    vrows = at("vrows", X_AT + 36864, [V_ROWS, P])
    ccrow = at("ccrow", X_AT + 37376, [2 * NB, CONVW])
    cq = at("cq", X_AT, [P, 2, NTOK])
    ckvT = at("ckvT", X_AT + 9216, [P, NTOK])
    ckv = at("ckv", X_AT + 13824, [P, TILES, P])
    krT = at("krT", X_AT + 18432, [P, NTOK])
    sqT = at("sqT", X_AT + 23040, [P, 2, NTOK])
    skT = at("skT", X_AT + 32256, [P, NTOK])
    sv = at("sv", X_AT + 36864, [P, TILES, P])
    raw_ckv = at("raw_ckv", X_AT, [P, 2, 4, P])
    raw_kr = at("raw_kr", X_AT + 4096, [P, 2, 4, P])
    mix = at("mix", G_AT, [P, KD, NTOK])
    tok = at("tok", G_AT, [P, TILES, D])
    raw = at("raw", RAW_AT, [P, 2, KD, 256])
    w_hi = [at(f"w_hi{s}", SPL_AT + 8192 * s, [P, KD, P], F32R) for s in range(2)]
    w_lo = [at(f"w_lo{s}", SPL_AT + 8192 * s + 4096, [P, KD, P], F32R) for s in range(2)]
    w_uq = at("w_uq", SPL_AT, [P, 2, 768])
    w_ukT = at("w_ukT", SPL_AT + 6144, [P, HEADS, P])
    w_ukv = at("w_ukv", SPL_AT + 8192, [P, HEADS, 256])
    kr_tok = at("kr_tok", SPL_AT + 12288, [P, TILES, 64])
    sk_tok = at("sk_tok", SPL_AT + 14592, [P, 2, P])
    crow = at("crow", SPL_AT, [1 + NB, D])
    frow = at("frow", SPL_AT + 8192, [KD, P])
    csil = at("csil", SPL_AT + 4096, [1 + NB, D])
    tab = at("tab", TAB_AT, [P, 2, NTOK])
    qas = at("qas", TAB_AT, [P, NB, 64])
    rot = at("rot", ZT_AT, [P, NTOK])
    svT = at("svT", ZT_AT + 4608, [P, NTOK])
    UW = 2 + SEQ + NB * (TS + 2)
    u = at("u", ZT_AT, [P, 2, UW])
    qn = at("qn", ZT_AT + 4608, [P, 2, BLK])
    probs = at("probs", H_AT, [P, SLOTS, 1024])
    qa = at("qa", H_AT + 24576, [P, HEADS, NTOK])
    qr = at("qr", H_AT + 43008, [P, 2, NTOK])
    pT = at("pT", H_AT + 52224, [P, 3, 512])
    oL = at("oL", H_AT + 58368, [P, 2, HEADS, P])
    ckvT_c = at("ckvT_c", H_AT + 62464, [P, 512])
    krT_c = at("krT_c", H_AT + 64512, [P, 512])
    sk_c = at("sk_c", H_AT + 66560, [P, 4, P])
    sv_c = at("sv_c", H_AT + 68608, [P, 4, P])
    skT_c = at("skT_c", H_AT + 70656, [P, 512])

    small = [SM_AT]

    def sm(name, shape, dt=F32):
        size = int(np.prod(shape[1:])) * (2 if dt == BF16 else 4)
        t = at(name, small[0], shape, dt)
        small[0] += -(-size // 32) * 32
        return t

    ident = sm("ident", [P, P])
    ones = sm("ones", [P, 1])
    mhalf = sm("mhalf", [P, TILES])
    vec = sm("vec", [P, V_ROWS])
    convc = sm("convc", [P, 2, 2 * NB])
    mod = sm("mod", [P, 3, KD, 1 + NB])
    amul = sm("amul", [P, KD, 1 + NB])
    cT = sm("cT", [P, KD, 1 + NB])
    fing = sm("fing", [P, KD])
    sink = sm("sink", [P, HEADS])
    nsink = sm("nsink", [P, HEADS])
    state = sm("state", [P, 2, 2 + 2 * NB])
    masks = sm("masks", [8, 128 + 640 + 128 + 256 + 512], BF16)
    mean = sm("mean", [P, TILES])
    rstd = sm("rstd", [P, TILES])
    meanl = sm("meanl", [P, 2, TILES])
    rstdl = sm("rstdl", [P, 2, TILES])
    qrs = sm("qrs", [P, NB, 64])
    state_tok = at("state_tok", H_AT + 72704, [2 + 2 * NB, CONVW])
    smax = sm("smax", [P, SLOTS, HEADS])
    nmax = sm("nmax", [P, SLOTS, HEADS])
    esink = sm("esink", [P, SLOTS, HEADS])
    psum_p = sm("psum_p", [P, SLOTS, HEADS])
    rinv = sm("rinv", [P, SLOTS, HEADS])
    assert base + small[0] <= nc.sbuf_usable_end, small[0]
    masks_f = at("masks_f", H_AT, [8, masks.shape[1]])
    own64 = masks[:, 1152:1664]
    own8, block_mask, half_rows, band_mask = (masks[:, 0:128], masks[:, 128:768], masks[:, 768:896],
                                              masks[:, 896:1152])

    psum = nc.alloc_psum_tensor("psum", [P, 8, 512], F32)
    xT = nc.dram_tensor("xT_scratch", (P, KD, NTOK), F32).ap()

    def sg(name, per=0, first=0):
        return Signal(nc, name, per, first)

    n_mod, n_ptile = 12, NUNITS
    weights_in = []
    slot_total = [0, 0]
    for n, (kind, i) in enumerate(LOADS):
        slot_total[n % 2] += 48 if kind == "out" else 32 if (kind, i) == ("in", CV_H) else 16
        weights_in.append((n % 2, slot_total[n % 2]))
    w_in = [sg(f"weights_landed{s}", slot_total[s]) for s in range(2)]
    vec_in = sg("vectors_landed", 16 * 7)
    tab_in = sg("rope_table_landed", 16 * 3)
    uq_in = sg("w_uq_landed", 64)
    ukv_in = sg("w_ukv_landed", 16)
    swc_in = sg("swa_cache_landed", 32)
    mlc_in = [sg(f"mla_cache_landed{s}", 48 * NB // 2) for s in range(2)]
    x_in = [sg(f"residual_landed{s}", 16) for s in range(2)]
    x_out = sg("residual_stored", 16 * KD, 16)
    outs = sg("states_stored", 16 * N_STORES)
    small_T = sg("vectors_turned", 1)
    small_v = sg("vectors_ready", 2)
    sq_x = sg("x_squared", NBLK)
    sum_x = sg("x_summed", NBLK)
    mean_x = sg("x_mean_ready", NBLK, 1)
    rstd_x = sg("x_rstd_ready", NBLK)
    bc_x = sg("x_rstd_spread", NBLK, 1)
    scaled_x = sg("x_scaled", NBLK, 1)
    mod_mm = sg("modulation_summed", n_mod)
    mod_v = sg("modulation_ready", 2)
    h_act = sg("h_modulated", NBLK)
    h_smp = sg("h_sample_modulated", 1)
    hi_h = sg("h_hi_ready", 2 * NBLK)
    lo_h = sg("h_lo_ready", 2 * NBLK, 1)
    hi_w = sg("w_hi_ready", NCHUNK)
    lo_w = sg("w_lo_ready", NCHUNK, 1)
    z_done = sg("chunk_summed", NCHUNK, 1)
    z_act = sg("chunk_read_by_scalar", len(ACT_CHUNKS))
    z_dve = sg("chunk_read_by_vector", NCHUNK, 1)
    roped = sg("rope_done", 4 + 2 * NBLK, 1)
    lat_sum = sg("latents_summed", 1)
    lat_mean = sg("latent_means_ready", 2)
    lat_rstd = sg("latent_rstds_ready", 2)
    lat_bc = sg("latent_rstds_spread", 2 * NBLK, 1)
    lat_ok = sg("latents_normed", 2 * NBLK)
    svt_T = sg("swa_values_turned", 3)
    svt_c = sg("swa_values_copied", 3)
    turn_T = sg("states_turned", 7)
    turn_c = sg("states_copied", 7)
    qr_mm = sg("q_rope_summed", 2 * NBLK)
    qr_rot = sg("q_rope_rotated", 2 * NBLK)
    qn_mm = sg("q_nope_summed", HEADS * NBLK)
    qn_c = sg("q_nope_copied", HEADS * NBLK)
    qa_mm = sg("q_latent_summed", HEADS * NBLK)
    qa_c = sg("q_latent_copied", HEADS * NBLK)
    qas_ok = sg("q_latent_sample_ready", 2)
    qrs_ok = sg("q_rope_sample_ready", 1, 1)
    score = sg("scores_ready", NJOBS)
    negmax = sg("negmax_ready", NJOBS)
    expd = sg("exp_ready", NJOBS)
    p_ok = sg("probs_ready", NJOBS)
    pt_T = sg("probs_turned", NUNITS)
    pt_c = [sg("probs_turned_copied_by_scalar", (NUNITS + 1) // 2), sg("probs_turned_copied_by_vector", NUNITS // 2)]
    pv = sg("values_weighted", NUNITS)
    swa_ok = sg("swa_gated", N_SWA)
    ol_c = sg("latent_out_copied", N_MLA)
    uv_mm = sg("mla_out_summed", TILES)
    uv_ok = sg("mla_gated", TILES, 1)
    ct_T = sg("caches_turned", 1 + 2 * NB)
    ct_c = sg("caches_copied", 1 + 2 * NB)
    act_step = sg("scalar_step", ACT_STEPS)
    dve_step = sg("vector_step", DVE_STEPS)
    s_const = sg("constants_landed")
    s_tok = [sg(f"tokens_landed{i}") for i in range(3)]
    s_c = sg("c_landed")
    s_cs = sg("c_silu")
    s_cT = sg("c_turned")
    s_xT = sg("tokens_turned")
    s_xa = sg("tokens_copied_by_scalar")
    s_xv = sg("tokens_copied_by_vector")
    s_cst = sg("constants_made")
    s_y = sg("y_normed")
    s_yT = sg("y_turned")
    s_ya = sg("y_copied_by_scalar")
    s_yv = sg("y_copied_by_vector")
    s_out = sg("y_stored")

    def zset(c):
        return psum[:, 3 * (c % 2):3 * (c % 2) + 3, 0:BLK]

    def b3(t):
        return t.rearrange("p (n t) -> p n t", t=BLK)

    def blk(n):
        return slice(n * BLK, (n + 1) * BLK)

    def spread(ap, n):
        return ap.unsqueeze(2).broadcast_to([ap.shape[0], ap.shape[1], n])

    def tile(t):
        return slice(t * P, (t + 1) * P)

    HALVES = (slice(0, 64), slice(64, 128))
    QUADS = [(0, 32), (32, 0), (64, 96), (96, 64)]

    def w_views(c):
        if c >= NIN:
            s = weights_in[LOAD_AT[("out", (c - NIN) // 2)]]
            src = raw[:, s[0], :, (c % 2) * P:(c % 2 + 1) * P]
            return s, src, lambda w: w[:, :, :]
        pair = c // 2
        s = weights_in[LOAD_AT[("in", pair)]]
        r = raw[:, s[0], :, :]
        if pair == KV_KR and c % 2 == 1:
            src = r[:, :, 128:192].unsqueeze(2).broadcast_to([P, KD, 2, 64])
            return s, src, lambda w: w[:, :, :].rearrange("p k (a d) -> p k a d", a=2)
        if pair in (S_Q, S_G):
            g = c % 2
            src = r.rearrange("p k (a g d) -> p k g a d", a=2, g=2)[:, :, g]
            return s, src, lambda w: w[:, :, :].rearrange("p k (a d) -> p k a d", a=2)
        return s, r[:, :, (c % 2) * P:(c % 2 + 1) * P], lambda w: w[:, :, :]

    def early(j, g_index):
        return j - SLOTS < GROUPS[g_index]["jobs"][0]

    def job_shape(j):
        g = GROUP_OF[j]
        if g["kind"] == "swa_p":
            return P, HEADS, P * len(g["keys"]), True
        if g["kind"] == "swa_s":
            return P, 1, 640, True
        if g["kind"] == "mla_p":
            return P, 1, P * len(g["keys"]), False
        return HEADS * TS, 1, 640, False

    def s_view(j):
        rows, nh, w, _ = job_shape(j)
        s = psum[0:rows, 2 * (j % 2):2 * (j % 2) + 2, :].rearrange("p a b -> p (a b)")
        if nh == 1:
            return s[:, 0:w].unsqueeze(1)
        return s.rearrange("p (h w) -> p h w", h=HEADS)[:, :, 0:w]

    def p_view(j):
        rows, nh, w, _ = job_shape(j)
        s = probs[0:rows, j % SLOTS, :]
        if nh == 1:
            return s[:, 0:w].unsqueeze(1)
        return s.rearrange("p (h w) -> p h w", h=HEADS)[:, :, 0:w]

    with nc.Block() as block:

        @block.sync
        def _(sp):
            sp.dma_start(ident[:], io["c_ident"]).then_inc(s_const.sem, 16)
            sp.dma_start(masks_f[:], io["c_masks"]).then_inc(s_const.sem, 16)
            sp.dma_start(crow[0:1, :], io["c_prompt"]).then_inc(s_c.sem, 16)
            sp.dma_start(crow[1:1 + NB, :], io["c_sample"]).then_inc(s_c.sem, 16)
            sp.dma_start(frow[:], io["final_norm_g"].rearrange("(k p) -> k p", p=P)).then_inc(s_c.sem, 16)
            xp = io["x_prompt"].rearrange("b (t p) d -> p (b t) d", p=P)
            for i, (a, b) in enumerate(((0, 4), (4, 8))):
                sp.dma_start(tok[:, a:b, :], xp[:, a:b, :]).then_inc(s_tok[i].sem, 16)
            sp.dma_start(tok[:, ST, :], io["x_sample"].rearrange("b t d -> (b t) d")).then_inc(s_tok[2].sem, 16)
            sp.wait_ge(s_xa.sem, TILES)
            sp.wait_ge(s_xv.sem, TILES)
            sp.dma_start(xT, x[:]).then_inc(x_out.sem, 16)
            with sp.Fori(0, DEPTH) as L:
                lane = Lane(sp, L)

                def load(n):
                    kind, i = LOADS[n]
                    slot, _ = weights_in[n]
                    if n < 2:
                        lane.wait(lo_w, 0)
                    else:
                        was, j = LOADS[n - 2]
                        if was == "mod":
                            lane.wait(mod_mm, j + 1)
                        else:
                            lane.wait(lo_w, 2 * j + 2 + (NIN if was == "out" else 0))
                    if kind == "mod":
                        src = io["w_mod"][L].rearrange("(k p) n -> p k n", p=P)[:, :, 256 * i:256 * i + 256]
                        sp.dma_start(raw[:, slot], src).then_inc(w_in[slot].sem, 16)
                    elif kind == "in":
                        c0, w = PAIRS[i]
                        src = io["w_in"][L].rearrange("(k p) n -> p k n", p=P)[:, :, c0:c0 + w]
                        for ks in ((slice(4, 8), slice(0, 4)) if i == CV_H else (slice(0, KD),)):
                            sp.dma_start(raw[:, slot, ks, 0:w], src[:, ks]).then_inc(w_in[slot].sem, 16)
                    else:
                        cols = slice(256 * i, 256 * i + 256)
                        src = io["w_out"][L, 0:768].rearrange("(k p) n -> p k n", p=P)[:, :, cols]
                        sp.dma_start(raw[:, slot, 0:6, :], src).then_inc(w_in[slot].sem, 16)
                        for kv in range(2):
                            src = io["w_out"][L, 768 + 128 * kv:896 + 128 * kv].rearrange(
                                "(g p) n -> p g n", g=2)[:, :, cols]
                            sp.dma_start(raw[HALVES[kv], slot, 6:8, :], src).then_inc(w_in[slot].sem, 16)

                def rope_table(which, used):
                    lane.wait(roped, used)
                    sp.dma_start(tab[:], io["c_rope"][which]).then_inc(tab_in.sem, 16)

                load(0)
                load(1)
                for a, b, name in ((V_G, V_BMOD, "norm_g"), (V_BMOD, V_QG, "b_mod"), (V_QG, V_KVG, "q_norm_g"),
                                   (V_KVG, V_CONV, "kv_norm_g")):
                    sp.dma_start(vrows[a:b, :], io[name][L].rearrange("(r c) -> r c", c=P)).then_inc(vec_in.sem, 16)
                sp.dma_start(vrows[V_CONV:V_ROWS, :], io["conv_w"][L].rearrange("k (j c) -> (k j) c", c=P))\
                    .then_inc(vec_in.sem, 16)
                sp.dma_start(ccrow[:], io["cache_conv"][L].rearrange("b t c -> (b t) c")).then_inc(vec_in.sem, 16)
                sp.dma_start(sink[:], io["swa_sink"][L].unsqueeze(0).broadcast_to([P, HEADS]))\
                    .then_inc(vec_in.sem, 16)
                rope_table(0, 0)
                for n in range(2, LOAD_AT[("in", S_Q)] + 1):
                    load(n)
                rope_table(1, 1)
                for n in range(LOAD_AT[("in", S_Q)] + 1, LOAD_AT[("in", CV_H)] + 1):
                    load(n)
                rope_table(0, 4)
                for n in range(LOAD_AT[("in", CV_H)] + 1, LOAD_AT[("mod", 10)]):
                    load(n)
                lane.wait(z_done, NIN)
                sp.dma_start(w_ukv[:], io["w_ukv"][L].rearrange("p (h n) -> p h n", h=HEADS)).then_inc(ukv_in.sem, 16)
                for k in range(2):
                    src = io["w_uq"][L, tile(k)].rearrange("p (h c) -> p h c", h=HEADS)
                    for a, w in ((0, P), (P, 64)):
                        dst = w_uq[:, k, HEADS * a:HEADS * (a + w)].rearrange("p (h c) -> p h c", h=HEADS)
                        sp.dma_start(dst, src[:, :, a:a + w]).then_inc(uq_in.sem, 16)
                for dst, name in ((sk_c, "cache_swa_k"), (sv_c, "cache_swa_v")):
                    sp.dma_start(dst[:], io[name][L].rearrange("b s h d -> (b s) (h d)")
                                 .rearrange("(t p) c -> p t c", p=P)).then_inc(swc_in.sem, 16)
                for n in range(LOAD_AT[("mod", 10)], LOAD_AT[("out", 2)]):
                    load(n)
                for b in range(NB):
                    s = b % 2
                    if b < 2:
                        lane.wait(qn_mm, HEADS * NBLK)
                    else:
                        g = [g for g in GROUPS if g["kind"] == "mla_s"][b - 2]
                        lane.wait(pv, g["units"][-1] + 1)
                    sp.dma_start(raw_ckv[:, s], io["cache_mla_ckv"][L, b].rearrange("(t p) c -> p t c", p=P))\
                        .then_inc(mlc_in[s].sem, 16)
                    for half in HALVES:
                        sp.dma_start(raw_kr[:, s, :, half],
                                     io["cache_mla_krope"][L, b].rearrange("(t p) c -> p t c", p=P))\
                            .then_inc(mlc_in[s].sem, 16)
                lane.wait(x_out, 0)
                lane.wait(hi_w, NIN + 1)
                for i in range(2):
                    sp.dma_start(x[:, 4 * i:4 * i + 4, :], xT[:, 4 * i:4 * i + 4, :]).then_inc(x_in[i].sem, 16)
                for n in range(LOAD_AT[("out", 2)], len(LOADS)):
                    load(n)
                for c in range(NIN, NCHUNK):
                    lane.wait(z_dve, c + 1)
                    sp.dma_start(xT[:, c - NIN, :], x[:, c - NIN, :]).then_inc(x_out.sem, 16)
            sp.wait_ge(x_out.sem, x_out.at(DEPTH, 0))
            for t in range(TILES):
                sp.wait_ge(s_ya.sem, t + 1)
                sp.wait_ge(s_yv.sem, t + 1)
                dst = (io["y_sample"].rearrange("b t d -> (b t) d") if t == ST
                       else io["y_prompt"][0, tile(t), :])
                sp.dma_start(dst, tok[:, t, :]).then_inc(s_out.sem, 16)
            sp.wait_ge(s_out.sem, 16 * TILES)
            sp.wait_ge(outs.sem, outs.at(DEPTH, 0))

        @block.gpsimd
        def _(pool):
            pool.memset(ones[:], 1.0).then_inc(s_cst.sem, 1)
            pool.memset(mhalf[:], -0.5).then_inc(s_cst.sem, 1)
            pool.memset(qrs[:], 0.0).then_inc(s_cst.sem, 1)
            pool.wait_ge(s_cst.sem, 4)

            def x_rstd(layer):
                for n in range(NBLK):
                    pool.wait_ge(mean_x.sem, mean_x.at(layer, n + 1))
                    if n == 0:
                        pool.wait_ge(bc_x.sem, bc_x.at(layer, 0))
                    pool.tensor_tensor(rstd[:, 3 * n:3 * n + 3], mean[:, 3 * n:3 * n + 3], mhalf[:, 0:3],
                                       ALU.pow).then_inc(rstd_x.sem, 1)

            with pool.Fori(0, DEPTH) as L:
                x_rstd(L)
                for i in range(2):
                    pool.wait_ge(lat_mean.sem, L * 2 + i + 1)
                    pool.wait_ge(lat_bc.sem, lat_bc.at(L, 0))
                    pool.tensor_tensor(rstdl[:, i, :], meanl[:, i, :], mhalf[:], ALU.pow).then_inc(lat_rstd.sem, 1)
            x_rstd(DEPTH)

        @block.tensor
        def _(pe):
            def x_sums(layer, n):
                pe.wait_ge(sq_x.sem, sq_x.at(layer, n + 1))
                pe.wait_ge(mean_x.sem, mean_x.at(layer, n))
                for i in range(3):
                    for k in range(KD):
                        mm = pe.matmul(psum[:, 6, i:i + 1], mix[:, k, n * BLK + i * P:n * BLK + i * P + P], ones[:],
                                       start=(k == 0), stop=(k == KD - 1))
                mm.then_inc(sum_x.sem, 1)

            def x_spread(layer, n):
                pe.wait_ge(rstd_x.sem, rstd_x.at(layer, n + 1))
                pe.wait_ge(scaled_x.sem, scaled_x.at(layer, n))
                for i in range(3):
                    mm = pe.matmul(psum[:, 4, tile(i)], rstd[:, 3 * n + i:3 * n + i + 1].broadcast_to([P, P]),
                                   ident[:], start=True, stop=True)
                mm.then_inc(bc_x.sem, 1)

            def x_norm(layer):
                x_sums(layer, 0)
                for n in range(NBLK):
                    if n + 1 < NBLK:
                        x_sums(layer, n + 1)
                    x_spread(layer, n)

            pe.wait_ge(s_const.sem, 32)
            pe.wait_ge(s_cst.sem, 4)
            bank = 0
            for t in range(TILES):
                pe.wait_ge(s_tok[min(t // 4, 2)].sem, 16)
                for half in range(2):
                    n = 2 * t + half
                    if t >= 2:
                        pe.wait_ge((s_xa, s_xv)[half].sem, t - 1)
                    for k in range(4):
                        mm = pe.transpose(psum[:, n % 4, tile(k)], tok[:, t, tile(4 * half + k)], ident[:])
                    mm.then_inc(s_xT.sem, 1)
            pe.wait_ge(s_cs.sem, 3)
            for k in range(KD):
                mm = pe.transpose(psum[:, 5, 16 * k:16 * k + 1 + NB], csil[:, tile(k)], ident[0:1 + NB, 0:1 + NB])
            mm = pe.transpose(psum[:, 5, 256:256 + KD], frow[:], ident[0:KD, 0:KD])
            mm.then_inc(s_cT.sem, 1)
            pe.wait_ge(s_cT.sem, 3)

            for sig in (z_done, bc_x, lat_bc):
                pe.sem_inc(sig.sem, 1)
            with pe.Fori(0, DEPTH) as L:
                lane = Lane(pe, L)

                def modulation(pairs, bank):
                    for i in pairs:
                        s, count = weights_in[LOAD_AT[("mod", i)]]
                        lane.wait(w_in[s], count)
                        for j in range(2):
                            at_ = (2 * i + j) * (1 + NB)
                            for k in range(KD):
                                mm = pe.matmul(psum[:, bank, at_:at_ + 1 + NB], raw[:, s, k, tile(j)], cT[:, k, :],
                                               start=(k == 0), stop=(k == KD - 1))
                        mm.then_inc(mod_mm.sem, 1)

                def chunk(c, s):
                    lane.wait(lo_w, c + 1)
                    lane.wait(z_dve, c - 1)
                    for n in range(NBLK):
                        for k in range(KD):
                            for i, (w, h) in enumerate(((w_hi, h_hi), (w_lo, h_hi), (w_hi, h_lo))):
                                mm = pe.matmul(psum[:, 3 * s + n, 0:BLK], w[s][:, k, :], h[:, k, blk(n)],
                                               start=(k == 0 and i == 0), stop=(k == KD - 1 and i == 2))
                    mm.then_inc(z_done.sem, 1)

                def first_chunk(c, s, half):
                    lane.wait(lo_w, c + 1)
                    if c >= 2:
                        lane.wait(z_dve, c - 1)
                    for n in range(NBLK):
                        lane.wait(lo_h, half * NBLK + n + 1)
                        for k in range(KD):
                            for i, (w, h) in enumerate(((w_hi, h_hi), (w_lo, h_hi), (w_hi, h_lo))):
                                mm = pe.matmul(psum[:, 3 * s + n, 0:BLK], w[s][:, k, :], h[:, k, blk(n)],
                                               start=(k == 0 and i == 0), stop=(k == KD - 1 and i == 2))
                    mm.then_inc(z_done.sem, 1)

                def chunks(first, last):
                    with pe.Fori(first, last, 2) as c:
                        chunk(c, 0)
                        chunk(c + 1, 1)

                lane.wait(z_dve, 0)
                lane.wait(uv_ok, 0)
                lane.wait(vec_in, 16 * 7)
                pe.matmul(psum[:, 5, 0:V_ROWS], vrows[:], ident[0:V_ROWS, 0:V_ROWS], start=True, stop=True)
                for j in range(2):
                    mm = pe.transpose(psum[:, 5, 64 + 16 * j:80 + 16 * j], ccrow[:, tile(j)], ident[0:16, 0:16])
                mm.then_inc(small_T.sem, 1)
                x_norm(L)
                modulation(range(8), 7)
                lane.wait(small_v, 2)
                lane.wait(scaled_x, NBLK)
                first_chunk(0, 0, 0)
                lane.wait(lo_w, 2)
                for n in range(NBLK):
                    for k in range(KD):
                        for i, (w, h) in enumerate(((w_hi, h_hi), (w_lo, h_hi), (w_hi, h_lo))):
                            mm = pe.matmul(psum[:, 3 + n, 0:BLK], w[1][:, k, :], h[:, k, blk(n)],
                                           start=(k == 0 and i == 0), stop=(k == KD - 1 and i == 2))
                mm.then_inc(z_done.sem, 1)
                chunks(2, 2 * SPLIT_AFTER)

                lane.wait(z_act, 2 * Q_LAT + 2)
                lane.wait(mod_v, 1)
                for i, parts in enumerate(((0,), (1, 5))):
                    for t in range(TILES):
                        for q, k in enumerate(parts):
                            mm = pe.matmul(psum[:, 6, 16 * i + t:16 * i + t + 1], mix[:, k, tile(t)], ones[:],
                                           start=(q == 0), stop=(q == len(parts) - 1))
                mm.then_inc(lat_sum.sem, 1)
                lane.wait(z_dve, 2 * SK_SV + 2)
                for n in range(3):
                    if n:
                        lane.wait(svt_c, n)
                    for i in range(4 if n < 2 else 1):
                        mm = pe.transpose(psum[:, 7, tile(i)], svT[:, tile(4 * n + i)], ident[:])
                    mm.then_inc(svt_T.sem, 1)
                chunks(2 * SPLIT_AFTER, 2 * SPLIT_AFTER + 2)
                lane.wait(lat_mean, 2)
                lane.wait(svt_c, 3)
                for m in range(2 * NBLK):
                    i, n = divmod(m, NBLK)
                    lane.wait(lat_rstd, i + 1)
                    if m >= 2:
                        lane.wait(lat_ok, m - 1)
                    for t in range(3):
                        mm = pe.matmul(psum[:, 6 + m % 2, tile(t)],
                                       rstdl[:, i, 3 * n + t:3 * n + t + 1].broadcast_to([P, P]), ident[:],
                                       start=True, stop=True)
                    mm.then_inc(lat_bc.sem, 1)
                chunks(2 * SPLIT_AFTER + 2, NIN)

                def turned(n, parts):
                    if n < 2:
                        lane.wait(z_dve, NIN)
                    else:
                        lane.wait(turn_c, n - 1)
                    for out, in_, k in parts:
                        mm = pe.transpose(psum[0:out[0], 4 + n % 2, out[1]:out[1] + k], in_, ident[0:k, 0:k])
                    mm.then_inc(turn_T.sem, 1)

                lane.wait(lat_ok, 2 * NBLK)
                lane.wait(svt_c, 3)
                for n in range(3):
                    turned(n, [((P, P * i), ckvT[:, tile(4 * n + i)], P) for i in range(4 if n < 2 else 1)])
                for i in range(2):
                    turned(3 + i, [((P, 0), skT[:, tile(ST - 1 + i)], P)]
                           + [((P, P + 64 * t), krT[0:64, tile(6 * i + t)], 64) for t in range(6 - 3 * i)])
                turned(5, [((2 + 2 * NB, P * j), state[:, j, :], P) for j in range(2)])
                lane.wait(ukv_in, 16)
                turned(6, [((P, P * h), w_ukv[:, h, 0:P], P) for h in range(HEADS)])
                modulation(range(8, 12), 7)

                lane.wait(uq_in, 64)
                lane.wait(turn_c, 7)
                lane.wait(mod_v, 2)
                for n in range(NBLK):
                    for j in range(2):
                        m = 2 * n + j
                        if m >= 2:
                            lane.wait(roped, 4 + m - 1)
                        for k in range(2):
                            w = w_uq[:, k, HEADS * P + P * j:HEADS * P + P * j + P]
                            mm = pe.matmul(psum[:, m % 2, 0:BLK], w, cq[:, k, blk(n)], start=(k == 0), stop=(k == 1))
                        mm.then_inc(qr_mm.sem, 1)

                def q_nope(m):
                    n, h = divmod(m, HEADS)
                    if m >= 2:
                        lane.wait(qn_c, m - 1)
                    for k in range(2):
                        mm = pe.matmul(psum[:, 6 + m % 2, 0:BLK], w_uq[:, k, tile(h)], cq[:, k, blk(n)],
                                       start=(k == 0), stop=(k == 1))
                    mm.then_inc(qn_mm.sem, 1)

                def q_latent(m):
                    lane.wait(qn_c, m + 1)
                    if m >= 2:
                        lane.wait(qa_c, m - 1)
                    pe.matmul(psum[:, 4 + m % 2, 0:BLK], w_ukT[:, m % HEADS, :], qn[:, m % 2, :],
                              start=True, stop=True).then_inc(qa_mm.sem, 1)

                q_nope(0)
                for m in range(HEADS * NBLK):
                    if m + 1 < HEADS * NBLK:
                        q_nope(m + 1)
                    q_latent(m)

                bank7 = [qn_c, HEADS * NBLK]

                def free_bank7():
                    lane.wait(bank7[0], bank7[1])

                turns = [0]

                def prepare(g):
                    if g["kind"] == "swa_s":
                        lane.wait(swc_in, 32)
                        parts = [sk_c]
                    elif g["kind"] == "mla_s":
                        s = g["idx"] % 2
                        lane.wait(mlc_in[s], 48 * (g["idx"] // 2 + 1))
                        parts = [raw_ckv[:, s], raw_kr[:, s]]
                    else:
                        return
                    for part in parts:
                        free_bank7()
                        for i in range(4):
                            mm = pe.transpose(psum[:, 7, tile(i)], part[:, i, :], ident[:])
                        mm.then_inc(ct_T.sem, 1)
                        turns[0] += 1
                        bank7[:] = [ct_c, turns[0]]

                def scores(g):
                    t = g["idx"]
                    for i, j in enumerate(g["jobs"]):
                        if j >= 2:
                            lane.wait(expd, j - 1)
                        else:
                            lane.wait(roped, 4 + 2 * NBLK)
                        out = psum[:, 2 * (j % 2):2 * (j % 2) + 2, :].rearrange("p a b -> p (a b)")
                        if g["kind"] == "swa_p":
                            ks, w = g["keys"], P * len(g["keys"])
                            for h in range(HEADS):
                                half = HALVES[h // 2]
                                pe.matmul(out[:, 256 * h:256 * h + w], sqT[half, h % 2, tile(t)],
                                          skT[half, ks[0] * P:(t + 1) * P], start=True, stop=False)
                                mm = pe.matmul(out[:, 256 * h:256 * h + w], half_rows[0:2, :], band_mask[0:2, 256 - w:256],
                                               start=False, stop=True)
                        elif g["kind"] == "swa_s":
                            half = HALVES[i // 2]
                            if i == 0:
                                lane.wait(ct_c, turns[0])
                            for a, b, keys in ((0, 512, skT_c[half, :]), (512, 640, skT[half, SEQ:NTOK])):
                                pe.matmul(out[:, a:b], sqT[half, i % 2, tile(ST)], keys, start=True, stop=False)
                                mm = pe.matmul(out[:, a:b], own8, block_mask[:, a:b], start=False, stop=True)
                        elif g["kind"] == "mla_p":
                            if i == 0:
                                lane.wait(qa_c, HEADS * NBLK)
                            w = (t + 1) * P
                            half = HALVES[i % 2]
                            for a in range(0, w, 512):
                                b = min(a + 512, w)
                                pe.matmul(out[:, a:b], qa[:, i, tile(t)], ckvT[:, a:b], start=True, stop=False)
                                mm = pe.matmul(out[:, a:b], qr[half, i // 2, tile(t)], krT[half, a:b],
                                               start=False, stop=(b < w))
                            mm = pe.matmul(out[:, w - CH:w], half_rows[0:1, :], band_mask[0:1, 256 - CH:256],
                                           start=False, stop=True)
                        else:
                            lane.wait(ct_c, turns[0])
                            lane.wait(qas_ok, 2)
                            b = t
                            for a, e, kc, kr_ in ((0, 512, ckvT_c[:], krT_c[:]),
                                                  (512, 640, ckvT[:, SEQ:NTOK], krT[:, SEQ:NTOK])):
                                pe.matmul(out[0:64, a:e], qas[:, b, :], kc, start=True, stop=False)
                                mm = pe.matmul(out[0:64, a:e], qrs[:, b, :], kr_, start=False, stop=(a == 0))
                            mm = pe.matmul(out[0:64, 512:640], own64[:, 64 * b:64 * b + 64], block_mask[:, 512:640], start=False, stop=True)
                        mm.then_inc(score.sem, 1)

                def turn_probs(g, i):
                    n = g["units"][i]
                    if n >= 2:
                        lane.wait(pt_c[n % 2], n // 2)
                    else:
                        lane.wait(qa_c, HEADS * NBLK)
                    if i == 0:
                        lane.wait(p_ok, g["jobs"][-1] + 1)
                    out = psum[:, 4 + n % 2, :]
                    if g["kind"] == "mla_s":
                        pr = probs[0:64, g["jobs"][0] % SLOTS, :]
                        for k in range(5):
                            mm = pe.matmul(out[:, 64 * k:64 * k + 64], pr[:, tile(k)], ident[0:64, 0:64],
                                           start=True, stop=True)
                    else:
                        for h in range(HEADS):
                            if g["kind"] == "swa_p":
                                pr = probs[:, g["jobs"][0] % SLOTS, 256 * h + P * i:256 * h + P * i + P]
                            else:
                                pr = probs[:, g["jobs"][h] % SLOTS, tile(i)]
                            mm = pe.transpose(out[:, tile(h)], pr, ident[:])
                    mm.then_inc(pt_T.sem, 1)

                def weigh(g, i):
                    n = g["units"][i]
                    last = i == len(g["units"]) - 1
                    lane.wait(pt_c[n % 2], n // 2 + 1)
                    if g["kind"] == "mla_s":
                        s = g["idx"] % 2
                        for k in range(5):
                            v = raw_ckv[:, s, k, :] if k < 4 else ckv[:, ST, :]
                            mm = pe.matmul(psum[:, 6, 0:64], v, pT[:, n % 3, 64 * k:64 * k + 64],
                                           start=(k == 0), stop=(k == 4))
                    else:
                        k = g["keys"][i]
                        v = {"swa_p": sv, "mla_p": ckv}.get(g["kind"])
                        v = v[:, k, :] if v is not None else (sv_c[:, k, :] if k < 4 else sv[:, ST, :])
                        mm = pe.matmul(psum[:, 6, :], v, pT[:, n % 3, :], start=(i == 0), stop=last)
                    mm.then_inc(pv.sem, 1)

                mla_done = [0]

                def up_values(slot):
                    free_bank7()
                    for h in range(HEADS):
                        mm = pe.matmul(psum[:, 7, tile(h)], w_ukv[:, h, P:256], oL[:, slot, h, :], start=True, stop=True)
                    mm.then_inc(uv_mm.sem, 1)
                    mla_done[0] += 1
                    bank7[:] = [uv_ok, mla_done[0]]

                prepare(GROUPS[0])
                scores(GROUPS[0])
                swa_n = mla_n = 0
                for gi, g in enumerate(GROUPS):
                    if gi < LAST:
                        prepare(GROUPS[gi + 1])
                        scores(GROUPS[gi + 1])
                    before = GROUPS[gi - 1] if gi else None
                    if before and before["kind"] == "mla_p":
                        lane.wait(ol_c, mla_n)
                        up_values(before["idx"] % 2)
                    if before and before["kind"][:3] == "swa":
                        lane.wait(swa_ok, swa_n)
                    elif before:
                        lane.wait(ol_c, mla_n)
                    turn_probs(g, 0)
                    for i in range(len(g["units"])):
                        if i + 1 < len(g["units"]):
                            turn_probs(g, i + 1)
                        weigh(g, i)
                    if g["kind"][:3] == "swa":
                        swa_n += 1
                    else:
                        mla_n += 1
                lane.wait(ol_c, mla_n)
                up_values(0)

                first_chunk(NIN, 0, 1)
                chunk(NIN + 1, 1)
                chunks(NIN + 2, NCHUNK)

            pe.wait_ge(z_dve.sem, z_dve.at(DEPTH, 0))
            x_norm(DEPTH)
            for t in range(TILES):
                if t % 3 == 0:
                    pe.wait_ge(s_y.sem, t // 3 + 1)
                for half in range(2):
                    if t >= 1:
                        pe.wait_ge((s_ya, s_yv)[half].sem, t)
                    for k in range(4):
                        mm = pe.transpose(psum[:, 2 * half, tile(k)], x[:, 4 * half + k, tile(t)], ident[:])
                    mm.then_inc(s_yT.sem, 1)

        @block.scalar
        def _(act):
            act.wait_ge(s_c.sem, 48)
            act.activation(csil[:], crow[:], ACT.Tanh, scale=0.5).then_inc(s_cs.sem, 1)
            for t in range(TILES):
                act.wait_ge(s_xT.sem, 2 * t + 1)
                act.activation(x[:, 0:4, tile(t)], psum[:, (2 * t) % 4, :].rearrange("p (k t) -> p k t", k=4), ACT.Copy)\
                    .then_inc(s_xa.sem, 1)
            act.wait_ge(s_xa.sem, TILES)
            act.wait_ge(s_xv.sem, TILES)

            with act.Fori(0, DEPTH) as L:
                lane = Lane(act, L, act_step)

                def split_w(c):
                    (s, count), src, view = w_views(c)
                    lane.wait(w_in[s], count)
                    lane.link(act.activation(view(w_hi[c % 2]), src, ACT.Copy), hi_w)

                def rotate(src, pick, sig):
                    for i, (a, b) in enumerate(QUADS):
                        ins = act.activation(pick(rot[a:a + 32, :]), src[b:b + 32], ACT.Copy)
                        lane.link(ins, sig if i == 3 else None)

                def chunk(c):
                    pair, j = divmod(c, 2)
                    z = zset(c)
                    lane.wait(z_done, c + 1)
                    if pair in (KV_KR, Q_LAT) and (pair, j) != (KV_KR, 1):
                        k = {0: 0, 2: 1, 3: 5}[c]
                        lane.link(act.activation(b3(mix[:, k, :]), z, ACT.Square), z_act)
                    elif (pair, j) in ((KV_KR, 1), (SK_SV, 0), (S_Q, 0), (S_Q, 1)):
                        n = {(KV_KR, 1): 0, (SK_SV, 0): 1, (S_Q, 0): 2, (S_Q, 1): 3}[(pair, j)]
                        lane.wait(roped, n)
                        if n == 0:
                            lane.wait(qrs_ok, 0)
                        rotate(z, b3, z_act)
                    elif pair in (S_G, M_G0, M_G1):
                        k = {S_G: 6, M_G0: 2, M_G1: 4}[pair] + j
                        if pair == M_G1:
                            lane.wait(lat_sum, 1)
                        lane.link(act.activation(b3(mix[:, k, :]), z, ACT.Tanh, scale=0.5), z_act)
                    elif pair == CV_G:
                        lane.wait(z_dve, 2 * CV_B + 2)
                        dst = (rot, svT)[j]
                        lane.link(act.activation(b3(dst[:]), z, ACT.Tanh, scale=0.5), z_act)

                lane.wait(lo_h, 0)
                lane.wait(z_dve, 0)
                for n in range(NBLK):
                    lane.link(act.activation(mix[:, :, blk(n)], x[:, :, blk(n)], ACT.Square), sq_x)
                lane.wait(z_done, 0)
                for n in range(NBLK):
                    lane.wait(scaled_x, n + 1)
                    lane.wait(mod_v, 1)
                    width = BLK if n < NBLK - 1 else SEQ - (NBLK - 1) * BLK
                    cols = slice(n * BLK, n * BLK + width)
                    for k in range(KD):
                        ins = act.activation(x[:, k, cols], x[:, k, cols], ACT.Identity,
                                             bias=mod[:, 0, k, 0:1], scale=amul[:, k, 0:1])
                        lane.link(ins, h_act if k == KD - 1 else None)
                    if n == NBLK - 1:
                        lane.wait(h_smp, 1)
                    lane.link(act.activation(h_hi[:, :, blk(n)], x[:, :, blk(n)], ACT.Copy), hi_h)
                    if n == 0:
                        split_w(0)
                split_w(1)
                for c in range(NIN):
                    if c + 2 < NIN:
                        lane.wait(z_done, c + 1)
                        split_w(c + 2)
                    if c in ACT_CHUNKS:
                        chunk(c)
                    if c == 2 * SPLIT_AFTER - 1:
                        for n in range(3):
                            lane.wait(svt_T, n + 1)
                            w = 4 if n < 2 else 1
                            lane.link(act.activation(sv[:, 4 * n:4 * n + w, :],
                                                     psum[:, 7, 0:P * w].rearrange("p (t c) -> p t c", c=P), ACT.Copy),
                                      svt_c)
                        for dst, src in ((io["swa_v_prompt"][L, 0].rearrange("s h d -> s (h d)"), sv[64:128, ST - 1, :]),
                                         (io["swa_v_sample"][L].rearrange("b t h d -> (b t) (h d)"), sv[:, ST, :])):
                            act.dma_start(dst, src).then_inc(outs.sem, 16)

                lane.wait(z_done, NIN)
                for n in range(7):
                    lane.wait(turn_T, n + 1)
                    src = psum[:, 4 + n % 2, :]
                    if n < 3:
                        w = 4 if n < 2 else 1
                        out, in_ = ckv[:, 4 * n:4 * n + w, :], src[:, 0:P * w].rearrange("p (t c) -> p t c", c=P)
                    elif n < 5:
                        w = 6 if n == 3 else 3
                        lane.link(act.activation(sk_tok[:, n - 3, :], src[:, 0:P], ACT.Copy))
                        out, in_ = kr_tok[:, 6 * (n - 3):6 * (n - 3) + w, :], src[:, P:P + 64 * w].rearrange(
                            "p (t c) -> p t c", c=64)
                    elif n == 5:
                        out, in_ = state_tok[:], src[0:2 + 2 * NB, 0:CONVW]
                    else:
                        out, in_ = w_ukT[:], src[:, :].rearrange("p (h c) -> p h c", c=P)
                    lane.link(act.activation(out, in_, ACT.Copy), turn_c)
                    stores = []
                    if n == 2:
                        stores = [(io["mla_ckv_prompt"][L, 0].rearrange("(t p) c -> p t c", p=P), ckv[:, 0:ST, :]),
                                  (io["mla_ckv_sample"][L].rearrange("b t c -> (b t) c"), ckv[:, ST, :])]
                    elif n == 4:
                        stores = [(io["mla_krope_prompt"][L, 0].rearrange("(t p) c -> p t c", p=P), kr_tok[:, 0:ST, :]),
                                  (io["mla_krope_sample"][L].rearrange("b t c -> (b t) c"), kr_tok[:, ST, :]),
                                  (io["swa_k_prompt"][L, 0].rearrange("s h d -> s (h d)"), sk_tok[64:128, 0, :]),
                                  (io["swa_k_sample"][L].rearrange("b t h d -> (b t) (h d)"), sk_tok[:, 1, :])]
                    elif n == 5:
                        stores = [(io["conv_state_prompt"][L, 0], state_tok[0:2, :]),
                                  (io["conv_state_sample"][L].rearrange("b t c -> (b t) c"), state_tok[2:, :])]
                    for dst, s in stores:
                        act.dma_start(dst, s).then_inc(outs.sem, 16)
                lane.wait(mod_v, 2)
                for m in range(2 * NBLK):
                    lane.wait(qr_mm, m + 1)
                    lane.wait(roped, 4 + m)
                    rotate(psum[:, m % 2, 0:BLK], lambda r: r[:, 0:BLK], qr_rot)
                for m in range(HEADS * NBLK):
                    lane.wait(qn_mm, m + 1)
                    if m >= 2:
                        lane.wait(qa_mm, m - 1)
                    lane.link(act.activation(qn[:, m % 2, :], psum[:, 6 + m % 2, 0:BLK], ACT.Copy), qn_c)

                turns = [0]

                def cache_copies(g):
                    dsts = {"swa_s": [skT_c], "mla_s": [ckvT_c, krT_c]}.get(g["kind"], [])
                    for dst in dsts:
                        turns[0] += 1
                        lane.wait(ct_T, turns[0])
                        lane.link(act.activation(dst[:], psum[:, 7, :], ACT.Copy), ct_c)

                def exps(j):
                    rows, nh, w, has_sink = job_shape(j)
                    g, s = GROUP_OF[j], j % SLOTS
                    scale = SWA_SCALE if has_sink else MLA_SCALE
                    lane.wait(negmax, j + 1)
                    if j >= SLOTS:
                        lane.wait(pt_T, GROUP_OF[j - SLOTS]["units"][-1] + 1)
                    for h in range(nh):
                        ins = act.activation(p_view(j)[:, h, :], s_view(j)[:, h, :], ACT.Exp, bias=nmax[0:rows, s, h:h + 1],
                                             scale=scale, accum_out=psum_p[0:rows, s, h:h + 1])
                        lane.link(ins, expd if h == nh - 1 and not has_sink else None)
                    if has_sink:
                        lane.link(act.activation(esink[:, s, 0:nh], esink[:, s, 0:nh], ACT.Exp), expd)

                cache_copies(GROUPS[0])
                for j in GROUPS[0]["jobs"]:
                    exps(j)
                for gi, g in enumerate(GROUPS):
                    nxt = GROUPS[gi + 1] if gi < LAST else None
                    if nxt:
                        cache_copies(nxt)
                        for j in nxt["jobs"]:
                            if early(j, gi):
                                exps(j)
                    for n in g["units"]:
                        if n % 2 == 0:
                            lane.wait(pt_T, n + 1)
                            if n >= 3:
                                lane.wait(pv, n - 2)
                            w = 320 if g["kind"] == "mla_s" else 512
                            lane.link(act.activation(pT[:, n % 3, 0:w], psum[:, 4, 0:w], ACT.Copy), pt_c[0])
                    if g["kind"] == "mla_p":
                        lane.wait(pv, g["units"][-1] + 1)
                        lane.link(act.activation(oL[:, g["idx"] % 2], psum[:, 6, :].rearrange("p (h t) -> p h t", h=HEADS),
                                                 ACT.Copy), ol_c)
                    elif g["kind"] == "mla_s":
                        lane.wait(pv, g["units"][-1] + 1)
                        if g["idx"] == 0:
                            lane.wait(uv_mm, ST - 1)
                        b = g["idx"]
                        lane.link(act.activation(
                            oL[:, 0].rearrange("p (j a) t -> p a j t", a=2)[:, :, :, TS * b:TS * b + TS],
                            psum[:, 6, 0:64].rearrange("p (a j t) -> p a j t", a=2, j=2), ACT.Copy), ol_c)
                    if nxt:
                        for j in nxt["jobs"]:
                            if not early(j, gi):
                                exps(j)

                lane.wait(uv_mm, TILES)
                lane.wait(outs, 16 * N_STORES)
                lane.wait(uv_ok, TILES)
                lane.wait(qrs_ok, 1)
                split_w(NIN)
                for n in range(NBLK):
                    lane.link(act.activation(h_hi[:, :, blk(n)], mix[:, :, blk(n)], ACT.Copy), hi_h)
                split_w(NIN + 1)
                for c in range(NIN + 2, NCHUNK):
                    lane.wait(z_done, c - 1)
                    split_w(c)
                assert lane.count[act_step.name] == ACT_STEPS

            act.wait_ge(z_dve.sem, z_dve.at(DEPTH, 0))
            act.wait_ge(lo_h.sem, lo_h.at(DEPTH, 0))
            for n in range(NBLK):
                act.activation(mix[:, :, blk(n)], x[:, :, blk(n)], ACT.Square).then_inc(sq_x.sem, 1)
            act.wait_ge(sum_x.sem, sum_x.at(DEPTH, NBLK))
            for t in range(TILES):
                act.wait_ge(s_yT.sem, 2 * t + 1)
                act.activation(tok[:, t, 0:512], psum[:, 0, :], ACT.Copy).then_inc(s_ya.sem, 1)

        @block.vector
        def _(dve):
            dve.wait_ge(s_const.sem, 32)
            dve.tensor_copy(masks[:], masks_f[:]).then_inc(s_cst.sem, 1)
            dve.wait_ge(s_cst.sem, 4)
            dve.wait_ge(s_cs.sem, 1)
            dve.scalar_tensor_tensor(csil[:], csil[:], 1.0, crow[:], ALU.add, ALU.mult).then_inc(s_cs.sem, 1)
            dve.wait_ge(s_cs.sem, 2)
            dve.tensor_scalar(csil[:], csil[:], 0.5, None, ALU.mult).then_inc(s_cs.sem, 1)
            for t in range(TILES):
                dve.wait_ge(s_xT.sem, 2 * t + 2)
                dve.tensor_copy(x[:, 4:8, tile(t)], psum[:, (2 * t + 1) % 4, :].rearrange("p (k t) -> p k t", k=4))\
                    .then_inc(s_xv.sem, 1)
            dve.wait_ge(s_cT.sem, 1)
            dve.tensor_copy(cT[:], psum[:, 5, 0:P].rearrange("p (k c) -> p k c", k=KD)[:, :, 0:1 + NB])\
                .then_inc(s_cT.sem, 1)
            dve.tensor_copy(fing[:], psum[:, 5, 256:256 + KD]).then_inc(s_cT.sem, 1)
            dve.wait_ge(s_cT.sem, 3)
            dve.wait_ge(x_out.sem, 16)

            def x_mean(layer, n):
                dve.wait_ge(sum_x.sem, sum_x.at(layer, n + 1))
                ins = dve.tensor_scalar(mean[:, 3 * n:3 * n + 3], psum[:, 6, 0:3], 1.0 / D, EPS, ALU.mult, ALU.add)
                ins.then_inc(mean_x.sem, 1)
                dve.wait_ge(mean_x.sem, mean_x.at(layer, n + 1))

            def x_scale(layer, n):
                dve.wait_ge(bc_x.sem, bc_x.at(layer, n + 1))
                dve.wait_ge(sq_x.sem, sq_x.at(layer, n + 1))
                ins = dve.tensor_tensor(x[:, :, blk(n)], x[:, :, blk(n)],
                                        psum[:, 4, 0:BLK].unsqueeze(1).broadcast_to([P, KD, BLK]), ALU.mult)
                ins.then_inc(scaled_x.sem, 1)
                dve.wait_ge(scaled_x.sem, scaled_x.at(layer, n + 1))

            def x_norm(layer):
                x_mean(layer, 0)
                for n in range(NBLK):
                    if n + 1 < NBLK:
                        x_mean(layer, n + 1)
                    x_scale(layer, n)

            for sig in (lo_w, lo_h, z_dve, roped, qrs_ok, uv_ok, mean_x, scaled_x):
                dve.sem_inc(sig.sem, 1)
            with dve.Fori(0, DEPTH) as L:
                lane = Lane(dve, L, dve_step)
                tt = lambda *a, sig=None: lane.link(dve.tensor_tensor(*a), sig)
                stt = lambda *a, sig=None: lane.link(dve.scalar_tensor_tensor(*a), sig)
                ts = lambda *a, sig=None: lane.link(dve.tensor_scalar(*a), sig)
                cp = lambda *a, sig=None: lane.link(dve.tensor_copy(*a), sig)

                def split_w(c):
                    _, src, view = w_views(c)
                    lane.wait(hi_w, c + 1)
                    if c >= 2:
                        lane.wait(z_done, c - 1)
                    tt(view(w_lo[c % 2]), src, view(w_hi[c % 2]).bitcast(F32), ALU.subtract, sig=lo_w)

                def rope(out, z, c_, s_, r, sig):
                    tt(out, z, c_, ALU.mult)
                    tt(r, r, s_, ALU.mult)
                    tt(out, out, r, ALU.add, sig=sig)

                def per_sample(ap):
                    return ap[:, SEQ:NTOK].rearrange("p (b t) -> p b t", t=TS)

                lane.wait(small_T, 1)
                lane.wait(vec_in, 16 * 7)
                cp(vec[:], psum[:, 5, 0:V_ROWS], sig=small_v)
                cp(convc[:], psum[:, 5, 64:96].rearrange("p (j c) -> p j c", j=2), sig=small_v)
                ts(nsink[:], sink[:], -1.0, None, ALU.mult)
                lane.wait(x_out, 0)
                x_norm(L)
                lane.wait(mod_mm, 8)
                tt(mod[:, 0:2].rearrange("p a k c -> p (a k) c"),
                   psum[:, 7, 0:16 * (1 + NB)].rearrange("p (k c) -> p k c", k=16),
                   spread(vec[:, V_BMOD:V_BMOD + 16], 1 + NB), ALU.add)
                stt(amul[:], mod[:, 1], 1.0, spread(vec[:, V_G:V_G + KD], 1 + NB), ALU.add, ALU.mult, sig=mod_v)
                xs = x[:, :, SEQ:NTOK].rearrange("p k (b t) -> p k b t", t=TS)

                def each(ap):
                    return ap.unsqueeze(3).broadcast_to([P, KD, NB, TS])

                tt(xs, xs, each(amul[:, :, 1:]), ALU.mult)
                tt(xs, xs, each(mod[:, 0, :, 1:]), ALU.add, sig=h_smp)
                for n in range(NBLK):
                    lane.wait(hi_h, n + 1)
                    tt(h_lo[:, :, blk(n)], x[:, :, blk(n)], h_hi[:, :, blk(n)].bitcast(F32), ALU.subtract, sig=lo_h)
                    if n == 0:
                        split_w(0)
                split_w(1)
                for c in range(NIN):
                    if c + 2 < NIN:
                        split_w(c + 2)
                    pair, j = divmod(c, 2)
                    z = zset(c)
                    lane.wait(z_done, c + 1)
                    if c in ACT_CHUNKS:
                        lane.wait(z_act, ACT_CHUNKS.index(c) + 1)
                    if c == 0:
                        lane.wait(lo_h, NBLK)
                    if pair == KV_KR and j == 0:
                        ts(b3(ckvT[:]), z, vec[:, V_KVG:V_KVG + 1], None, ALU.mult, sig=z_dve)
                    elif pair == Q_LAT:
                        ts(b3(cq[:, j, :]), z, vec[:, V_QG + j:V_QG + j + 1], None, ALU.mult, sig=z_dve)
                    elif pair == SK_SV and j == 1:
                        cp(b3(svT[:]), z, sig=z_dve)
                    elif pair in (KV_KR, SK_SV, S_Q):
                        lane.wait(tab_in, 16 if pair == KV_KR else 32)
                        out = {KV_KR: krT[:], SK_SV: skT[:], S_Q: sqT[:, j, :]}[pair]
                        tt(b3(out), z, b3(tab[:, 0, :]), ALU.mult, sig=z_dve)
                        tt(rot[:], rot[:], tab[:, 1, :], ALU.mult)
                        tt(out, out, rot[:], ALU.add, sig=roped)
                    elif pair in (S_G, M_G0, M_G1):
                        k = {S_G: 6, M_G0: 2, M_G1: 4}[pair] + j
                        stt(b3(mix[:, k, :]), b3(mix[:, k, :]), 1.0, z, ALU.add, ALU.mult, sig=z_dve)
                    elif pair == CV_H:
                        lane.wait(lat_sum, 1)
                        cp(b3(mix[:, j, :]), z, sig=z_dve)
                    elif pair == CV_C:
                        up, us = u[:, j, 0:2 + SEQ], u[:, j, 2 + SEQ:].rearrange("p (b t) -> p b t", t=TS + 2)
                        y = mix[:, j, :]
                        if j == 0:
                            lane.wait(svt_T, 3)
                        lane.link(dve.memset(up[:, 0:2], 0.0))
                        cp(us[:, :, 0:2], convc[:, j, :].rearrange("p (b t) -> p b t", t=2))
                        tt(up[:, 2:2 + 2 * BLK].rearrange("p (n t) -> p n t", t=BLK), z[:, 0:2, :],
                           y[:, 0:2 * BLK].rearrange("p (n t) -> p n t", t=BLK), ALU.mult)
                        tt(up[:, 2 + 2 * BLK:2 + SEQ], z[:, 2, 0:SEQ - 2 * BLK], y[:, 2 * BLK:SEQ], ALU.mult)
                        tt(us[:, :, 2:], z[:, 2, SEQ - 2 * BLK:].rearrange("p (b t) -> p b t", t=TS), per_sample(y),
                           ALU.mult, sig=z_dve)
                        for i in range(3):
                            w = vec[:, V_CONV + 2 * i + j:V_CONV + 2 * i + j + 1]
                            for out, in_ in ((y[:, 0:SEQ], up[:, i:i + SEQ]), (per_sample(y), us[:, :, i:i + TS])):
                                if i == 0:
                                    ts(out, in_, w, None, ALU.mult)
                                else:
                                    stt(out, in_, w, out, ALU.mult, ALU.add)
                        cp(state[:, j, 0:2], up[:, SEQ:SEQ + 2])
                        cp(state[:, j, 2:].rearrange("p (b t) -> p b t", t=2), us[:, :, TS:TS + 2])
                    elif pair == CV_B:
                        tt(b3(mix[:, j, :]), z, b3(mix[:, j, :]), ALU.mult, sig=z_dve)
                    else:
                        r = (rot, svT)[j]
                        stt(b3(r[:]), b3(r[:]), 1.0, z, ALU.add, ALU.mult, sig=z_dve)
                        stt(mix[:, j, :], r[:], 0.5, mix[:, j, :], ALU.mult, ALU.mult)
                    if c == 2 * SPLIT_AFTER - 1:
                        lane.wait(lat_sum, 1)
                        for i, width in enumerate((128, 256)):
                            ts(meanl[:, i, :], psum[:, 6, 16 * i:16 * i + TILES], 1.0 / width, EPS, ALU.mult, ALU.add,
                               sig=lat_mean)
                    if c == 2 * SPLIT_AFTER + 1:
                        for i in range(2):
                            for n in range(NBLK):
                                m = NBLK * i + n
                                lane.wait(lat_bc, m + 1)
                                r = psum[:, 6 + m % 2, 0:BLK]
                                if i == 0:
                                    tt(ckvT[:, blk(n)], ckvT[:, blk(n)], r, ALU.mult, sig=lat_ok)
                                else:
                                    tt(cq[:, :, blk(n)], cq[:, :, blk(n)], r.unsqueeze(1).broadcast_to([P, 2, BLK]),
                                       ALU.mult, sig=lat_ok)

                lane.wait(mod_mm, n_mod)
                tt(mod[:, 2], psum[:, 7, 16 * (1 + NB):24 * (1 + NB)].rearrange("p (k c) -> p k c", k=KD),
                   spread(vec[:, V_BMOD + 16:V_BMOD + 24], 1 + NB), ALU.add, sig=mod_v)
                lane.wait(tab_in, 48)
                lane.wait(z_done, NIN)
                for m in range(2 * NBLK):
                    n, j = divmod(m, 2)
                    lane.wait(qr_rot, m + 1)
                    rope(qr[:, j, blk(n)], psum[:, m % 2, 0:BLK], tab[:, 0, blk(n)], tab[:, 1, blk(n)], rot[:, 0:BLK],
                         roped)
                lane.wait(turn_T, 6)
                for a, half in enumerate(HALVES):
                    ins = dve.tensor_copy(
                        qrs[half, :, 32 * a:32 * a + 32].rearrange("p b (j t) -> p b j t", j=2),
                        qr[half, :, SEQ:NTOK].rearrange("p j (b t) -> p b j t", t=TS))
                    lane.link(ins, qrs_ok if a else None)
                for m in range(HEADS * NBLK):
                    n, h = divmod(m, HEADS)
                    lane.wait(qa_mm, m + 1)
                    cp(qa[:, h, blk(n)], psum[:, 4 + m % 2, 0:BLK], sig=qa_c)
                for a in range(2):
                    cp(qas[:, :, 32 * a:32 * a + 32].rearrange("p b (j t) -> p b j t", j=2),
                       qa[:].rearrange("p (j a) t -> p a j t", a=2)[:, a, :, SEQ:NTOK]
                       .rearrange("p j (b t) -> p b j t", t=TS), sig=qas_ok)

                def maxima(j):
                    rows, nh, w, has_sink = job_shape(j)
                    s = j % SLOTS
                    lane.wait(score, j + 1)
                    lane.link(dve.tensor_reduce(smax[0:rows, s, 0:nh], s_view(j), AX.X, ALU.max))
                    if not has_sink:
                        ts(nmax[0:rows, s, 0:nh], smax[0:rows, s, 0:nh], -MLA_SCALE, None, ALU.mult, sig=negmax)
                        return
                    h0 = GROUP_OF[j]["jobs"].index(j)
                    stt(nmax[:, s, 0:nh], smax[:, s, 0:nh], -SWA_SCALE, nsink[:, h0:h0 + nh], ALU.mult, ALU.min)
                    tt(esink[:, s, 0:nh], nmax[:, s, 0:nh], sink[:, h0:h0 + nh], ALU.add, sig=negmax)

                def normalise(j):
                    rows, nh, w, has_sink = job_shape(j)
                    s = j % SLOTS
                    lane.wait(expd, j + 1)
                    total = psum_p[0:rows, s, 0:nh]
                    if has_sink:
                        tt(total, total, esink[:, s, 0:nh], ALU.add)
                    lane.link(dve.reciprocal(rinv[0:rows, s, 0:nh], total))
                    if nh == 1:
                        ts(p_view(j)[:, 0, :], p_view(j)[:, 0, :], rinv[0:rows, s, 0:1], None, ALU.mult, sig=p_ok)
                    else:
                        tt(p_view(j), p_view(j), spread(rinv[:, s, :], w), ALU.mult, sig=p_ok)

                def gate_mla(t):
                    g = mix[:, 2:6, tile(t)]
                    stt(g, psum[:, 7, :].rearrange("p (h t) -> p h t", h=HEADS), 0.5, g, ALU.mult, ALU.mult, sig=uv_ok)

                for j in GROUPS[0]["jobs"]:
                    maxima(j)
                    normalise(j)
                n_uv = 0
                for gi, g in enumerate(GROUPS):
                    nxt = GROUPS[gi + 1] if gi < LAST else None
                    late, ready = [], None
                    for j in (nxt["jobs"] if nxt else []):
                        maxima(j)
                        if ready is not None:
                            normalise(ready)
                            ready = None
                        if early(j, gi):
                            ready = j
                        else:
                            late.append(j)
                    if ready is not None:
                        normalise(ready)
                    if gi and GROUPS[gi - 1]["kind"] == "mla_p":
                        n_uv += 1
                        lane.wait(uv_mm, n_uv)
                        gate_mla(n_uv - 1)
                    for n in g["units"]:
                        if n % 2 == 1:
                            lane.wait(pt_T, n + 1)
                            if n >= 3:
                                lane.wait(pv, n - 2)
                            w = 320 if g["kind"] == "mla_s" else 512
                            cp(pT[:, n % 3, 0:w], psum[:, 5, 0:w], sig=pt_c[1])
                    if g["kind"][:3] == "swa":
                        lane.wait(pv, g["units"][-1] + 1)
                        for kv, half in enumerate(HALVES):
                            out = mix[half, 6:8, tile(g["idx"])]
                            in_ = psum[half, 6, 256 * kv:256 * kv + 256].rearrange("p (g t) -> p g t", g=2)
                            stt(out, in_, 0.5, out, ALU.mult, ALU.mult, sig=swa_ok if kv else None)
                    for j in late:
                        normalise(j)
                lane.wait(uv_mm, TILES)
                gate_mla(ST)

                split_w(NIN)
                for n in range(NBLK):
                    lane.wait(hi_h, NBLK + n + 1)
                    tt(h_lo[:, :, blk(n)], mix[:, :, blk(n)], h_hi[:, :, blk(n)].bitcast(F32), ALU.subtract, sig=lo_h)
                split_w(NIN + 1)
                for c in range(NIN, NCHUNK):
                    if c + 2 < NCHUNK:
                        split_w(c + 2)
                    k, z = c - NIN, zset(c)
                    lane.wait(z_done, c + 1)
                    if k % 4 == 0:
                        lane.wait(x_in[k // 4], 16)
                    gate = mod[:, 2, k, 0:1]
                    xk = x[:, k, :]
                    two = xk[:, 0:2 * BLK].rearrange("p (n t) -> p n t", t=BLK)
                    stt(two, z[:, 0:2, :], gate, two, ALU.mult, ALU.add)
                    stt(xk[:, 2 * BLK:SEQ], z[:, 2, 0:SEQ - 2 * BLK], gate, xk[:, 2 * BLK:SEQ], ALU.mult, ALU.add)
                    tmp = rot[:, 0:P].rearrange("p (b t) -> p b t", t=TS)
                    tt(tmp, z[:, 2, SEQ - 2 * BLK:].rearrange("p (b t) -> p b t", t=TS), spread(mod[:, 2, k, 1:], TS),
                       ALU.mult)
                    tt(per_sample(xk), per_sample(xk), tmp, ALU.add, sig=z_dve)
                assert lane.count[dve_step.name] == DVE_STEPS

            dve.wait_ge(x_out.sem, x_out.at(DEPTH, 0))
            x_norm(DEPTH)
            for n in range(NBLK):
                dve.tensor_tensor(x[:, :, blk(n)], x[:, :, blk(n)], spread(fing[:], BLK), ALU.mult).then_inc(s_y.sem, 1)
            dve.wait_ge(sum_x.sem, sum_x.at(DEPTH, NBLK))
            for t in range(TILES):
                dve.wait_ge(s_yT.sem, 2 * t + 2)
                dve.tensor_copy(tok[:, t, 512:1024], psum[:, 2, :]).then_inc(s_yv.sem, 1)


_OUTS = [("y_prompt", (1, 1024, 1024)), ("y_sample", (8, 16, 1024)),
         ("conv_state_prompt", (2, 1, 2, 256)), ("conv_state_sample", (2, 8, 2, 256)),
         ("mla_ckv_prompt", (2, 1, 1024, 128)), ("mla_ckv_sample", (2, 8, 16, 128)),
         ("mla_krope_prompt", (2, 1, 1024, 64)), ("mla_krope_sample", (2, 8, 16, 64)),
         ("swa_k_prompt", (2, 1, 64, 2, 64)), ("swa_k_sample", (2, 8, 16, 2, 64)),
         ("swa_v_prompt", (2, 1, 64, 2, 64)), ("swa_v_sample", (2, 8, 16, 2, 64))]
_INS = ["x_prompt", "x_sample", "c_prompt", "c_sample", "cache_conv", "cache_mla_ckv", "cache_mla_krope",
        "cache_swa_k", "cache_swa_v", "norm_g", "w_mod", "b_mod", "w_in", "conv_w", "q_norm_g", "kv_norm_g",
        "w_uq", "w_ukv", "swa_sink", "w_out", "final_norm_g"]


def constants():
    masks = np.zeros((8, 1664), np.float32)
    for b in range(8):
        masks[b, 16 * b:16 * b + 16] = 1
        masks[b, 1152 + 64 * b:1152 + 64 * b + 64] = 1
        own = np.zeros(640, bool)
        own[64 * b:64 * b + 64] = True
        own[512 + 16 * b:512 + 16 * b + 16] = True
        masks[b, 128:768] = np.where(own, 0, NEG)
    masks[0, 768:832] = 1
    masks[1, 832:896] = 1
    masks[0, 896:896 + 64] = NEG
    masks[0, 896 + 192:1152] = NEG
    masks[1, 896:896 + 128] = NEG
    pos = np.concatenate([np.arange(1024), np.tile(512 + np.arange(16), 8)]).astype(np.float32)
    rope = np.zeros((2, 128, 2, 1152), np.float32)
    for i, theta in enumerate((10000.0, 150000.0)):
        inv = np.float32(theta) ** (-np.arange(32, dtype=np.float32) / np.float32(32))
        ang = (pos[None, :] * inv[:, None]).astype(np.float32)
        cos, sin = np.cos(ang), np.sin(ang)
        rope[i, :, 0] = np.tile(cos, (4, 1))
        rope[i, :, 1] = np.concatenate([-sin, sin, -sin, sin])
    return {"c_ident": np.eye(128, dtype=np.float32), "c_masks": masks,
            "c_rope": rope}


def kernel(**inputs):
    import concourse.bacc as bacc
    from concourse.bass_utils import run_bass_kernel_spmd

    nc = bacc.Bacc("TRN2", target_bir_lowering=False, num_devices=1)
    arrays, io = {}, {}
    named = {n: np.ascontiguousarray(inputs[n]) for n in _INS}
    named.update(constants())
    for name, a in named.items():
        arrays[f"in_{name}"] = a
        io[name] = nc.dram_tensor(f"in_{name}", a.shape, mybir.dt.from_np(a.dtype), kind="ExternalInput").ap()
    for name, shape in _OUTS:
        io[name] = nc.dram_tensor(f"out_{name}", shape, F32, kind="ExternalOutput").ap()
    build(nc, io)
    r = run_bass_kernel_spmd(nc, [arrays], core_ids=[0])
    return tuple(r.results[0][f"out_{name}"] for name, _ in _OUTS)
```

```python
import numpy as np
import concourse.bass as bass
from concourse import mybir

F32 = mybir.dt.float32
F32R = mybir.dt.float32r
BF16 = mybir.dt.bfloat16
ACT = mybir.ActivationFunctionType
ALU = mybir.AluOpType
AX = mybir.AxisListType

P = 128
D = 1024
KD = D // P
DEPTH = 2
SEQ, NB, TS = 1024, 8, 16
NTOK = SEQ + NB * TS
TILES = NTOK // P
ST = TILES - 1
PAST = 512
BLK = 384
NBLK = NTOK // BLK
D_IN = 2752
EPS = 1e-6
NEG = -1e30
HEADS = 4
MLA_SCALE = (128 + 64) ** -0.5
SWA_SCALE = 64 ** -0.5
CH = 64
CONVW = 256

KV_KR, Q_LAT, SK_SV, S_Q, S_G, M_G0, M_G1, CV_H, CV_C, CV_B, CV_G = range(11)
PAIRS = [(1280, 192), (1024, 256), (2240, 256), (1984, 256), (2496, 256), (1472, 256), (1728, 256),
         (0, 256), (512, 256), (256, 256), (768, 256)]
NIN, NOUT = 2 * len(PAIRS), KD
NCHUNK = NIN + NOUT
ACT_CHUNKS = [c for c in range(NIN) if c // 2 in (KV_KR, Q_LAT, S_Q, S_G, M_G0, M_G1, CV_G) or c == 2 * SK_SV]
SPLIT_AFTER = S_G + 1

N_SHIFT_SCALE, N_GATE = 8, 4


def plan_loads(last):
    loads = [("in", i) for i in range(2, len(PAIRS))] + [("uq", 0), ("ukv", 0)]
    loads += [("gate", i) for i in range(N_GATE)]
    loads += [] if last else [("next", i) for i in range(N_SHIFT_SCALE)]
    slots = [n % 2 for n in range(len(loads))]
    outs = [("out", i) for i in range(NOUT // 2)]
    slots += [(len(loads) + n) % 2 for n in range(len(outs))]
    loads += outs
    if not last:
        loads += [("after", 0), ("after", 1)]
        slots += [0, 1]
    landed, plan = [0, 0], {}
    for x, slot in zip(loads, slots):
        landed[slot] += 16 * {"out": 3, "uq": 4}.get(x[0], 2 if x in (("in", CV_H), ("next", 0)) else 1)
        plan[x] = (slot, landed[slot])
    plan[("in", 0)], plan[("in", 1)] = (0, 0), (1, 0)
    return loads, plan, landed


V_G, V_BMOD, V_QG, V_KVG, V_CONV, V_ROWS = 0, 8, 32, 34, 35, 41

SLOTS = 8
CACHE_SLOTS = 5


def plan_attention():
    groups, job, unit = [], 0, 0

    def add(kind, idx, jobs, keys):
        nonlocal job, unit
        units = 1 if kind == "mla_s" else len(keys)
        groups.append(dict(kind=kind, idx=idx, jobs=list(range(job, job + jobs)), keys=keys,
                           units=list(range(unit, unit + units))))
        job += jobs
        unit += units

    for t in range(ST):
        add("swa_p", t, 1, [t - 1, t] if t else [t])
    add("swa_s", ST, HEADS, list(range(5)))
    for t in range(ST):
        add("mla_p", t, HEADS, list(range(t + 1)))
    for b in range(NB):
        add("mla_s", b, 1, list(range(5)))
    return groups, job, unit


GROUPS, NJOBS, NUNITS = plan_attention()
GROUP_OF = {j: g for g in GROUPS for j in g["jobs"]}
UNIT_OF = {n: g for g in GROUPS for n in g["units"]}
LAST = len(GROUPS) - 1
N_SWA = sum(g["kind"][:3] == "swa" for g in GROUPS)
N_MLA = len(GROUPS) - N_SWA

GATE_AT = dict(zip((3, 6, 9, 11), range(N_GATE)))
NEXT_AT = dict(zip((12, 14, 16, 17, 18, 19, 20, 21), range(N_SHIFT_SCALE)))
FIRST_S = [g["kind"] for g in GROUPS].index("mla_s")


def slot_of(j):
    g = GROUP_OF[j]
    i = g["jobs"].index(j)
    if g["kind"] == "swa_p":
        return j % 4
    if g["kind"] == "swa_s":
        return (4, 5, 0, 1)[i]
    if g["kind"] == "mla_p":
        return ((2, 3, 6, 7), (4, 5, 0, 1))[g["idx"] % 2][i]
    return 2 + g["idx"] % 2


SLOT_FREE = {}
for _j in range(NJOBS):
    _same = [i for i in range(_j) if slot_of(i) == slot_of(_j)]
    SLOT_FREE[_j] = GROUP_OF[_same[-1]]["units"][-1] if _same else None


def plan_steps():
    steps, done = [], {"exp": -1, "norm": -1, "turn": -1, "scores": -1}

    def put(what, i):
        steps.append((what, i))
        if what in done:
            done[what] = i

    def exps(upto):
        while done["exp"] < min(upto, done["scores"]):
            j = done["exp"] + 1
            if SLOT_FREE[j] is not None and SLOT_FREE[j] > done["turn"]:
                return
            put("exp", j)

    def norms(upto):
        while done["norm"] < min(upto, done["exp"]):
            put("norm", done["norm"] + 1)

    def scores():
        put("scores", done["scores"] + 1)
        put("maxima", done["scores"])

    scores()
    scores()
    exps(1)
    norms(0)
    for gi, g in enumerate(GROUPS):
        ahead = GROUPS[gi + 1]["jobs"][-1] + 1 if gi < LAST else NJOBS - 1
        js = list(range(done["scores"] + 1, min(ahead, NJOBS - 1) + 1))
        units = g["units"]
        at = [len(units) * i // len(js) for i in range(len(js))]
        cached = gi + 3 if gi + 3 <= LAST and GROUPS[min(gi + 3, LAST)]["kind"] in ("swa_s", "mla_s") else None
        if cached:
            put("cache", (cached, 0))
        for q, n in enumerate(units):
            if q == 0:
                for _ in range(at.count(0)):
                    exps(done["scores"] - 1)
                    scores()
                if cached and GROUPS[cached]["kind"] == "mla_s":
                    put("cache", (cached, 1))
                put("turn", n)
                put("copy", n)
                if gi and GROUPS[gi - 1]["kind"] == "mla_p":
                    put("up", gi - 1)
                if gi in GATE_AT or gi in NEXT_AT:
                    put("mod", gi)
            else:
                for _ in range(at.count(q)):
                    if done["exp"] < done["scores"] - 1:
                        exps(done["scores"] - 1)
                    if done["exp"] >= done["scores"] - 1:
                        scores()
            if q + 1 < len(units):
                put("turn", n + 1)
                put("copy", n + 1)
            put("weigh", n)
            if n == units[-1]:
                put("out", gi)
            before = done["exp"]
            exps(done["scores"])
            norms(before)
        while js and done["scores"] < js[-1]:
            exps(done["scores"] - 1)
            scores()
        if gi < LAST:
            exps(GROUPS[gi + 1]["jobs"][-1])
            norms(GROUPS[gi + 1]["jobs"][-1])
    put("up", LAST)
    return steps


STEPS = plan_steps()
N_STORES = 10
DVE_STEPS, ACT_STEPS = 206, 92


class Signal:

    def __init__(self, nc, name, per, first=0):
        self.sem, self.per, self.name, self.first = nc.alloc_semaphore(name), per, name, first

    def at(self, layer, k):
        return layer * self.per + k + self.first


class Lane:

    def __init__(self, eng, layer, own=None):
        self.eng, self.layer, self.own, self.count = eng, layer, own, {}

    def wait(self, sig, k):
        self.eng.wait_ge(sig.sem, sig.at(self.layer, k))

    def link(self, ins, sig=None):
        sig = sig or self.own
        ins.then_inc(sig.sem, 1)
        self.count[sig.name] = self.count.get(sig.name, 0) + 1
        self.wait(sig, self.count[sig.name])


def build(nc, io):
    H_AT, X_AT, G_AT, RAW_AT, SPL_AT, TAB_AT, ZT_AT, SM_AT = (
        0, 73728, 115200, 152064, 168448, 184832, 194048, 203424)

    base = -(-nc.sbuf_base // 32) * 32

    def at(name, off, shape, dt=F32):
        return nc.alloc_sbuf_tensor_at(name, shape, dt, offset=base + off)

    h_hi = at("h_hi", H_AT, [P, KD, NTOK], F32R)
    h_lo = at("h_lo", H_AT + 36864, [P, KD, NTOK], F32R)
    x = at("x", X_AT, [P, KD, NTOK])
    vrows = at("vrows", X_AT + 36864, [V_ROWS, P])
    ccrow = at("ccrow", X_AT + 37376, [2 * NB, CONVW])
    cq = at("cq", X_AT, [P, 2, NTOK])
    ckvT = at("ckvT", X_AT + 9216, [P, NTOK])
    ckv = at("ckv", X_AT + 13824, [P, TILES, P])
    krT = at("krT", X_AT + 18432, [P, NTOK])
    sqT = at("sqT", X_AT + 23040, [P, 2, NTOK])
    skT = at("skT", X_AT + 32256, [P, NTOK])
    sv = at("sv", X_AT + 36864, [P, TILES, P])
    cache_at = [X_AT, X_AT + 4096, X_AT + 32256, X_AT + 23040, X_AT + 27136]
    raw_ckv = [at(f"raw_ckv{i}", a, [P, 4, P]) for i, a in enumerate(cache_at)]
    raw_kr = [at(f"raw_kr{i}", a + 2048, [P, 4, P]) for i, a in enumerate(cache_at)]
    mix = at("mix", G_AT, [P, KD, NTOK])
    tok = at("tok", G_AT, [P, TILES, D])
    raw = at("raw", RAW_AT, [P, 2, KD, 256])
    w_hi = [at(f"w_hi{s}", SPL_AT + 8192 * s, [P, KD, P], F32R) for s in range(2)]
    w_lo = [at(f"w_lo{s}", SPL_AT + 8192 * s + 4096, [P, KD, P], F32R) for s in range(2)]
    w_uq = at("w_uq", RAW_AT + 8192, [P, 2, 768])
    w_uv = at("w_uv", SPL_AT, [P, HEADS, P])
    w_ukT = at("w_ukT", SPL_AT + 6144, [P, HEADS, P])
    w_ukv = at("w_ukv", RAW_AT, [P, HEADS, 256])
    kr_tok = at("kr_tok", SPL_AT + 12288, [P, TILES, 64])
    sk_tok = at("sk_tok", SPL_AT + 14592, [P, 2, P])
    crow = at("crow", SPL_AT, [1 + NB, D])
    frow = at("frow", SPL_AT + 8192, [KD, P])
    csil = at("csil", SPL_AT + 4096, [1 + NB, D])
    tab = at("tab", TAB_AT, [P, 2, NTOK])
    qas = at("qas", ZT_AT + 2048, [P, NB, 64])
    rot = at("rot", ZT_AT, [P, NTOK])
    svT = at("svT", ZT_AT + 4608, [P, NTOK])
    UW = 2 + SEQ + NB * (TS + 2)
    u = at("u", ZT_AT, [P, 2, UW])
    w_uqT = at("w_uqT", SPL_AT + 2048, [P, HEADS, 2 * P])
    mq = at("mq", SPL_AT + 8192, [P, 2, HEADS, P])
    probs_lo = at("probs_lo", H_AT, [P, 6, 1024])
    probs_hi = at("probs_hi", X_AT + 23040, [P, 2, 1024])
    qa = at("qa", H_AT + 24576, [P, HEADS, NTOK])
    qr = at("qr", H_AT + 43008, [P, 2, NTOK])
    pT = at("pT", H_AT + 52224, [P, 3, 512])
    oL = at("oL", H_AT + 58368, [P, 2, HEADS, P])
    ckvT_c = [at("ckvT_c0", H_AT + 62464, [P, 512]), at("ckvT_c1", H_AT + 66560, [P, 512])]
    krT_c = [at("krT_c0", H_AT + 64512, [P, 512]), at("krT_c1", H_AT + 68608, [P, 512])]
    sk_c = at("sk_c", H_AT + 66560, [P, 4, P])
    sv_c = at("sv_c", H_AT + 68608, [P, 4, P])
    skT_c = at("skT_c", H_AT + 70656, [P, 512])

    small = [SM_AT]

    def sm(name, shape, dt=F32):
        size = int(np.prod(shape[1:])) * (2 if dt == BF16 else 4)
        t = at(name, small[0], shape, dt)
        small[0] += -(-size // 32) * 32
        return t

    ident = sm("ident", [P, P])
    ones = sm("ones", [P, 1])
    mhalf = sm("mhalf", [P, TILES])
    vec = sm("vec", [P, V_ROWS])
    convc = sm("convc", [P, 2, 2 * NB])
    mod = sm("mod", [P, 3, KD, 1 + NB])
    amul = sm("amul", [P, KD, 1 + NB])
    cT = sm("cT", [P, KD, 1 + NB])
    fing = sm("fing", [P, KD])
    sink = sm("sink", [P, HEADS])
    nsink = sm("nsink", [P, HEADS])
    state = sm("state", [P, 2, 2 + 2 * NB])
    masks = sm("masks", [8, 128 + 640 + 128 + 256 + 512], BF16)
    mean = sm("mean", [P, TILES])
    rstd = sm("rstd", [P, TILES])
    meanl = sm("meanl", [P, 2, TILES])
    rstdl = sm("rstdl", [P, 2, TILES])
    qrs = sm("qrs", [P, NB, 64])
    state_tok = at("state_tok", H_AT + 72704, [2 + 2 * NB, CONVW])
    smax = sm("smax", [P, SLOTS, HEADS])
    nmax = sm("nmax", [P, SLOTS, HEADS])
    esink = sm("esink", [P, SLOTS, HEADS])
    psum_p = sm("psum_p", [P, SLOTS, HEADS])
    rinv = sm("rinv", [P, SLOTS, HEADS])
    assert base + small[0] <= nc.sbuf_usable_end, small[0]
    masks_f = at("masks_f", ZT_AT, [8, masks.shape[1]])
    own64 = masks[:, 1152:1664]
    own8, block_mask, half_rows, band_mask = (masks[:, 0:128], masks[:, 128:768], masks[:, 768:896],
                                              masks[:, 896:1152])

    psum = nc.alloc_psum_tensor("psum", [P, 8, 512], F32)
    modw = at("modw", H_AT, [P, KD, 2 * D])
    xT = nc.dram_tensor("xT_scratch", (P, KD, NTOK), F32).ap()

    def sg(name, per=0, first=0):
        return Signal(nc, name, per, first)

    plans = {last: plan_loads(last) for last in (False, True)}
    w_in = [sg(f"weights_landed{s}", plans[False][2][s], 16) for s in range(2)]
    vec_in = sg("vectors_landed", 16 * 7, 16 * 7)
    tab_in = sg("rope_table_landed", 16 * 2, 16)
    swc_in = sg("swa_cache_landed", 32)
    mlc_in = [sg(f"mla_cache_landed{s}", 48 * len(range(s, NB, CACHE_SLOTS))) for s in range(CACHE_SLOTS)]
    x_in = [sg(f"residual_landed{s}", 16) for s in range(2)]
    x_out = sg("residual_stored", 16 * KD, 16)
    outs = sg("states_stored", 16 * N_STORES)
    small_T = sg("vectors_turned", 1, 1)
    small_v = sg("vectors_ready", 2, 2)
    sq_x = sg("x_squared", KD, KD)
    sum_x = sg("x_summed", 1, 1)
    mean_x = sg("x_mean_ready", 1, 1)
    rstd_x = sg("x_rstd_ready", 1, 1)
    bc_x = sg("x_rstd_spread", NBLK)
    scaled_x = sg("x_scaled", 2 * NBLK)
    gate_mm = sg("gate_summed", N_GATE)
    gate_c = sg("gate_copied", N_GATE)
    next_mm = sg("next_modulation_summed", N_SHIFT_SCALE)
    next_c = sg("next_modulation_copied", N_SHIFT_SCALE)
    mod_v = sg("modulation_ready", 1, 1)
    h_smp = sg("h_sample_modulated", 1)
    hi_h = sg("h_hi_ready", 4 * NBLK)
    lo_h = sg("h_lo_ready", 4 * NBLK)
    hi_w = sg("w_hi_ready", NCHUNK)
    lo_w = sg("w_lo_ready", NCHUNK)
    z_done = sg("chunk_summed", NCHUNK, 1)
    z_act = sg("chunk_read_by_scalar", len(ACT_CHUNKS))
    z_dve = sg("chunk_read_by_vector", NCHUNK, 1)
    roped = sg("rope_done", 4 + 2 * NBLK)
    lat_sum = sg("latents_summed", 1)
    lat_mean = sg("latent_means_ready", 2)
    lat_rstd = sg("latent_rstds_ready", 2)
    lat_bc = sg("latent_rstds_spread", 2 * NBLK)
    lat_ok = sg("latents_normed", 2 * NBLK)
    svt_T = sg("swa_values_turned", 3)
    svt_c = sg("swa_values_copied", 3)
    w_uv_ok = sg("w_uv_ready", 1)
    turn_T = sg("states_turned", 9)
    turn_c = sg("states_copied", 9)
    qr_mm = sg("q_rope_summed", 2 * NBLK)
    qr_rot = sg("q_rope_rotated", 2 * NBLK)
    mq_mm = sg("q_weights_summed", 2)
    mq_c = sg("q_weights_copied", 2)
    qa_mm = sg("q_latent_summed", HEADS * NBLK)
    qa_c = sg("q_latent_copied", HEADS * NBLK)
    qas_ok = sg("q_latent_sample_ready", 2)
    qrs_ok = sg("q_rope_sample_ready", 1)
    score = sg("scores_ready", NJOBS)
    negmax = sg("negmax_ready", NJOBS)
    expd = sg("exp_ready", NJOBS)
    p_ok = sg("probs_ready", NJOBS)
    pt_T = sg("probs_turned", NUNITS)
    pt_c = [sg("probs_turned_copied_by_scalar", (NUNITS + 1) // 2), sg("probs_turned_copied_by_vector", NUNITS // 2)]
    pv = sg("values_weighted", NUNITS)
    swa_ok = sg("swa_gated", N_SWA)
    ol_c = sg("latent_out_copied", N_MLA)
    conv_ok = sg("convolution_gated", 1)
    uv_mm = sg("mla_out_summed", TILES)
    uv_ok = sg("mla_gated", TILES)
    ct_T = sg("caches_turned", 1 + 2 * NB)
    ct_c = sg("caches_copied", 1 + 2 * NB)
    act_before = sg("scalar_step_before")
    dve_before = sg("vector_step_before")
    act_step = sg("scalar_step", ACT_STEPS)
    dve_step = sg("vector_step", DVE_STEPS)
    s_const = sg("constants_landed")
    s_tok = [sg(f"tokens_landed{i}") for i in range(3)]
    s_modw = [sg(f"first_modulation_landed{i}") for i in range(4)]
    s_mod = sg("first_modulation_summed")
    s_modc = sg("first_modulation_copied")
    s_c = sg("c_landed")
    s_cs = sg("c_silu")
    s_cT = sg("c_turned")
    s_xT = sg("tokens_turned")
    s_xa = sg("tokens_copied_by_scalar")
    s_xv = sg("tokens_copied_by_vector")
    s_cst = sg("constants_made")
    s_y = sg("y_normed")
    s_yT = sg("y_turned")
    s_ya = sg("y_copied_by_scalar")
    s_yv = sg("y_copied_by_vector")
    s_out = sg("y_stored")

    def zset(c):
        return psum[:, 3 * (c % 2):3 * (c % 2) + 3, 0:BLK]

    def b3(t):
        return t.rearrange("p (n t) -> p n t", t=BLK)

    def blk(n):
        return slice(n * BLK, (n + 1) * BLK)

    def spread(ap, n):
        return ap.unsqueeze(2).broadcast_to([ap.shape[0], ap.shape[1], n])

    def tile(t):
        return slice(t * P, (t + 1) * P)

    HALVES = (slice(0, 64), slice(64, 128))
    QUADS = [(0, 32), (32, 0), (64, 96), (96, 64)]

    def w_views(c, last):
        if c >= NIN:
            s = plans[last][1][("out", (c - NIN) // 2)]
            src = raw[:, s[0], :, (c % 2) * P:(c % 2 + 1) * P]
            return s, src, lambda w: w[:, :, :]
        pair = c // 2
        s = plans[last][1][("in", pair)]
        r = raw[:, s[0], :, :]
        if pair == KV_KR and c % 2 == 1:
            src = r[:, :, 128:192].unsqueeze(2).broadcast_to([P, KD, 2, 64])
            return s, src, lambda w: w[:, :, :].rearrange("p k (a d) -> p k a d", a=2)
        if pair in (S_Q, S_G):
            g = c % 2
            src = r.rearrange("p k (a g d) -> p k g a d", a=2, g=2)[:, :, g]
            return s, src, lambda w: w[:, :, :].rearrange("p k (a d) -> p k a d", a=2)
        return s, r[:, :, (c % 2) * P:(c % 2 + 1) * P], lambda w: w[:, :, :]

    def job_shape(j):
        g = GROUP_OF[j]
        if g["kind"] == "swa_p":
            return P, HEADS, P * len(g["keys"]), True
        if g["kind"] == "swa_s":
            return P, 1, 640, True
        if g["kind"] == "mla_p":
            return P, 1, P * len(g["keys"]), False
        return HEADS * TS, 1, 640, False

    def s_view(j):
        rows, nh, w, _ = job_shape(j)
        s = psum[0:rows, 2 * (j % 2):2 * (j % 2) + 2, :].rearrange("p a b -> p (a b)")
        if nh == 1:
            return s[:, 0:w].unsqueeze(1)
        return s.rearrange("p (h w) -> p h w", h=HEADS)[:, :, 0:w]

    def probs(j):
        s = slot_of(j)
        return probs_lo[:, s, :] if s < 6 else probs_hi[:, s - 6, :]

    def p_view(j):
        rows, nh, w, _ = job_shape(j)
        s = probs(j)[0:rows, :]
        if nh == 1:
            return s[:, 0:w].unsqueeze(1)
        return s.rearrange("p (h w) -> p h w", h=HEADS)[:, :, 0:w]

    with nc.Block() as block:

        @block.sync
        def _(sp):
            sp.dma_start(ident[:], io["c_ident"]).then_inc(s_const.sem, 16)
            sp.dma_start(masks_f[:], io["c_masks"]).then_inc(s_const.sem, 16)
            sp.dma_start(crow[0:1, :], io["c_prompt"]).then_inc(s_c.sem, 16)
            sp.dma_start(crow[1:1 + NB, :], io["c_sample"]).then_inc(s_c.sem, 16)
            sp.dma_start(frow[:], io["final_norm_g"].rearrange("(k p) -> k p", p=P)).then_inc(s_c.sem, 16)
            xp = io["x_prompt"].rearrange("b (t p) d -> p (b t) d", p=P)
            for i, (a, b) in enumerate(((0, 4), (4, 8))):
                sp.dma_start(tok[:, a:b, :], xp[:, a:b, :]).then_inc(s_tok[i].sem, 16)
            sp.dma_start(tok[:, ST, :], io["x_sample"].rearrange("b t d -> (b t) d")).then_inc(s_tok[2].sem, 16)
            for k in range(KD):
                sp.dma_start(modw[:, k, :], io["w_mod"][0, tile(k), 0:2 * D]).then_inc(s_modw[k // 2].sem, 16)

            def load_pair(layer, i, slot):
                c0, w = PAIRS[i]
                src = io["w_in"][layer].rearrange("(k p) n -> p k n", p=P)[:, :, c0:c0 + w]
                for ks in ((slice(4, 8), slice(0, 4)) if i == CV_H else (slice(0, KD),)):
                    sp.dma_start(raw[:, slot, ks, 0:w], src[:, ks]).then_inc(w_in[slot].sem, 16)

            def load_vectors(layer):
                for a, b, name in ((V_G, V_BMOD, "norm_g"), (V_BMOD, V_QG, "b_mod"), (V_QG, V_KVG, "q_norm_g"),
                                   (V_KVG, V_CONV, "kv_norm_g")):
                    sp.dma_start(vrows[a:b, :], io[name][layer].rearrange("(r c) -> r c", c=P))\
                        .then_inc(vec_in.sem, 16)
                sp.dma_start(vrows[V_CONV:V_ROWS, :], io["conv_w"][layer].rearrange("k (j c) -> (k j) c", c=P))\
                    .then_inc(vec_in.sem, 16)
                sp.dma_start(ccrow[:], io["cache_conv"][layer].rearrange("b t c -> (b t) c")).then_inc(vec_in.sem, 16)
                sp.dma_start(sink[:], io["swa_sink"][layer].unsqueeze(0).broadcast_to([P, HEADS]))\
                    .then_inc(vec_in.sem, 16)

            load_vectors(0)
            load_pair(0, 0, 0)
            load_pair(0, 1, 1)
            sp.dma_start(tab[:], io["c_rope"][0]).then_inc(tab_in.sem, 16)
            sp.wait_ge(s_xa.sem, TILES)
            sp.wait_ge(s_xv.sem, TILES)
            sp.dma_start(xT, x[:]).then_inc(x_out.sem, 16)

            def layer(L, last):
                lane = Lane(sp, L)
                loads, plan, _ = plans[last]

                def free(x):
                    kind, i = x
                    if kind in ("in", "out"):
                        lane.wait(lo_w, 2 * i + 2 + (NIN if kind == "out" else 0))
                    elif kind == "uq":
                        lane.wait(qr_mm, 2 * NBLK)
                    elif kind == "ukv":
                        lane.wait(w_uv_ok, 1)
                    elif kind == "gate":
                        lane.wait(gate_mm, i + 1)
                    else:
                        lane.wait(next_mm, i + 1)

                def load(x):
                    kind, i = x
                    slot = plan[x][0]
                    before = [y for y in [("in", 0), ("in", 1)] + loads[:loads.index(x)] if plan[y][0] == slot][-1]
                    free(before)
                    sem = w_in[slot].sem
                    if kind in ("gate", "next"):
                        lm, col = (L, 2 * D + 256 * i) if kind == "gate" else (L + 1, 256 * i)
                        src = io["w_mod"][lm].rearrange("(k p) n -> p k n", p=P)[:, :, col:col + 256]
                        for ks in ((slice(4, 8), slice(0, 4)) if col == 0 else (slice(0, KD),)):
                            sp.dma_start(raw[:, slot, ks], src[:, ks]).then_inc(sem, 16)
                    elif kind == "in":
                        load_pair(L, i, slot)
                    elif kind == "after":
                        load_pair(L + 1, i, slot)
                    elif kind == "ukv":
                        sp.dma_start(w_ukv[:], io["w_ukv"][L].rearrange("p (h n) -> p h n", h=HEADS)).then_inc(sem, 16)
                    elif kind == "uq":
                        for k in range(2):
                            src = io["w_uq"][L, tile(k)].rearrange("p (h c) -> p h c", h=HEADS)
                            for a, w in ((P, 64), (0, P)):
                                dst = w_uq[:, k, HEADS * a:HEADS * (a + w)].rearrange("p (h c) -> p h c", h=HEADS)
                                sp.dma_start(dst, src[:, :, a:a + w]).then_inc(sem, 16)
                    else:
                        cols = slice(256 * i, 256 * i + 256)
                        src = io["w_out"][L, 0:768].rearrange("(k p) n -> p k n", p=P)[:, :, cols]
                        for kv in range(2):
                            src2 = io["w_out"][L, 768 + 128 * kv:896 + 128 * kv].rearrange(
                                "(g p) n -> p g n", g=2)[:, :, cols]
                            sp.dma_start(raw[HALVES[kv], slot, 6:8, :], src2).then_inc(sem, 16)
                        sp.dma_start(raw[:, slot, 0:6, :], src).then_inc(sem, 16)

                def rope_table(which, used):
                    lane.wait(roped, used)
                    sp.dma_start(tab[:], io["c_rope"][which]).then_inc(tab_in.sem, 16)

                def cache(b):
                    s = b % CACHE_SLOTS
                    if b < 2:
                        lane.wait(qa_mm, HEADS * NBLK)
                    elif b == 2:
                        lane.wait(pv, GROUPS[ST]["units"][-1] + 1)
                    elif b < CACHE_SLOTS:
                        lane.wait(pv, GROUPS[FIRST_S - 2]["units"][-1] + 1)
                    else:
                        lane.wait(pv, GROUPS[FIRST_S + b - CACHE_SLOTS]["units"][-1] + 1)
                    sp.dma_start(raw_ckv[s][:], io["cache_mla_ckv"][L, b].rearrange("(t p) c -> p t c", p=P))\
                        .then_inc(mlc_in[s].sem, 16)
                    for half in HALVES:
                        sp.dma_start(raw_kr[s][:, :, half],
                                     io["cache_mla_krope"][L, b].rearrange("(t p) c -> p t c", p=P))\
                            .then_inc(mlc_in[s].sem, 16)

                for x_ in loads[:len(PAIRS) - 2]:
                    load(x_)
                    if x_ == ("in", S_Q):
                        rope_table(1, 1)
                    elif x_ == ("in", CV_H):
                        rope_table(0, 4)
                load(("uq", 0))
                load(("ukv", 0))
                lane.wait(z_done, NIN)
                for dst, name in ((sk_c, "cache_swa_k"), (sv_c, "cache_swa_v")):
                    sp.dma_start(dst[:], io[name][L].rearrange("b s h d -> (b s) (h d)")
                                 .rearrange("(t p) c -> p t c", p=P)).then_inc(swc_in.sem, 16)
                when = {("gate", i): gi for gi, i in GATE_AT.items()}
                when.update({("next", i): gi for gi, i in NEXT_AT.items()})
                when.update({("uq", 0): -2, ("ukv", 0): -3})
                todo = [(-1 if b < 2 else ST + 0.5 if b == 2 else FIRST_S - 1.5 if b < CACHE_SLOTS
                         else FIRST_S + b - CACHE_SLOTS + 0.5, cache, b) for b in range(NB)]
                for x_ in [x for x in loads if x[0] in ("gate", "next") or x in (("out", 0), ("out", 1))]:
                    slot = plan[x_][0]
                    before = [y for y in loads[:loads.index(x_)] if plan[y][0] == slot][-1]
                    todo.append((when[before], load, x_))
                for _, do, what in sorted(todo, key=lambda e: e[0]):
                    do(what)
                lane.wait(x_out, 0)
                lane.wait(hi_w, NIN + 1)
                for i in range(2):
                    sp.dma_start(x[:, 4 * i:4 * i + 4, :], xT[:, 4 * i:4 * i + 4, :]).then_inc(x_in[i].sem, 16)
                load(("out", 2))
                load(("out", 3))
                if last:
                    return
                load_vectors(L + 1)
                for k in range(KD):
                    lane.wait(z_dve, NIN + k + 1)
                    sp.dma_start(xT[:, k, :], x[:, k, :]).then_inc(x_out.sem, 16)
                    if k in (3, 5):
                        load(("after", (5 - k) // 2))

            with sp.Fori(0, DEPTH - 1) as L:
                layer(L, False)
            layer(DEPTH - 1, True)
            for t in range(TILES):
                sp.wait_ge(s_ya.sem, t + 1)
                sp.wait_ge(s_yv.sem, t + 1)
                dst = (io["y_sample"].rearrange("b t d -> (b t) d") if t == ST
                       else io["y_prompt"][0, tile(t), :])
                sp.dma_start(dst, tok[:, t, :]).then_inc(s_out.sem, 16)
            sp.wait_ge(s_out.sem, 16 * TILES)
            sp.wait_ge(outs.sem, outs.at(DEPTH, 0))
            sp.wait_ge(x_out.sem, x_out.at(DEPTH - 1, 0))

        @block.gpsimd
        def _(pool):
            pool.memset(ones[:], 1.0).then_inc(s_cst.sem, 1)
            pool.memset(mhalf[:], -0.5).then_inc(s_cst.sem, 1)
            pool.memset(qrs[:], 0.0).then_inc(s_cst.sem, 1)
            pool.wait_ge(s_cst.sem, 4)

            def x_rstd(lane, before):
                lane.wait(mean_x, 1)
                if before:
                    lane.wait(bc_x, NBLK)
                pool.tensor_tensor(rstd[:], mean[:], mhalf[:], ALU.pow).then_inc(rstd_x.sem, 1)

            def layer(L, last):
                lane = Lane(pool, L)
                for i in range(2):
                    lane.wait(lat_mean, i + 1)
                    pool.tensor_tensor(rstdl[:, i, :], meanl[:, i, :], mhalf[:], ALU.pow).then_inc(lat_rstd.sem, 1)
                x_rstd(lane, True)

            x_rstd(Lane(pool, -1), False)
            with pool.Fori(0, DEPTH - 1) as L:
                layer(L, False)
            layer(DEPTH - 1, True)

        @block.tensor
        def _(pe):
            def x_sums(lane, ks):
                for k in ks:
                    lane.wait(sq_x, k + 1)
                    for t in range(TILES):
                        mm = pe.matmul(psum[:, 6, t:t + 1], mix[:, k, tile(t)], ones[:],
                                       start=(k == 0 and t == 0), stop=(k == KD - 1 and t == TILES - 1))
                if KD - 1 in ks:
                    mm.then_inc(sum_x.sem, 1)

            def turn_vectors(lane):
                lane.wait(vec_in, 16 * 7)
                pe.matmul(psum[:, 7, 0:V_ROWS], vrows[:], ident[0:V_ROWS, 0:V_ROWS], start=True, stop=True)
                for j in range(2):
                    mm = pe.transpose(psum[:, 7, 64 + 16 * j:80 + 16 * j], ccrow[:, tile(j)], ident[0:16, 0:16])
                mm.then_inc(small_T.sem, 1)

            def x_spread(lane, final=False):
                for n in range(NBLK):
                    if n == 0:
                        lane.wait(rstd_x, 0)
                    elif n == 1 and not final:
                        lane.wait(mod_v, 0)
                    elif n == 2:
                        lane.wait(scaled_x, 2)
                    for i in range(3):
                        mm = pe.matmul(psum[:, 6 + n % 2, tile(i)],
                                       rstd[:, 3 * n + i:3 * n + i + 1].broadcast_to([P, P]),
                                       ident[:], start=True, stop=True)
                    mm.then_inc(bc_x.sem, 1)

            pe.wait_ge(s_const.sem, 32)
            pe.wait_ge(s_cst.sem, 4)
            bank = 0
            for t in range(TILES):
                pe.wait_ge(s_tok[min(t // 4, 2)].sem, 16)
                for half in range(2):
                    n = 2 * t + half
                    if t >= 2:
                        pe.wait_ge((s_xa, s_xv)[half].sem, t - 1)
                    for k in range(4):
                        mm = pe.transpose(psum[:, n % 4, tile(k)], tok[:, t, tile(4 * half + k)], ident[:])
                    mm.then_inc(s_xT.sem, 1)
            pe.wait_ge(s_cs.sem, 3)
            for k in range(KD):
                mm = pe.transpose(psum[:, 5, 16 * k:16 * k + 1 + NB], csil[:, tile(k)], ident[0:1 + NB, 0:1 + NB])
            mm = pe.transpose(psum[:, 5, 256:256 + KD], frow[:], ident[0:KD, 0:KD])
            mm.then_inc(s_cT.sem, 1)
            pe.wait_ge(s_cT.sem, 3)

            for k in range(KD):
                if k % 2 == 0:
                    pe.wait_ge(s_modw[k // 2].sem, 32)
                for i in range(2 * KD):
                    mm = pe.matmul(psum[:, 7, i * (1 + NB):(i + 1) * (1 + NB)], modw[:, k, tile(i)], cT[:, k, :],
                                   start=(k == 0 and i == 0), stop=(k == KD - 1 and i == 2 * KD - 1))
            mm.then_inc(s_mod.sem, 1)
            before = Lane(pe, -1)
            x_sums(before, range(KD))
            pe.wait_ge(s_modc.sem, 1)
            turn_vectors(before)
            pe.sem_inc(z_done.sem, 1)

            def layer(L, last):
                lane = Lane(pe, L)
                plan = plans[last][1]

                def modulation(kind, i, sig):
                    s, count = plan[(kind, i)]
                    lane.wait(w_in[s], count)
                    for j in range(2):
                        for k in range(KD):
                            mm = pe.matmul(psum[:, 7, j * (1 + NB):(j + 1) * (1 + NB)], raw[:, s, k, tile(j)],
                                           cT[:, k, :], start=(k == 0), stop=(k == KD - 1))
                    mm.then_inc(sig.sem, 1)

                def chunk(c, s):
                    lane.wait(lo_w, c + 1)
                    lane.wait(z_dve, c - 1)
                    for n in range(NBLK):
                        for k in range(KD):
                            for i, (w, h) in enumerate(((w_hi, h_hi), (w_lo, h_hi), (w_hi, h_lo))):
                                mm = pe.matmul(psum[:, 3 * s + n, 0:BLK], w[s][:, k, :], h[:, k, blk(n)],
                                               start=(k == 0 and i == 0), stop=(k == KD - 1 and i == 2))
                    mm.then_inc(z_done.sem, 1)

                def first_chunks(c, base):
                    lane.wait(lo_w, c + 2)
                    lane.wait(z_dve, c)

                    def part(s, n, half):
                        for k in range(4 * half, 4 * half + 4):
                            for i, (w, h) in enumerate(((w_hi, h_hi), (w_lo, h_hi), (w_hi, h_lo))):
                                mm = pe.matmul(psum[:, 3 * s + n, 0:BLK], w[s][:, k, :], h[:, k, blk(n)],
                                               start=(k == 0 and i == 0), stop=(k == KD - 1 and i == 2))
                        return mm

                    for n in range(NBLK - 1):
                        for half in range(2):
                            lane.wait(lo_h, base + 2 * n + half + 1)
                            part(0, n, half)
                            part(1, n, half)
                    for half in range(2):
                        lane.wait(lo_h, base + 2 * (NBLK - 1) + half + 1)
                        mm = part(0, NBLK - 1, half)
                    mm.then_inc(z_done.sem, 1)
                    part(1, NBLK - 1, 0)
                    part(1, NBLK - 1, 1).then_inc(z_done.sem, 1)

                def chunks(first, end):
                    with pe.Fori(first, end, 2) as c:
                        chunk(c, 0)
                        chunk(c + 1, 1)

                x_spread(lane)
                first_chunks(0, 0)
                chunks(2, 2 * SPLIT_AFTER)

                lane.wait(z_act, 2 * Q_LAT + 2)
                lane.wait(scaled_x, 2 * NBLK)
                for i, parts in enumerate(((0,), (1, 5))):
                    for t in range(TILES):
                        for q, k in enumerate(parts):
                            mm = pe.matmul(psum[:, 6, 16 * i + t:16 * i + t + 1], mix[:, k, tile(t)], ones[:],
                                           start=(q == 0), stop=(q == len(parts) - 1))
                mm.then_inc(lat_sum.sem, 1)
                lane.wait(z_dve, 2 * SK_SV + 2)
                for n in range(3):
                    if n:
                        lane.wait(svt_c, n)
                    for i in range(4 if n < 2 else 1):
                        mm = pe.transpose(psum[:, 7, tile(i)], svT[:, tile(4 * n + i)], ident[:])
                    mm.then_inc(svt_T.sem, 1)
                chunks(2 * SPLIT_AFTER, 2 * SPLIT_AFTER + 2)
                lane.wait(lat_mean, 2)
                lane.wait(svt_c, 3)
                for m in range(2 * NBLK):
                    i, n = divmod(m, NBLK)
                    lane.wait(lat_rstd, i + 1)
                    if m >= 2:
                        lane.wait(lat_ok, m - 1)
                    for t in range(3):
                        mm = pe.matmul(psum[:, 6 + m % 2, tile(t)],
                                       rstdl[:, i, 3 * n + t:3 * n + t + 1].broadcast_to([P, P]), ident[:],
                                       start=True, stop=True)
                    mm.then_inc(lat_bc.sem, 1)
                chunks(2 * SPLIT_AFTER + 2, NIN)

                def turned(n, parts):
                    if n < 2:
                        lane.wait(z_dve, NIN)
                    else:
                        lane.wait(turn_c, n - 1)
                    for out, in_, k in parts:
                        mm = pe.transpose(psum[0:out[0], 4 + n % 2, out[1]:out[1] + k], in_, ident[0:k, 0:k])
                    mm.then_inc(turn_T.sem, 1)

                lane.wait(lat_ok, 2 * NBLK)
                lane.wait(svt_c, 3)
                for n in range(3):
                    turned(n, [((P, P * i), ckvT[:, tile(4 * n + i)], P) for i in range(4 if n < 2 else 1)])
                for i in range(2):
                    turned(3 + i, [((P, 0), skT[:, tile(ST - 1 + i)], P)]
                           + [((P, P + 64 * t), krT[0:64, tile(6 * i + t)], 64) for t in range(6 - 3 * i)])
                turned(5, [((2 + 2 * NB, P * j), state[:, j, :], P) for j in range(2)])
                lane.wait(w_in[plan[("ukv", 0)][0]], plan[("ukv", 0)][1])
                turned(6, [((P, P * h), w_ukv[:, h, 0:P], P) for h in range(HEADS)])

                s_uq, count = plan[("uq", 0)]
                lane.wait(w_in[s_uq], count)
                for k in range(2):
                    turned(7 + k, [((P, P * h), w_uq[:, k, tile(h)], P) for h in range(HEADS)])

                def q_rope(m):
                    n, j = divmod(m, 2)
                    if m >= 2:
                        lane.wait(roped, 4 + m - 1)
                    for k in range(2):
                        w = w_uq[:, k, HEADS * P + P * j:HEADS * P + P * j + P]
                        mm = pe.matmul(psum[:, m % 2, 0:BLK], w, cq[:, k, blk(n)], start=(k == 0), stop=(k == 1))
                    mm.then_inc(qr_mm.sem, 1)

                def q_latent(m):
                    n, h = divmod(m, HEADS)
                    if m >= 2:
                        lane.wait(qa_c, m - 1)
                    for k in range(2):
                        mm = pe.matmul(psum[:, 4 + m % 2, 0:BLK], mq[:, k, h, :], cq[:, k, blk(n)],
                                       start=(k == 0), stop=(k == 1))
                    mm.then_inc(qa_mm.sem, 1)

                q_rope(0)
                q_rope(1)
                lane.wait(turn_c, 9)
                for k in range(2):
                    for h in range(HEADS):
                        mm = pe.matmul(psum[:, 6 + k, tile(h)], w_uqT[:, h, tile(k)], w_ukT[:, h, :], start=True, stop=True)
                    mm.then_inc(mq_mm.sem, 1)
                lane.wait(mq_c, 2)
                for n in range(NBLK):
                    if n:
                        q_rope(2 * n)
                        q_rope(2 * n + 1)
                    for h in range(HEADS):
                        q_latent(HEADS * n + h)

                bank7 = [mq_c, 2]
                turns = [0]
                turned_for = {}
                summed = {"swa": 0, "mla": 0}

                def free_bank7():
                    lane.wait(bank7[0], bank7[1])

                def cache(gi, part):
                    g = GROUPS[gi]
                    if g["kind"] == "swa_s":
                        lane.wait(swc_in, 32)
                        src = sk_c
                    else:
                        s = g["idx"] % CACHE_SLOTS
                        lane.wait(mlc_in[s], 48 * (g["idx"] // CACHE_SLOTS + 1))
                        src = (raw_ckv, raw_kr)[part][s]
                    free_bank7()
                    for i in range(4):
                        mm = pe.transpose(psum[:, 7, tile(i)], src[:, i, :], ident[:])
                    mm.then_inc(ct_T.sem, 1)
                    turns[0] += 1
                    turned_for[gi] = turns[0]
                    bank7[:] = [ct_c, turns[0]]

                def scores(j):
                    g = GROUP_OF[j]
                    gi, t, i = GROUPS.index(g), g["idx"], g["jobs"].index(j)
                    if j >= 2:
                        lane.wait(expd, j - 1)
                    else:
                        lane.wait(roped, 4 + 2 * NBLK)
                    out = psum[:, 2 * (j % 2):2 * (j % 2) + 2, :].rearrange("p a b -> p (a b)")
                    if g["kind"] == "swa_p":
                        ks, w = g["keys"], P * len(g["keys"])
                        for h in range(HEADS):
                            half = HALVES[h // 2]
                            pe.matmul(out[:, 256 * h:256 * h + w], sqT[half, h % 2, tile(t)],
                                      skT[half, ks[0] * P:(t + 1) * P], start=True, stop=False)
                            mm = pe.matmul(out[:, 256 * h:256 * h + w], half_rows[0:2, :], band_mask[0:2, 256 - w:256],
                                           start=False, stop=True)
                    elif g["kind"] == "swa_s":
                        half = HALVES[i // 2]
                        if i == 0:
                            lane.wait(ct_c, turned_for[gi])
                        for a, b, keys in ((0, 512, skT_c[half, :]), (512, 640, skT[half, SEQ:NTOK])):
                            pe.matmul(out[:, a:b], sqT[half, i % 2, tile(ST)], keys, start=True, stop=False)
                            mm = pe.matmul(out[:, a:b], own8, block_mask[:, a:b], start=False, stop=True)
                    elif g["kind"] == "mla_p":
                        if i == 0:
                            lane.wait(qa_c, HEADS * NBLK)
                        w = (t + 1) * P
                        half = HALVES[i % 2]
                        for a in range(0, w, 512):
                            b = min(a + 512, w)
                            pe.matmul(out[:, a:b], qa[:, i, tile(t)], ckvT[:, a:b], start=True, stop=False)
                            mm = pe.matmul(out[:, a:b], qr[half, i // 2, tile(t)], krT[half, a:b],
                                           start=False, stop=(b < w))
                        mm = pe.matmul(out[:, w - CH:w], half_rows[0:1, :], band_mask[0:1, 256 - CH:256],
                                       start=False, stop=True)
                    else:
                        lane.wait(ct_c, turned_for[gi])
                        lane.wait(qas_ok, 2)
                        for a, e, kc, kr_ in ((0, 512, ckvT_c[t % 2][:], krT_c[t % 2][:]),
                                              (512, 640, ckvT[:, SEQ:NTOK], krT[:, SEQ:NTOK])):
                            pe.matmul(out[0:64, a:e], qas[:, t, :], kc, start=True, stop=False)
                            mm = pe.matmul(out[0:64, a:e], qrs[:, t, :], kr_, start=False, stop=(a == 0))
                        mm = pe.matmul(out[0:64, 512:640], own64[:, 64 * t:64 * t + 64], block_mask[:, 512:640],
                                       start=False, stop=True)
                    mm.then_inc(score.sem, 1)

                def turn_probs(n):
                    g = UNIT_OF[n]
                    i = g["units"].index(n)
                    if n >= 2:
                        lane.wait(pt_c[n % 2], n // 2)
                    else:
                        lane.wait(qa_c, HEADS * NBLK)
                    if i == 0:
                        lane.wait(p_ok, g["jobs"][-1] + 1)
                    out = psum[:, 4 + n % 2, :]
                    if g["kind"] == "mla_s":
                        for k in range(5):
                            mm = pe.matmul(out[:, 64 * k:64 * k + 64], probs(g["jobs"][0])[0:64, tile(k)], ident[0:64, 0:64],
                                           start=True, stop=True)
                    else:
                        for h in range(HEADS):
                            if g["kind"] == "swa_p":
                                pr = probs(g["jobs"][0])[:, 256 * h + P * i:256 * h + P * i + P]
                            else:
                                pr = probs(g["jobs"][h])[:, tile(i)]
                            mm = pe.transpose(out[:, tile(h)], pr, ident[:])
                    mm.then_inc(pt_T.sem, 1)

                def weigh(n):
                    g = UNIT_OF[n]
                    i = g["units"].index(n)
                    gi = GROUPS.index(g)
                    last_one = i == len(g["units"]) - 1
                    if i == 0 and gi:
                        if GROUPS[gi - 1]["kind"][:3] == "swa":
                            lane.wait(swa_ok, summed["swa"])
                        else:
                            lane.wait(ol_c, summed["mla"])
                    lane.wait(pt_c[n % 2], n // 2 + 1)
                    if g["kind"] == "mla_s":
                        s = g["idx"] % CACHE_SLOTS
                        for k in range(5):
                            v = raw_ckv[s][:, k, :] if k < 4 else ckv[:, ST, :]
                            mm = pe.matmul(psum[:, 6, 0:64], v, pT[:, n % 3, 64 * k:64 * k + 64],
                                           start=(k == 0), stop=(k == 4))
                    else:
                        k = g["keys"][i]
                        if g["kind"] == "mla_p":
                            v = ckv[:, k, :]
                        elif g["kind"] == "swa_p":
                            v = sv[:, k, :]
                        else:
                            v = sv_c[:, k, :] if k < 4 else sv[:, ST, :]
                        mm = pe.matmul(psum[:, 6, :], v, pT[:, n % 3, :], start=(i == 0), stop=last_one)
                    mm.then_inc(pv.sem, 1)
                    if last_one:
                        summed[g["kind"][:3]] += 1

                mla_done = [0]

                def up_values(gi):
                    slot = GROUPS[gi]["idx"] % 2 if GROUPS[gi]["kind"] == "mla_p" else 0
                    lane.wait(ol_c, gi - ST)
                    free_bank7()
                    for h in range(HEADS):
                        mm = pe.matmul(psum[:, 7, tile(h)], w_uv[:, h, :], oL[:, slot, h, :], start=True, stop=True)
                    mm.then_inc(uv_mm.sem, 1)
                    mla_done[0] += 1
                    bank7[:] = [uv_ok, mla_done[0]]

                for what, i in STEPS:
                    if what == "scores":
                        scores(i)
                    elif what == "turn":
                        turn_probs(i)
                    elif what == "weigh":
                        weigh(i)
                    elif what == "cache":
                        cache(*i)
                    elif what == "up":
                        up_values(i)
                    elif what == "mod" and i in GATE_AT:
                        free_bank7()
                        modulation("gate", GATE_AT[i], gate_mm)
                        bank7[:] = [gate_c, GATE_AT[i] + 1]
                    elif what == "mod" and not last:
                        free_bank7()
                        modulation("next", NEXT_AT[i], next_mm)
                        bank7[:] = [next_c, NEXT_AT[i] + 1]

                first_chunks(NIN, 2 * NBLK)
                chunks(NIN + 2, NCHUNK - 2)
                chunk(NCHUNK - 2, 0)
                x_sums(lane, range(5))
                lane.wait(uv_ok, TILES)
                if not last:
                    turn_vectors(lane)
                chunk(NCHUNK - 1, 1)
                x_sums(lane, range(5, KD))

            with pe.Fori(0, DEPTH - 1) as L:
                layer(L, False)
            layer(DEPTH - 1, True)

            x_spread(Lane(pe, DEPTH), final=True)
            for t in range(TILES):
                if t % 3 == 0:
                    pe.wait_ge(s_y.sem, t // 3 + 1)
                for half in range(2):
                    if t >= 1:
                        pe.wait_ge((s_ya, s_yv)[half].sem, t)
                    for k in range(4):
                        mm = pe.transpose(psum[:, 2 * half, tile(k)], x[:, 4 * half + k, tile(t)], ident[:])
                    mm.then_inc(s_yT.sem, 1)

        @block.scalar
        def _(act):
            act.wait_ge(s_c.sem, 48)
            act.activation(csil[:], crow[:], ACT.Tanh, scale=0.5).then_inc(s_cs.sem, 1)
            for t in range(TILES):
                act.wait_ge(s_xT.sem, 2 * t + 1)
                act.activation(x[:, 0:4, tile(t)], psum[:, (2 * t) % 4, :].rearrange("p (k t) -> p k t", k=4), ACT.Copy)\
                    .then_inc(s_xa.sem, 1)
            act.wait_ge(s_xa.sem, TILES)
            act.wait_ge(s_xv.sem, TILES)
            act.wait_ge(s_cT.sem, 1)

            def x_square(lane, k):
                lane.link(act.activation(mix[:, k, :], x[:, k, :], ACT.Square), sq_x)

            before = Lane(act, -1, act_before)
            for k in range(KD):
                x_square(before, k)

            def layer(L, last):
                lane = Lane(act, L, act_step)

                def split_w(c):
                    (s, count), src, view = w_views(c, last)
                    lane.wait(w_in[s], count)
                    lane.link(act.activation(view(w_hi[c % 2]), src, ACT.Copy), hi_w)

                def rotate(src, pick, sig):
                    for i, (a, b) in enumerate(QUADS):
                        ins = act.activation(pick(rot[a:a + 32, :]), src[b:b + 32], ACT.Copy)
                        lane.link(ins, sig if i == 3 else None)

                def chunk(c):
                    pair, j = divmod(c, 2)
                    z = zset(c)
                    lane.wait(z_done, c + 1)
                    if pair in (KV_KR, Q_LAT) and (pair, j) != (KV_KR, 1):
                        k = {0: 0, 2: 1, 3: 5}[c]
                        lane.link(act.activation(b3(mix[:, k, :]), z, ACT.Square), z_act)
                    elif (pair, j) in ((KV_KR, 1), (SK_SV, 0), (S_Q, 0), (S_Q, 1)):
                        n = {(KV_KR, 1): 0, (SK_SV, 0): 1, (S_Q, 0): 2, (S_Q, 1): 3}[(pair, j)]
                        if n:
                            lane.wait(roped, n)
                        rotate(z, b3, z_act)
                    elif pair in (S_G, M_G0, M_G1):
                        k = {S_G: 6, M_G0: 2, M_G1: 4}[pair] + j
                        if pair == M_G1:
                            lane.wait(lat_sum, 1)
                        lane.link(act.activation(b3(mix[:, k, :]), z, ACT.Tanh, scale=0.5), z_act)
                    elif pair == CV_G:
                        lane.wait(z_dve, 2 * CV_B + 2)
                        dst = (rot, svT)[j]
                        lane.link(act.activation(b3(dst[:]), z, ACT.Tanh, scale=0.5), z_act)

                lane.wait(z_done, 0)
                split_w(0)
                split_w(1)
                lane.wait(mod_v, 0)
                for n in range(NBLK):
                    width = BLK if n < NBLK - 1 else SEQ - (NBLK - 1) * BLK
                    cols = slice(n * BLK, n * BLK + width)
                    for half in range(2):
                        ks = slice(4 * half, 4 * half + 4)
                        lane.wait(scaled_x, 2 * n + half + 1)
                        for k in range(4 * half, 4 * half + 4):
                            lane.link(act.activation(x[:, k, cols], x[:, k, cols], ACT.Identity,
                                                     bias=mod[:, 0, k, 0:1], scale=amul[:, k, 0:1]))
                        if n == NBLK - 1:
                            lane.wait(h_smp, 1)
                        lane.link(act.activation(h_hi[:, ks, blk(n)], x[:, ks, blk(n)], ACT.Copy), hi_h)
                for c in range(NIN):
                    if c + 2 < NIN:
                        lane.wait(z_done, c + 1)
                        split_w(c + 2)
                    if c in ACT_CHUNKS:
                        chunk(c)
                    if c == 2 * SPLIT_AFTER - 1:
                        for n in range(3):
                            lane.wait(svt_T, n + 1)
                            w = 4 if n < 2 else 1
                            lane.link(act.activation(sv[:, 4 * n:4 * n + w, :],
                                                     psum[:, 7, 0:P * w].rearrange("p (t c) -> p t c", c=P), ACT.Copy),
                                      svt_c)
                        for dst, src in ((io["swa_v_prompt"][L, 0].rearrange("s h d -> s (h d)"), sv[64:128, ST - 1, :]),
                                         (io["swa_v_sample"][L].rearrange("b t h d -> (b t) (h d)"), sv[:, ST, :])):
                            act.dma_start(dst, src).then_inc(outs.sem, 16)

                lane.wait(z_done, NIN)
                for n in range(9):
                    lane.wait(turn_T, n + 1)
                    src = psum[:, 4 + n % 2, :]
                    if n < 3:
                        w = 4 if n < 2 else 1
                        out, in_ = ckv[:, 4 * n:4 * n + w, :], src[:, 0:P * w].rearrange("p (t c) -> p t c", c=P)
                    elif n < 5:
                        w = 6 if n == 3 else 3
                        lane.link(act.activation(sk_tok[:, n - 3, :], src[:, 0:P], ACT.Copy))
                        out, in_ = kr_tok[:, 6 * (n - 3):6 * (n - 3) + w, :], src[:, P:P + 64 * w].rearrange(
                            "p (t c) -> p t c", c=64)
                    elif n == 5:
                        out, in_ = state_tok[:], src[0:2 + 2 * NB, 0:CONVW]
                    else:
                        out, in_ = (w_ukT[:] if n == 6 else w_uqT[:, :, tile(n - 7)]), src[:, :].rearrange(
                            "p (h c) -> p h c", c=P)
                    lane.link(act.activation(out, in_, ACT.Copy), turn_c)
                    stores = []
                    if n == 2:
                        stores = [(io["mla_ckv_prompt"][L, 0].rearrange("(t p) c -> p t c", p=P), ckv[:, 0:ST, :]),
                                  (io["mla_ckv_sample"][L].rearrange("b t c -> (b t) c"), ckv[:, ST, :])]
                    elif n == 4:
                        stores = [(io["mla_krope_prompt"][L, 0].rearrange("(t p) c -> p t c", p=P), kr_tok[:, 0:ST, :]),
                                  (io["mla_krope_sample"][L].rearrange("b t c -> (b t) c"), kr_tok[:, ST, :]),
                                  (io["swa_k_prompt"][L, 0].rearrange("s h d -> s (h d)"), sk_tok[64:128, 0, :]),
                                  (io["swa_k_sample"][L].rearrange("b t h d -> (b t) (h d)"), sk_tok[:, 1, :])]
                    elif n == 5:
                        stores = [(io["conv_state_prompt"][L, 0], state_tok[0:2, :]),
                                  (io["conv_state_sample"][L].rearrange("b t c -> (b t) c"), state_tok[2:, :])]
                    for dst, s in stores:
                        act.dma_start(dst, s).then_inc(outs.sem, 16)
                lane.link(act.activation(w_uv[:], w_ukv[:, :, P:256], ACT.Copy), w_uv_ok)
                lane.wait(z_dve, NIN)
                lane.wait(conv_ok, 1)
                for n in range(NBLK):
                    for m in (2 * n, 2 * n + 1):
                        lane.wait(qr_mm, m + 1)
                        lane.wait(roped, 4 + m)
                        rotate(psum[:, m % 2, 0:BLK], lambda r: r[:, 0:BLK], qr_rot)
                    for h in range(HEADS):
                        m = HEADS * n + h
                        lane.wait(qa_mm, m + 1)
                        lane.link(act.activation(qa[:, h, blk(n)], psum[:, 4 + m % 2, 0:BLK], ACT.Copy), qa_c)

                turns = [0]

                def cache_copy(gi, part):
                    g = GROUPS[gi]
                    turns[0] += 1
                    lane.wait(ct_T, turns[0])
                    if g["kind"] == "swa_s":
                        dst = skT_c
                    else:
                        dst = (ckvT_c, krT_c)[part][g["idx"] % 2]
                        if g["idx"] >= 2:
                            lane.wait(score, g["jobs"][0] - 1)
                        elif g["idx"] == 1:
                            lane.wait(pv, GROUPS[ST]["units"][-1] + 1)
                    lane.link(act.activation(dst[:], psum[:, 7, :], ACT.Copy), ct_c)

                def exps(j):
                    rows, nh, w, has_sink = job_shape(j)
                    s = slot_of(j)
                    scale = SWA_SCALE if has_sink else MLA_SCALE
                    lane.wait(negmax, j + 1)
                    if SLOT_FREE[j] is not None:
                        lane.wait(pt_T, SLOT_FREE[j] + 1)
                    for h in range(nh):
                        ins = act.activation(p_view(j)[:, h, :], s_view(j)[:, h, :], ACT.Exp, bias=nmax[0:rows, s, h:h + 1],
                                             scale=scale, accum_out=psum_p[0:rows, s, h:h + 1])
                        lane.link(ins, expd if h == nh - 1 and not has_sink else None)
                    if has_sink:
                        lane.link(act.activation(esink[:, s, 0:nh], esink[:, s, 0:nh], ACT.Exp), expd)

                def out(g):
                    lane.wait(pv, g["units"][-1] + 1)
                    if g["kind"] == "mla_p":
                        if g["idx"] >= 2:
                            lane.wait(uv_mm, g["idx"] - 1)
                        lane.link(act.activation(oL[:, g["idx"] % 2], psum[:, 6, :].rearrange("p (h t) -> p h t", h=HEADS),
                                                 ACT.Copy), ol_c)
                    else:
                        if g["idx"] == 0:
                            lane.wait(uv_mm, ST - 1)
                        b = g["idx"]
                        lane.link(act.activation(
                            oL[:, 0].rearrange("p (j a) t -> p a j t", a=2)[:, :, :, TS * b:TS * b + TS],
                            psum[:, 6, 0:64].rearrange("p (a j t) -> p a j t", a=2, j=2), ACT.Copy), ol_c)

                for what, i in STEPS:
                    if what == "exp":
                        exps(i)
                    elif what == "cache":
                        cache_copy(*i)
                    elif what == "copy" and i % 2 == 0:
                        lane.wait(pt_T, i + 1)
                        if i >= 3:
                            lane.wait(pv, i - 2)
                        w = 320 if UNIT_OF[i]["kind"] == "mla_s" else 512
                        lane.link(act.activation(pT[:, i % 3, 0:w], psum[:, 4, 0:w], ACT.Copy), pt_c[0])
                    elif what == "out" and GROUPS[i]["kind"][:3] == "mla":
                        out(GROUPS[i])

                lane.wait(uv_mm, TILES)
                lane.wait(outs, 16 * N_STORES)
                lane.wait(uv_ok, TILES)
                lane.wait(qrs_ok, 1)
                split_w(NIN)
                split_w(NIN + 1)
                for n in range(NBLK):
                    for half in range(2):
                        ks = slice(4 * half, 4 * half + 4)
                        lane.link(act.activation(h_hi[:, ks, blk(n)], mix[:, ks, blk(n)], ACT.Copy), hi_h)
                for c in range(NIN + 2, NCHUNK + 3):
                    if c < NCHUNK:
                        lane.wait(z_done, c - 1)
                        split_w(c)
                    k = c - 3 - NIN
                    if k >= 0:
                        if k == 0:
                            lane.wait(lo_h, 4 * NBLK)
                        lane.wait(z_dve, NIN + k + 1)
                        x_square(lane, k)
                assert last or lane.count[act_step.name] == ACT_STEPS

            with act.Fori(0, DEPTH - 1) as L:
                layer(L, False)
            layer(DEPTH - 1, True)

            act.wait_ge(sum_x.sem, sum_x.at(DEPTH, 0))
            for t in range(TILES):
                act.wait_ge(s_yT.sem, 2 * t + 1)
                act.activation(tok[:, t, 0:512], psum[:, 0, :], ACT.Copy).then_inc(s_ya.sem, 1)

        @block.vector
        def _(dve):
            dve.wait_ge(s_const.sem, 32)
            dve.tensor_copy(masks[:], masks_f[:]).then_inc(s_cst.sem, 1)
            dve.wait_ge(s_cst.sem, 4)
            dve.wait_ge(s_cs.sem, 1)
            dve.scalar_tensor_tensor(csil[:], csil[:], 1.0, crow[:], ALU.add, ALU.mult).then_inc(s_cs.sem, 1)
            dve.wait_ge(s_cs.sem, 2)
            dve.tensor_scalar(csil[:], csil[:], 0.5, None, ALU.mult).then_inc(s_cs.sem, 1)
            for t in range(TILES):
                dve.wait_ge(s_xT.sem, 2 * t + 2)
                dve.tensor_copy(x[:, 4:8, tile(t)], psum[:, (2 * t + 1) % 4, :].rearrange("p (k t) -> p k t", k=4))\
                    .then_inc(s_xv.sem, 1)
            dve.wait_ge(s_cT.sem, 1)
            dve.tensor_copy(cT[:], psum[:, 5, 0:P].rearrange("p (k c) -> p k c", k=KD)[:, :, 0:1 + NB])\
                .then_inc(s_cT.sem, 1)
            dve.tensor_copy(fing[:], psum[:, 5, 256:256 + KD]).then_inc(s_cT.sem, 1)
            dve.wait_ge(s_cT.sem, 3)
            dve.wait_ge(s_mod.sem, 1)
            dve.tensor_copy(mod[:, 0:2].rearrange("p a k c -> p (a k c)"), psum[:, 7, 0:16 * (1 + NB)])\
                .then_inc(s_modc.sem, 1)
            dve.wait_ge(s_modc.sem, 1)

            def x_mean(lane):
                lane.wait(sum_x, 1)
                lane.link(dve.tensor_scalar(mean[:], psum[:, 6, 0:TILES], 1.0 / D, EPS, ALU.mult, ALU.add), mean_x)

            def next_vectors(lane):
                lane.wait(small_T, 1)
                lane.link(dve.tensor_copy(vec[:], psum[:, 7, 0:V_ROWS]), small_v)
                lane.link(dve.tensor_copy(convc[:], psum[:, 7, 64:96].rearrange("p (j c) -> p j c", j=2)), small_v)
                lane.wait(vec_in, 16 * 7)
                lane.link(dve.tensor_scalar(nsink[:], sink[:], -1.0, None, ALU.mult))
                both = mod[:, 0:2].rearrange("p a k c -> p (a k) c")
                lane.link(dve.tensor_tensor(both, both, spread(vec[:, V_BMOD:V_BMOD + 16], 1 + NB), ALU.add))
                lane.link(dve.scalar_tensor_tensor(amul[:], mod[:, 1], 1.0, spread(vec[:, V_G:V_G + KD], 1 + NB),
                                                   ALU.add, ALU.mult), mod_v)

            def x_scale(lane, n, half):
                lane.wait(bc_x, n + 1)
                xb = x[:, 4 * half:4 * half + 4, blk(n)]
                lane.link(dve.tensor_tensor(xb, xb, psum[:, 6 + n % 2, 0:BLK].unsqueeze(1).broadcast_to([P, 4, BLK]),
                                            ALU.mult), scaled_x)

            before = Lane(dve, -1, dve_before)
            next_vectors(before)
            x_mean(before)
            dve.sem_inc(z_dve.sem, 1)

            def layer(L, last):
                lane = Lane(dve, L, dve_step)
                tt = lambda *a, sig=None: lane.link(dve.tensor_tensor(*a), sig)
                stt = lambda *a, sig=None: lane.link(dve.scalar_tensor_tensor(*a), sig)
                ts = lambda *a, sig=None: lane.link(dve.tensor_scalar(*a), sig)
                cp = lambda *a, sig=None: lane.link(dve.tensor_copy(*a), sig)

                def split_w(c):
                    _, src, view = w_views(c, last)
                    lane.wait(hi_w, c + 1)
                    if c >= 2:
                        lane.wait(z_done, c - 1)
                    tt(view(w_lo[c % 2]), src, view(w_hi[c % 2]).bitcast(F32), ALU.subtract, sig=lo_w)

                def rope(out, z, c_, s_, r, sig):
                    tt(out, z, c_, ALU.mult)
                    tt(r, r, s_, ALU.mult)
                    tt(out, out, r, ALU.add, sig=sig)

                def per_sample(ap):
                    return ap[:, SEQ:NTOK].rearrange("p (b t) -> p b t", t=TS)

                split_w(0)
                split_w(1)
                lane.wait(x_out, 0)
                xs = x[:, :, SEQ:NTOK].rearrange("p k (b t) -> p k b t", t=TS)

                def each(ap):
                    return ap.unsqueeze(3).broadcast_to([P, KD, NB, TS])

                def lo(n, half, src, base=0):
                    ks = slice(4 * half, 4 * half + 4)
                    lane.wait(hi_h, base + 2 * n + half + 1)
                    tt(h_lo[:, ks, blk(n)], src[:, ks, blk(n)], h_hi[:, ks, blk(n)].bitcast(F32), ALU.subtract, sig=lo_h)

                for n in range(NBLK):
                    for half in range(2):
                        x_scale(lane, n, half)
                        if n:
                            lo(n - 1, half, x)
                tt(xs, xs, each(amul[:, :, 1:]), ALU.mult)
                tt(xs, xs, each(mod[:, 0, :, 1:]), ALU.add, sig=h_smp)
                for half in range(2):
                    lo(NBLK - 1, half, x)
                for c in range(NIN):
                    if c + 2 < NIN:
                        split_w(c + 2)
                    pair, j = divmod(c, 2)
                    z = zset(c)
                    lane.wait(z_done, c + 1)
                    if c in ACT_CHUNKS:
                        lane.wait(z_act, ACT_CHUNKS.index(c) + 1)
                    if pair == KV_KR and j == 0:
                        ts(b3(ckvT[:]), z, vec[:, V_KVG:V_KVG + 1], None, ALU.mult, sig=z_dve)
                    elif pair == Q_LAT:
                        ts(b3(cq[:, j, :]), z, vec[:, V_QG + j:V_QG + j + 1], None, ALU.mult, sig=z_dve)
                    elif pair == SK_SV and j == 1:
                        cp(b3(svT[:]), z, sig=z_dve)
                    elif pair in (KV_KR, SK_SV, S_Q):
                        lane.wait(tab_in, 0 if pair == KV_KR else 16)
                        out = {KV_KR: krT[:], SK_SV: skT[:], S_Q: sqT[:, j, :]}[pair]
                        tt(b3(out), z, b3(tab[:, 0, :]), ALU.mult, sig=z_dve)
                        tt(rot[:], rot[:], tab[:, 1, :], ALU.mult)
                        tt(out, out, rot[:], ALU.add, sig=roped)
                    elif pair in (S_G, M_G0, M_G1):
                        k = {S_G: 6, M_G0: 2, M_G1: 4}[pair] + j
                        stt(b3(mix[:, k, :]), b3(mix[:, k, :]), 1.0, z, ALU.add, ALU.mult, sig=z_dve)
                    elif pair == CV_H:
                        lane.wait(lat_sum, 1)
                        cp(b3(mix[:, j, :]), z, sig=z_dve)
                    elif pair == CV_C:
                        up, us = u[:, j, 0:2 + SEQ], u[:, j, 2 + SEQ:].rearrange("p (b t) -> p b t", t=TS + 2)
                        y = mix[:, j, :]
                        if j == 0:
                            lane.wait(svt_T, 3)
                        lane.link(dve.memset(up[:, 0:2], 0.0))
                        cp(us[:, :, 0:2], convc[:, j, :].rearrange("p (b t) -> p b t", t=2))
                        tt(up[:, 2:2 + 2 * BLK].rearrange("p (n t) -> p n t", t=BLK), z[:, 0:2, :],
                           y[:, 0:2 * BLK].rearrange("p (n t) -> p n t", t=BLK), ALU.mult)
                        tt(up[:, 2 + 2 * BLK:2 + SEQ], z[:, 2, 0:SEQ - 2 * BLK], y[:, 2 * BLK:SEQ], ALU.mult)
                        tt(us[:, :, 2:], z[:, 2, SEQ - 2 * BLK:].rearrange("p (b t) -> p b t", t=TS), per_sample(y),
                           ALU.mult, sig=z_dve)
                        for i in range(3):
                            w = vec[:, V_CONV + 2 * i + j:V_CONV + 2 * i + j + 1]
                            for out, in_ in ((y[:, 0:SEQ], up[:, i:i + SEQ]), (per_sample(y), us[:, :, i:i + TS])):
                                if i == 0:
                                    ts(out, in_, w, None, ALU.mult)
                                else:
                                    stt(out, in_, w, out, ALU.mult, ALU.add)
                        cp(state[:, j, 0:2], up[:, SEQ:SEQ + 2])
                        cp(state[:, j, 2:].rearrange("p (b t) -> p b t", t=2), us[:, :, TS:TS + 2])
                    elif pair == CV_B:
                        tt(b3(mix[:, j, :]), z, b3(mix[:, j, :]), ALU.mult, sig=z_dve)
                    else:
                        r = (rot, svT)[j]
                        stt(b3(r[:]), b3(r[:]), 1.0, z, ALU.add, ALU.mult, sig=z_dve)
                        stt(mix[:, j, :], r[:], 0.5, mix[:, j, :], ALU.mult, ALU.mult, sig=conv_ok if j else None)
                    if c == 2 * SPLIT_AFTER - 1:
                        lane.wait(lat_sum, 1)
                        for i, width in enumerate((128, 256)):
                            ts(meanl[:, i, :], psum[:, 6, 16 * i:16 * i + TILES], 1.0 / width, EPS, ALU.mult, ALU.add,
                               sig=lat_mean)
                    if c == 2 * SPLIT_AFTER + 1:
                        for i in range(2):
                            for n in range(NBLK):
                                m = NBLK * i + n
                                lane.wait(lat_bc, m + 1)
                                r = psum[:, 6 + m % 2, 0:BLK]
                                if i == 0:
                                    tt(ckvT[:, blk(n)], ckvT[:, blk(n)], r, ALU.mult, sig=lat_ok)
                                else:
                                    tt(cq[:, :, blk(n)], cq[:, :, blk(n)], r.unsqueeze(1).broadcast_to([P, 2, BLK]),
                                       ALU.mult, sig=lat_ok)

                lane.wait(tab_in, 32)
                lane.wait(z_done, NIN)
                for k in range(2):
                    lane.wait(mq_mm, k + 1)
                    cp(mq[:, k], psum[:, 6 + k, :].rearrange("p (h c) -> p h c", h=HEADS), sig=mq_c)
                for m in range(2 * NBLK):
                    n, j = divmod(m, 2)
                    lane.wait(qr_rot, m + 1)
                    rope(qr[:, j, blk(n)], psum[:, m % 2, 0:BLK], tab[:, 0, blk(n)], tab[:, 1, blk(n)], rot[:, 0:BLK],
                         roped)
                for a, half in enumerate(HALVES):
                    ins = dve.tensor_copy(
                        qrs[half, :, 32 * a:32 * a + 32].rearrange("p b (j t) -> p b j t", j=2),
                        qr[half, :, SEQ:NTOK].rearrange("p j (b t) -> p b j t", t=TS))
                    lane.link(ins, qrs_ok if a else None)
                lane.wait(qa_c, HEADS * NBLK)
                for a in range(2):
                    cp(qas[:, :, 32 * a:32 * a + 32].rearrange("p b (j t) -> p b j t", j=2),
                       qa[:].rearrange("p (j a) t -> p a j t", a=2)[:, a, :, SEQ:NTOK]
                       .rearrange("p j (b t) -> p b j t", t=TS), sig=qas_ok)

                def maxima(j):
                    rows, nh, w, has_sink = job_shape(j)
                    s = slot_of(j)
                    lane.wait(score, j + 1)
                    lane.link(dve.tensor_reduce(smax[0:rows, s, 0:nh], s_view(j), AX.X, ALU.max))
                    if not has_sink:
                        ts(nmax[0:rows, s, 0:nh], smax[0:rows, s, 0:nh], -MLA_SCALE, None, ALU.mult, sig=negmax)
                        return
                    h0 = GROUP_OF[j]["jobs"].index(j)
                    stt(nmax[:, s, 0:nh], smax[:, s, 0:nh], -SWA_SCALE, nsink[:, h0:h0 + nh], ALU.mult, ALU.min)
                    tt(esink[:, s, 0:nh], nmax[:, s, 0:nh], sink[:, h0:h0 + nh], ALU.add, sig=negmax)

                def normalise(j):
                    rows, nh, w, has_sink = job_shape(j)
                    s = slot_of(j)
                    lane.wait(expd, j + 1)
                    total = psum_p[0:rows, s, 0:nh]
                    if has_sink:
                        tt(total, total, esink[:, s, 0:nh], ALU.add)
                    lane.link(dve.reciprocal(rinv[0:rows, s, 0:nh], total))
                    if nh == 1:
                        ts(p_view(j)[:, 0, :], p_view(j)[:, 0, :], rinv[0:rows, s, 0:1], None, ALU.mult, sig=p_ok)
                    else:
                        tt(p_view(j), p_view(j), spread(rinv[:, s, :], w), ALU.mult, sig=p_ok)

                def gate_mla(t):
                    g = mix[:, 2:6, tile(t)]
                    stt(g, psum[:, 7, :].rearrange("p (h t) -> p h t", h=HEADS), 0.5, g, ALU.mult, ALU.mult, sig=uv_ok)

                def gate_swa(g):
                    lane.wait(pv, g["units"][-1] + 1)
                    for kv, half in enumerate(HALVES):
                        out = mix[half, 6:8, tile(g["idx"])]
                        in_ = psum[half, 6, 256 * kv:256 * kv + 256].rearrange("p (g t) -> p g t", g=2)
                        stt(out, in_, 0.5, out, ALU.mult, ALU.mult, sig=swa_ok if kv else None)

                n_uv = 0
                for what, i in STEPS:
                    if what == "maxima":
                        maxima(i)
                    elif what == "norm":
                        normalise(i)
                    elif what == "copy" and i % 2 == 1:
                        lane.wait(pt_T, i + 1)
                        if i >= 3:
                            lane.wait(pv, i - 2)
                        w = 320 if UNIT_OF[i]["kind"] == "mla_s" else 512
                        cp(pT[:, i % 3, 0:w], psum[:, 5, 0:w], sig=pt_c[1])
                    elif what == "out" and GROUPS[i]["kind"][:3] == "swa":
                        gate_swa(GROUPS[i])
                    elif what == "up":
                        n_uv += 1
                        lane.wait(uv_mm, n_uv)
                        gate_mla(n_uv - 1)
                    elif what == "mod":
                        sums = psum[:, 7, 0:2 * (1 + NB)].rearrange("p (k c) -> p k c", k=2)
                        if i in GATE_AT:
                            m = GATE_AT[i]
                            lane.wait(gate_mm, m + 1)
                            tt(mod[:, 2, 2 * m:2 * m + 2], sums,
                               spread(vec[:, V_BMOD + 16 + 2 * m:V_BMOD + 18 + 2 * m], 1 + NB), ALU.add, sig=gate_c)
                        elif not last:
                            m = NEXT_AT[i]
                            lane.wait(next_mm, m + 1)
                            cp(mod[:, m // 4, 2 * (m % 4):2 * (m % 4) + 2], sums, sig=next_c)

                split_w(NIN)
                split_w(NIN + 1)
                for n in range(NBLK):
                    for half in range(2):
                        lo(n, half, mix, 2 * NBLK)
                for c in range(NIN, NCHUNK):
                    if c + 2 < NCHUNK:
                        split_w(c + 2)
                    k, z = c - NIN, zset(c)
                    lane.wait(z_done, c + 1)
                    if k % 4 == 0:
                        lane.wait(x_in[k // 4], 16)
                    gate = mod[:, 2, k, 0:1]
                    xk = x[:, k, :]
                    two = xk[:, 0:2 * BLK].rearrange("p (n t) -> p n t", t=BLK)
                    stt(two, z[:, 0:2, :], gate, two, ALU.mult, ALU.add)
                    stt(xk[:, 2 * BLK:SEQ], z[:, 2, 0:SEQ - 2 * BLK], gate, xk[:, 2 * BLK:SEQ], ALU.mult, ALU.add)
                    tmp = rot[:, 0:P].rearrange("p (b t) -> p b t", t=TS)
                    tt(tmp, z[:, 2, SEQ - 2 * BLK:].rearrange("p (b t) -> p b t", t=TS), spread(mod[:, 2, k, 1:], TS),
                       ALU.mult)
                    tt(per_sample(xk), per_sample(xk), tmp, ALU.add, sig=z_dve)
                    if c == NCHUNK - 2 and not last:
                        next_vectors(lane)
                x_mean(lane)
                assert last or lane.count[dve_step.name] == DVE_STEPS

            with dve.Fori(0, DEPTH - 1) as L:
                layer(L, False)
            layer(DEPTH - 1, True)

            end = Lane(dve, DEPTH)
            for n in range(NBLK):
                for half in range(2):
                    x_scale(end, n, half)
                dve.tensor_tensor(x[:, :, blk(n)], x[:, :, blk(n)], spread(fing[:], BLK), ALU.mult).then_inc(s_y.sem, 1)
            dve.wait_ge(sum_x.sem, sum_x.at(DEPTH, 0))
            for t in range(TILES):
                dve.wait_ge(s_yT.sem, 2 * t + 2)
                dve.tensor_copy(tok[:, t, 512:1024], psum[:, 2, :]).then_inc(s_yv.sem, 1)


_OUTS = [("y_prompt", (1, 1024, 1024)), ("y_sample", (8, 16, 1024)),
         ("conv_state_prompt", (2, 1, 2, 256)), ("conv_state_sample", (2, 8, 2, 256)),
         ("mla_ckv_prompt", (2, 1, 1024, 128)), ("mla_ckv_sample", (2, 8, 16, 128)),
         ("mla_krope_prompt", (2, 1, 1024, 64)), ("mla_krope_sample", (2, 8, 16, 64)),
         ("swa_k_prompt", (2, 1, 64, 2, 64)), ("swa_k_sample", (2, 8, 16, 2, 64)),
         ("swa_v_prompt", (2, 1, 64, 2, 64)), ("swa_v_sample", (2, 8, 16, 2, 64))]
_INS = ["x_prompt", "x_sample", "c_prompt", "c_sample", "cache_conv", "cache_mla_ckv", "cache_mla_krope",
        "cache_swa_k", "cache_swa_v", "norm_g", "w_mod", "b_mod", "w_in", "conv_w", "q_norm_g", "kv_norm_g",
        "w_uq", "w_ukv", "swa_sink", "w_out", "final_norm_g"]


def constants():
    masks = np.zeros((8, 1664), np.float32)
    for b in range(8):
        masks[b, 16 * b:16 * b + 16] = 1
        masks[b, 1152 + 64 * b:1152 + 64 * b + 64] = 1
        own = np.zeros(640, bool)
        own[64 * b:64 * b + 64] = True
        own[512 + 16 * b:512 + 16 * b + 16] = True
        masks[b, 128:768] = np.where(own, 0, NEG)
    masks[0, 768:832] = 1
    masks[1, 832:896] = 1
    masks[0, 896:896 + 64] = NEG
    masks[0, 896 + 192:1152] = NEG
    masks[1, 896:896 + 128] = NEG
    pos = np.concatenate([np.arange(1024), np.tile(512 + np.arange(16), 8)]).astype(np.float32)
    rope = np.zeros((2, 128, 2, 1152), np.float32)
    for i, theta in enumerate((10000.0, 150000.0)):
        inv = np.float32(theta) ** (-np.arange(32, dtype=np.float32) / np.float32(32))
        ang = (pos[None, :] * inv[:, None]).astype(np.float32)
        cos, sin = np.cos(ang), np.sin(ang)
        rope[i, :, 0] = np.tile(cos, (4, 1))
        rope[i, :, 1] = np.concatenate([-sin, sin, -sin, sin])
    return {"c_ident": np.eye(128, dtype=np.float32), "c_masks": masks,
            "c_rope": rope}


def kernel(**inputs):
    import concourse.bacc as bacc
    from concourse.bass_utils import run_bass_kernel_spmd

    nc = bacc.Bacc("TRN2", target_bir_lowering=False, num_devices=1)
    arrays, io = {}, {}
    named = {n: np.ascontiguousarray(inputs[n]) for n in _INS}
    named.update(constants())
    for name, a in named.items():
        arrays[f"in_{name}"] = a
        io[name] = nc.dram_tensor(f"in_{name}", a.shape, mybir.dt.from_np(a.dtype), kind="ExternalInput").ap()
    for name, shape in _OUTS:
        io[name] = nc.dram_tensor(f"out_{name}", shape, F32, kind="ExternalOutput").ap()
    build(nc, io)
    r = run_bass_kernel_spmd(nc, [arrays], core_ids=[0])
    return tuple(r.results[0][f"out_{name}"] for name, _ in _OUTS)
```

```python
import numpy as np
import concourse.bass as bass
from concourse import mybir

F32 = mybir.dt.float32
F32R = mybir.dt.float32r
BF16 = mybir.dt.bfloat16
ACT = mybir.ActivationFunctionType
ALU = mybir.AluOpType
AX = mybir.AxisListType

P = 128
D = 1024
KD = D // P
DEPTH = 2
SEQ, NB, TS = 1024, 8, 16
NTOK = SEQ + NB * TS
TILES = NTOK // P
ST = TILES - 1
PAST = 512
BLK = 384
NBLK = NTOK // BLK
D_IN = 2752
EPS = 1e-6
NEG = -1e30
HEADS = 4
MLA_SCALE = (128 + 64) ** -0.5
SWA_SCALE = 64 ** -0.5
CH = 64
CONVW = 256

KV_KR, Q_LAT, SK_SV, S_Q, S_G, M_G0, M_G1, CV_H, CV_C, CV_B, CV_G = range(11)
PAIRS = [(1280, 192), (1024, 256), (2240, 256), (1984, 256), (2496, 256), (1472, 256), (1728, 256),
         (0, 256), (512, 256), (256, 256), (768, 256)]
NIN, NOUT = 2 * len(PAIRS), KD
NCHUNK = NIN + NOUT
ACT_CHUNKS = [c for c in range(NIN) if c // 2 in (KV_KR, Q_LAT, S_Q, S_G, M_G0, M_G1, CV_G) or c == 2 * SK_SV]
SPLIT_AFTER = S_G + 1

N_SHIFT_SCALE, N_GATE = 8, 4


def plan_loads(last):
    loads = [("in", i) for i in range(2, len(PAIRS))] + [("uq", 0), ("ukv", 0)]
    loads += [("gate", i) for i in range(N_GATE)]
    loads += [] if last else [("next", i) for i in range(N_SHIFT_SCALE)]
    slots = [n % 2 for n in range(len(loads))]
    outs = [("out", i) for i in range(NOUT // 2)]
    slots += [(len(loads) + n) % 2 for n in range(len(outs))]
    loads += outs
    if not last:
        loads += [("after", 0), ("after", 1)]
        slots += [0, 1]
    landed, plan = [0, 0], {}
    for x, slot in zip(loads, slots):
        landed[slot] += 16 * {"out": 3, "uq": 4}.get(x[0], 2 if x in (("in", CV_H), ("next", 0)) else 1)
        plan[x] = (slot, landed[slot])
    plan[("in", 0)], plan[("in", 1)] = (0, 0), (1, 0)
    return loads, plan, landed


V_G, V_BMOD, V_QG, V_KVG, V_CONV, V_ROWS = 0, 8, 32, 34, 35, 41

SLOTS = 8
SPLIT_FROM = 3
CACHE_SLOTS = 5


def plan_attention():
    groups, job, unit = [], 0, 0

    def add(kind, idx, jobs, keys):
        nonlocal job, unit
        units = 1 if kind == "mla_s" else len(keys)
        groups.append(dict(kind=kind, idx=idx, jobs=list(range(job, job + jobs)), keys=keys,
                           units=list(range(unit, unit + units))))
        job += jobs
        unit += units

    for t in range(ST):
        add("swa_p", t, 1, [t - 1, t] if t else [t])
    add("swa_s", ST, HEADS, list(range(5)))
    for t in range(ST):
        add("mla_p", t, HEADS, list(range(t + 1)))
    for b in range(NB):
        add("mla_s", b, 1, list(range(5)))
    return groups, job, unit


GROUPS, NJOBS, NUNITS = plan_attention()
GROUP_OF = {j: g for g in GROUPS for j in g["jobs"]}
UNIT_OF = {n: g for g in GROUPS for n in g["units"]}
COPIER = [0 if UNIT_OF[n]["kind"][:3] == "swa" else n % 2 for n in range(NUNITS)]
COPIES = [COPIER[:n + 1].count(COPIER[n]) for n in range(NUNITS)]
LAST = len(GROUPS) - 1
N_SWA = sum(g["kind"][:3] == "swa" for g in GROUPS)
N_MLA = len(GROUPS) - N_SWA

GATE_AT = dict(zip((1, 3, 5, 7), range(N_GATE)))
NEXT_AT = dict(zip((10, 13, 15, 17, 18, 19, 20, 21), range(N_SHIFT_SCALE)))
FIRST_S = [g["kind"] for g in GROUPS].index("mla_s")


def slot_of(j):
    g = GROUP_OF[j]
    i = g["jobs"].index(j)
    if g["kind"] == "swa_p":
        return j % 4
    if g["kind"] == "swa_s":
        return (4, 5, 0, 1)[i]
    if g["kind"] == "mla_p":
        return ((2, 3, 6, 7), (4, 5, 0, 1))[g["idx"] % 2][i]
    return 2 + g["idx"] % 2


SLOT_FREE = {}
for _j in range(NJOBS):
    _same = [i for i in range(_j) if slot_of(i) == slot_of(_j)]
    SLOT_FREE[_j] = GROUP_OF[_same[-1]]["units"][-1] if _same else None


def plan_steps():
    steps, done = [], {"exp": -1, "norm": -1, "turn": -1, "scores": -1}

    def put(what, i):
        steps.append((what, i))
        if what in done:
            done[what] = i

    def exps(upto):
        while done["exp"] < min(upto, done["scores"]):
            j = done["exp"] + 1
            if SLOT_FREE[j] is not None and SLOT_FREE[j] > done["turn"]:
                return
            put("exp", j)

    def norms(upto):
        while done["norm"] < min(upto, done["exp"]):
            put("norm", done["norm"] + 1)

    def scores():
        g = GROUP_OF[done["scores"] + 1]
        if g["kind"] == "mla_p" and g["idx"] >= SPLIT_FROM and g["jobs"][0] == done["scores"] + 1:
            put("stack_q", g["idx"])
        put("scores", done["scores"] + 1)
        put("maxima", done["scores"])

    scores()
    scores()
    exps(1)
    norms(0)
    for gi, g in enumerate(GROUPS):
        ahead = GROUPS[gi + 1]["jobs"][-1] + 1 if gi < LAST else NJOBS - 1
        js = list(range(done["scores"] + 1, min(ahead, NJOBS - 1) + 1))
        units = g["units"]
        at = [len(units) * i // len(js) for i in range(len(js))]
        cached = gi + 3 if gi + 3 <= LAST and GROUPS[min(gi + 3, LAST)]["kind"] in ("swa_s", "mla_s") else None
        if cached:
            put("cache", (cached, 0))
        if gi == 1:
            put("split_keys", 0)
        if SPLIT_FROM <= gi - ST + 1 < ST:
            put("split_q", gi - ST + 1)
        for q, n in enumerate(units):
            if q == 0:
                for _ in range(at.count(0)):
                    exps(done["scores"] - 1)
                    scores()
                if cached and GROUPS[cached]["kind"] == "mla_s":
                    put("cache", (cached, 1))
                put("turn", n)
                put("copy", n)
                if gi and GROUPS[gi - 1]["kind"] == "mla_p":
                    put("up", gi - 1)
                if gi in GATE_AT or gi in NEXT_AT:
                    put("mod", gi)
            else:
                for _ in range(at.count(q)):
                    if done["exp"] < done["scores"] - 1:
                        exps(done["scores"] - 1)
                    if done["exp"] >= done["scores"] - 1:
                        scores()
            if q + 1 < len(units):
                put("turn", n + 1)
                put("copy", n + 1)
            put("weigh", n)
            if n == units[-1]:
                put("out", gi)
                if gi in GATE_AT or gi in NEXT_AT:
                    put("modT", gi)
            before = done["exp"]
            exps(done["scores"])
            norms(before)
        while js and done["scores"] < js[-1]:
            exps(done["scores"] - 1)
            scores()
        if gi < LAST:
            exps(GROUPS[gi + 1]["jobs"][-1])
            norms(GROUPS[gi + 1]["jobs"][-1])
        if gi == LAST - 1:
            put("split", NIN)
            put("split", NIN + 1)
    put("up", LAST)
    return steps


STEPS = plan_steps()
N_STORES = 10
DVE_STEPS, ACT_STEPS = 216, 107


class Signal:

    def __init__(self, nc, name, per, first=0):
        self.sem, self.per, self.name, self.first = nc.alloc_semaphore(name), per, name, first

    def at(self, layer, k):
        return layer * self.per + k + self.first


class Lane:

    def __init__(self, eng, layer, own=None):
        self.eng, self.layer, self.own, self.count = eng, layer, own, {}

    def link(self, ins, sig=None):
        sig = sig or self.own
        ins.then_inc(sig.sem, 1)
        self.count[sig.name] = self.count.get(sig.name, 0) + 1
        self.eng.wait_ge(sig.sem, sig.at(self.layer, self.count[sig.name]))


def build(nc, io):
    H_AT, X_AT, G_AT, RAW_AT, SPL_AT, TAB_AT, ZT_AT, SM_AT = (
        0, 73728, 115200, 152064, 168448, 184832, 194048, 203424)

    base = -(-nc.sbuf_base // 32) * 32

    def at(name, off, shape, dt=F32):
        return nc.alloc_sbuf_tensor_at(name, shape, dt, offset=base + off)

    h_hi = at("h_hi", H_AT, [P, KD, NTOK], F32R)
    h_lo = at("h_lo", H_AT + 36864, [P, KD, NTOK], F32R)
    x = at("x", X_AT, [P, KD, NTOK])
    vrows = at("vrows", X_AT + 36864, [V_ROWS, P])
    ccrow = at("ccrow", X_AT + 37376, [2 * NB, CONVW])
    cq = at("cq", X_AT, [P, 2, NTOK])
    ckvT = at("ckvT", X_AT + 9216, [P, NTOK])
    ckv = at("ckv", X_AT + 13824, [P, TILES, P])
    krT = at("krT", X_AT + 18432, [P, NTOK])
    sqT = at("sqT", X_AT + 23040, [P, 2, NTOK])
    skT = at("skT", X_AT + 32256, [P, NTOK])
    sv = at("sv", X_AT + 36864, [P, TILES, P])
    cache_at = [X_AT, X_AT + 4096, X_AT + 32256, X_AT + 23040, X_AT + 27136]
    raw_ckv = [at(f"raw_ckv{i}", a, [P, 4, P]) for i, a in enumerate(cache_at)]
    raw_kr = [at(f"raw_kr{i}", a + 2048, [P, 4, P]) for i, a in enumerate(cache_at)]
    mix = at("mix", G_AT, [P, KD, NTOK])
    tok = at("tok", G_AT, [P, TILES, D])
    raw = at("raw", RAW_AT, [P, 2, KD, 256])
    w_hi = [at(f"w_hi{s}", SPL_AT + 8192 * s, [P, KD, P], F32R) for s in range(2)]
    w_lo = [at(f"w_lo{s}", SPL_AT + 8192 * s + 4096, [P, KD, P], F32R) for s in range(2)]
    w_uq = at("w_uq", RAW_AT + 8192, [P, 2, 768])
    modrow0 = at("modrow0", H_AT + 65536, [1 + NB, 2 * D])
    modrow = at("modrow", H_AT + 72704, [1 + NB, 256])
    w_uv = at("w_uv", ZT_AT + 4608, [P, HEADS, P])
    w_ukT = at("w_ukT", SPL_AT + 6144, [P, HEADS, P])
    w_ukv = at("w_ukv", RAW_AT, [P, HEADS, 256])
    kr_tok = at("kr_tok", SPL_AT + 12288, [P, TILES, 64])
    sk_tok = at("sk_tok", SPL_AT + 14592, [P, 2, P])
    crow = at("crow", SPL_AT, [1 + NB, D])
    frow = at("frow", SPL_AT + 8192, [KD, P])
    csil = at("csil", SPL_AT + 4096, [1 + NB, D])
    tab = at("tab", TAB_AT, [P, 2, NTOK])
    qas = at("qas", ZT_AT + 2048, [P, NB, 64])
    rot = at("rot", ZT_AT, [P, NTOK])
    svT = at("svT", ZT_AT + 4608, [P, NTOK])
    UW = 2 + SEQ + NB * (TS + 2)
    u = at("u", ZT_AT, [P, 2, UW])
    w_uqT = at("w_uqT", SPL_AT + 2048, [P, HEADS, 2 * P])
    mq = at("mq", SPL_AT + 8192, [P, 2, HEADS, P])
    probs_lo = at("probs_lo", H_AT, [P, 6, 1024])
    probs_hi = at("probs_hi", X_AT + 23040, [P, 2, 1024])
    qa = at("qa", H_AT + 24576, [P, HEADS, NTOK])
    qr = at("qr", H_AT + 43008, [P, 2, NTOK])
    pT = at("pT", H_AT + 52224, [P, 3, 512])
    oL = at("oL", H_AT + 58368, [P, 2, HEADS, P])
    ckvT_c = [at("ckvT_c0", H_AT + 62464, [P, 512]), at("ckvT_c1", H_AT + 66560, [P, 512])]
    krT_c = [at("krT_c0", H_AT + 64512, [P, 512]), at("krT_c1", H_AT + 68608, [P, 512])]
    sk_c = at("sk_c", H_AT + 66560, [P, 4, P])
    sv_c = at("sv_c", H_AT + 68608, [P, 4, P])
    skT_c = at("skT_c", H_AT + 70656, [P, 512])

    small = [SM_AT]

    def sm(name, shape, dt=F32):
        size = int(np.prod(shape[1:])) * (2 if dt == BF16 else 4)
        t = at(name, small[0], shape, dt)
        small[0] += -(-size // 32) * 32
        return t

    ident = sm("ident", [P, P])
    ones = sm("ones", [P, 1])
    mhalf = sm("mhalf", [P, TILES])
    vec = sm("vec", [P, V_ROWS])
    convc = sm("convc", [P, 2, 2 * NB])
    mod = sm("mod", [P, 3, KD, 1 + NB])
    amul = sm("amul", [P, KD, 1 + NB])
    cT = sm("cT", [P, KD, 1 + NB])
    fing = sm("fing", [P, KD])
    sink = sm("sink", [P, HEADS])
    nsink = sm("nsink", [P, HEADS])
    state = sm("state", [P, 2, 2 + 2 * NB])
    masks = sm("masks", [8, 128 + 640 + 128 + 256 + 512], BF16)
    mean = sm("mean", [P, TILES])
    rstd = sm("rstd", [P, TILES])
    meanl = sm("meanl", [P, 2, TILES])
    rstdl = sm("rstdl", [P, 2, TILES])
    qrs = sm("qrs", [P, NB, 64])
    state_tok = at("state_tok", H_AT + 72704, [2 + 2 * NB, CONVW])
    smax = sm("smax", [P, SLOTS, HEADS])
    nmax = sm("nmax", [P, SLOTS, HEADS])
    esink = sm("esink", [P, SLOTS, HEADS])
    psum_p = sm("psum_p", [P, SLOTS, HEADS])
    rinv = sm("rinv", [P, SLOTS, HEADS])
    assert base + small[0] <= nc.sbuf_usable_end, small[0]
    ckv_hi = at("ckv_hi", TAB_AT, [P, NTOK], F32R)
    ckv_lo = at("ckv_lo", TAB_AT + 4608, [P, NTOK], F32R)
    kr_hi = at("kr_hi", SPL_AT, [P, NTOK], F32R)
    kr_lo = at("kr_lo", SPL_AT + 4608, [P, NTOK], F32R)
    qa_hi = [at(f"qa_hi{i}", a, [P, HEADS, P], F32R) for i, a in enumerate((ZT_AT, X_AT + 36864))]
    qa_lo = [at(f"qa_lo{i}", a, [P, HEADS, P], F32R) for i, a in enumerate((ZT_AT + 6656, X_AT + 38912))]
    qst = [at(f"qst{i}", a, [P, 2, 2, P], F32R) for i, a in enumerate((SPL_AT + 9216, H_AT + 70656))]
    qr_lo = at("qr_lo", SPL_AT + 11264, [P, 2, P], F32R)
    masks_f = at("masks_f", ZT_AT, [8, masks.shape[1]])
    own64 = masks[:, 1152:1664]
    own8, block_mask, half_rows, band_mask = (masks[:, 0:128], masks[:, 128:768], masks[:, 768:896],
                                              masks[:, 896:1152])

    psum = nc.alloc_psum_tensor("psum", [P, 8, 512], F32)
    modw = at("modw", H_AT, [P, KD, 2 * D])
    xT = nc.dram_tensor("xT_scratch", (P, KD, NTOK), F32).ap()

    def sg(name, per=0, first=0):
        return Signal(nc, name, per, first)

    plans = {last: plan_loads(last) for last in (False, True)}
    w_in = [sg(f"weights_landed{s}", plans[False][2][s], 16) for s in range(2)]
    vec_in = sg("vectors_landed", 16 * 7, 16 * 7)
    tab_in = sg("rope_table_landed", 16 * 3, 16)
    swc_in = sg("swa_cache_landed", 32)
    mlc_in = [sg(f"mla_cache_landed{s}", 48 * len(range(s, NB, CACHE_SLOTS))) for s in range(CACHE_SLOTS)]
    x_in = [sg(f"residual_landed{s}", 16) for s in range(2)]
    x_out = sg("residual_stored", 16 * KD, 16)
    outs = sg("states_stored", 16 * N_STORES)
    small_T = sg("vectors_turned", 1, 1)
    small_v = sg("vectors_ready", 2, 2)
    sq_x = sg("x_squared", KD, KD)
    acc_x = sg("x_squares_added", KD - 2, KD - 2)
    lat_acc = sg("latent_squares_added", 1)
    sum_x = sg("x_summed", 1, 1)
    mean_x = sg("x_mean_ready", 1, 1)
    rstd_x = sg("x_rstd_ready", 1, 1)
    bc_x = sg("x_rstd_spread", NBLK)
    scaled_x = sg("x_scaled", 2 * NBLK)
    gate_mm = sg("gate_summed", N_GATE)
    row_c = sg("modulation_row_copied", N_GATE + N_SHIFT_SCALE)
    row_T = sg("modulation_row_turned", N_GATE + N_SHIFT_SCALE)
    gate_c = sg("gate_copied", N_GATE)
    next_mm = sg("next_modulation_summed", N_SHIFT_SCALE)
    next_c = sg("next_modulation_copied", N_SHIFT_SCALE)
    mod_v = sg("modulation_ready", 1, 1)
    h_smp = sg("h_sample_modulated", 1)
    hi_h = sg("h_hi_ready", 4 * NBLK)
    lo_h = sg("h_lo_ready", 4 * NBLK)
    hi_w = sg("w_hi_ready", NCHUNK)
    lo_w = sg("w_lo_ready", NCHUNK)
    z_done = sg("chunk_summed", NCHUNK, 1)
    z_act = sg("chunk_read_by_scalar", len(ACT_CHUNKS))
    z_dve = sg("chunk_read_by_vector", NCHUNK, 1)
    roped = sg("rope_done", 4 + 2 * NBLK)
    lat_sum = sg("latents_summed", 1)
    lat_mean = sg("latent_means_ready", 2)
    lat_rstd = sg("latent_rstds_ready", 2)
    lat_bc = sg("latent_rstds_spread", 2 * NBLK)
    lat_ok = sg("latents_normed", 2 * NBLK)
    svt_T = sg("swa_values_turned", 3)
    svt_c = sg("swa_values_copied", 3)
    w_uv_ok = sg("w_uv_ready", 1)
    turn_T = sg("states_turned", 9)
    turn_c = sg("states_copied", 9)
    qr_mm = sg("q_rope_summed", 2 * NBLK)
    qr_rot = sg("q_rope_rotated", 2 * NBLK)
    key_hi = sg("keys_hi_ready", 2)
    key_lo = sg("keys_lo_ready", 2)
    q_hi = sg("queries_hi_ready", ST - SPLIT_FROM)
    q_lo = sg("queries_lo_ready", ST - SPLIT_FROM)
    q_st = sg("queries_stacked", ST - SPLIT_FROM)
    mq_mm = sg("q_weights_summed", 2)
    mq_c = sg("q_weights_copied", 2)
    qa_mm = sg("q_latent_summed", HEADS * NBLK)
    qa_c = sg("q_latent_copied", HEADS * NBLK)
    qas_ok = sg("q_latent_sample_ready", 2)
    qrs_ok = sg("q_rope_sample_ready", 1)
    score = sg("scores_ready", NJOBS)
    negmax = sg("negmax_ready", NJOBS)
    expd = sg("exp_ready", NJOBS)
    p_ok = sg("probs_ready", NJOBS)
    pt_T = sg("probs_turned", NUNITS)
    pt_c = [sg("probs_turned_copied_by_scalar", COPIER.count(0)), sg("probs_turned_copied_by_vector", COPIER.count(1))]
    pv = sg("values_weighted", NUNITS)
    swa_ok = sg("swa_gated", N_SWA)
    ol_c = sg("latent_out_copied", N_MLA)
    conv_ok = sg("convolution_gated", 1)
    uv_mm = sg("mla_out_summed", TILES)
    uv_ok = sg("mla_gated", TILES)
    ct_T = sg("caches_turned", 1 + 2 * NB)
    ct_c = sg("caches_copied", 1 + 2 * NB)
    act_before = sg("scalar_step_before")
    dve_before = sg("vector_step_before")
    act_step = sg("scalar_step", ACT_STEPS)
    dve_step = sg("vector_step", DVE_STEPS)
    s_const = sg("constants_landed")
    s_tok = [sg(f"tokens_landed{i}") for i in range(3)]
    s_modw = [sg(f"first_modulation_landed{i}") for i in range(4)]
    s_row = sg("first_modulation_rows_summed")
    s_rowc = sg("first_modulation_rows_copied")
    s_mod = sg("first_modulation_summed")
    s_modc = sg("first_modulation_copied")
    s_c = sg("c_landed")
    s_cs = sg("c_silu")
    s_cT = sg("c_turned")
    s_xT = sg("tokens_turned")
    s_xa = sg("tokens_copied_by_scalar")
    s_xv = sg("tokens_copied_by_vector")
    s_cst = sg("constants_made")
    s_yT = sg("y_turned")
    s_ya = sg("y_copied_by_scalar")
    s_yv = sg("y_copied_by_vector")
    s_out = sg("y_stored")

    def zset(c):
        return psum[:, 3 * (c % 2):3 * (c % 2) + 3, 0:BLK]

    def b3(t):
        return t.rearrange("p (n t) -> p n t", t=BLK)

    def blk(n):
        return slice(n * BLK, (n + 1) * BLK)

    def spread(ap, n):
        return ap.unsqueeze(2).broadcast_to([ap.shape[0], ap.shape[1], n])

    def tile(t):
        return slice(t * P, (t + 1) * P)

    HALVES = (slice(0, 64), slice(64, 128))
    QUADS = [(0, 32), (32, 0), (64, 96), (96, 64)]

    def w_views(c, last):
        if c >= NIN:
            s = plans[last][1][("out", (c - NIN) // 2)]
            src = raw[:, s[0], :, (c % 2) * P:(c % 2 + 1) * P]
            return s, src, lambda w: w[:, :, :]
        pair = c // 2
        s = plans[last][1][("in", pair)]
        r = raw[:, s[0], :, :]
        if pair == KV_KR and c % 2 == 1:
            src = r[:, :, 128:192].unsqueeze(2).broadcast_to([P, KD, 2, 64])
            return s, src, lambda w: w[:, :, :].rearrange("p k (a d) -> p k a d", a=2)
        if pair in (S_Q, S_G):
            g = c % 2
            src = r.rearrange("p k (a g d) -> p k g a d", a=2, g=2)[:, :, g]
            return s, src, lambda w: w[:, :, :].rearrange("p k (a d) -> p k a d", a=2)
        return s, r[:, :, (c % 2) * P:(c % 2 + 1) * P], lambda w: w[:, :, :]

    def job_shape(j):
        g = GROUP_OF[j]
        if g["kind"] == "swa_p":
            return P, HEADS, P * len(g["keys"]), True
        if g["kind"] == "swa_s":
            return P, 1, 640, True
        if g["kind"] == "mla_p":
            return P, 1, P * len(g["keys"]), False
        return HEADS * TS, 1, 640, False

    def s_view(j):
        rows, nh, w, _ = job_shape(j)
        s = psum[0:rows, 2 * (j % 2):2 * (j % 2) + 2, :].rearrange("p a b -> p (a b)")
        if nh == 1:
            return s[:, 0:w].unsqueeze(1)
        return s.rearrange("p (h w) -> p h w", h=HEADS)[:, :, 0:w]

    def probs(j):
        s = slot_of(j)
        return probs_lo[:, s, :] if s < 6 else probs_hi[:, s - 6, :]

    def p_view(j):
        rows, nh, w, _ = job_shape(j)
        s = probs(j)[0:rows, :]
        if nh == 1:
            return s[:, 0:w].unsqueeze(1)
        return s.rearrange("p (h w) -> p h w", h=HEADS)[:, :, 0:w]

    with nc.Block() as block:

        @block.sync
        def _(sp):
            sp.dma_start(ident[:], io["c_ident"]).then_inc(s_const.sem, 16)
            sp.dma_start(masks_f[:], io["c_masks"]).then_inc(s_const.sem, 16)
            sp.dma_start(crow[0:1, :], io["c_prompt"]).then_inc(s_c.sem, 16)
            sp.dma_start(crow[1:1 + NB, :], io["c_sample"]).then_inc(s_c.sem, 16)
            sp.dma_start(frow[:], io["final_norm_g"].rearrange("(k p) -> k p", p=P)).then_inc(s_c.sem, 16)
            xp = io["x_prompt"].rearrange("b (t p) d -> p (b t) d", p=P)
            for i, (a, b) in enumerate(((0, 4), (4, 8))):
                sp.dma_start(tok[:, a:b, :], xp[:, a:b, :]).then_inc(s_tok[i].sem, 16)
            sp.dma_start(tok[:, ST, :], io["x_sample"].rearrange("b t d -> (b t) d")).then_inc(s_tok[2].sem, 16)
            def load_pair(layer, i, slot):
                c0, w = PAIRS[i]
                src = io["w_in"][layer].rearrange("(k p) n -> p k n", p=P)[:, :, c0:c0 + w]
                for ks in ((slice(4, 8), slice(0, 4)) if i == CV_H else (slice(0, KD),)):
                    sp.dma_start(raw[:, slot, ks, 0:w], src[:, ks]).then_inc(w_in[slot].sem, 16)

            def load_vectors(layer):
                for a, b, name in ((V_G, V_BMOD, "norm_g"), (V_BMOD, V_QG, "b_mod"), (V_QG, V_KVG, "q_norm_g"),
                                   (V_KVG, V_CONV, "kv_norm_g")):
                    sp.dma_start(vrows[a:b, :], io[name][layer].rearrange("(r c) -> r c", c=P))\
                        .then_inc(vec_in.sem, 16)
                sp.dma_start(vrows[V_CONV:V_ROWS, :], io["conv_w"][layer].rearrange("k (j c) -> (k j) c", c=P))\
                    .then_inc(vec_in.sem, 16)
                sp.dma_start(ccrow[:], io["cache_conv"][layer].rearrange("b t c -> (b t) c")).then_inc(vec_in.sem, 16)
                sp.dma_start(sink[:], io["swa_sink"][layer].unsqueeze(0).broadcast_to([P, HEADS]))\
                    .then_inc(vec_in.sem, 16)

            load_vectors(0)
            for k in range(KD):
                sp.dma_start(modw[:, k, :], io["w_mod"][0, tile(k), 0:2 * D]).then_inc(s_modw[k // 2].sem, 16)
            load_pair(0, 0, 0)
            load_pair(0, 1, 1)
            sp.dma_start(tab[:], io["c_rope"][0]).then_inc(tab_in.sem, 16)
            sp.wait_ge(s_xa.sem, TILES)
            sp.wait_ge(s_xv.sem, TILES)
            sp.dma_start(xT, x[:]).then_inc(x_out.sem, 16)

            def layer(L, last):
                lane = Lane(sp, L)
                loads, plan, _ = plans[last]

                def free(x):
                    kind, i = x
                    if kind in ("in", "out"):
                        sp.wait_ge(lo_w.sem, lo_w.at(lane.layer, 2 * i + 2 + (NIN if kind == "out" else 0)))
                    elif kind == "uq":
                        sp.wait_ge(qr_mm.sem, qr_mm.at(lane.layer, 2 * NBLK))
                    elif kind == "ukv":
                        sp.wait_ge(w_uv_ok.sem, w_uv_ok.at(lane.layer, 1))
                    elif kind == "gate":
                        sp.wait_ge(gate_mm.sem, gate_mm.at(lane.layer, i + 1))
                    else:
                        sp.wait_ge(next_mm.sem, next_mm.at(lane.layer, i + 1))

                def load(x):
                    kind, i = x
                    slot = plan[x][0]
                    before = [y for y in [("in", 0), ("in", 1)] + loads[:loads.index(x)] if plan[y][0] == slot][-1]
                    free(before)
                    sem = w_in[slot].sem
                    if kind in ("gate", "next"):
                        lm, col = (L, 2 * D + 256 * i) if kind == "gate" else (L + 1, 256 * i)
                        src = io["w_mod"][lm].rearrange("(k p) n -> p k n", p=P)[:, :, col:col + 256]
                        for ks in ((slice(4, 8), slice(0, 4)) if col == 0 else (slice(0, KD),)):
                            sp.dma_start(raw[:, slot, ks], src[:, ks]).then_inc(sem, 16)
                    elif kind == "in":
                        load_pair(L, i, slot)
                    elif kind == "after":
                        load_pair(L + 1, i, slot)
                    elif kind == "ukv":
                        sp.dma_start(w_ukv[:], io["w_ukv"][L].rearrange("p (h n) -> p h n", h=HEADS)).then_inc(sem, 16)
                    elif kind == "uq":
                        for k in range(2):
                            src = io["w_uq"][L, tile(k)].rearrange("p (h c) -> p h c", h=HEADS)
                            for a, w in ((P, 64), (0, P)):
                                dst = w_uq[:, k, HEADS * a:HEADS * (a + w)].rearrange("p (h c) -> p h c", h=HEADS)
                                sp.dma_start(dst, src[:, :, a:a + w]).then_inc(sem, 16)
                    else:
                        cols = slice(256 * i, 256 * i + 256)
                        src = io["w_out"][L, 0:768].rearrange("(k p) n -> p k n", p=P)[:, :, cols]
                        for kv in range(2):
                            src2 = io["w_out"][L, 768 + 128 * kv:896 + 128 * kv].rearrange(
                                "(g p) n -> p g n", g=2)[:, :, cols]
                            sp.dma_start(raw[HALVES[kv], slot, 6:8, :], src2).then_inc(sem, 16)
                        sp.dma_start(raw[:, slot, 0:6, :], src).then_inc(sem, 16)

                def rope_table(which, used):
                    sp.wait_ge(roped.sem, roped.at(lane.layer, used))
                    sp.dma_start(tab[:], io["c_rope"][which]).then_inc(tab_in.sem, 16)

                def cache(b):
                    s = b % CACHE_SLOTS
                    if b < 2:
                        sp.wait_ge(qa_mm.sem, qa_mm.at(lane.layer, HEADS * NBLK))
                    elif b == 2:
                        sp.wait_ge(pv.sem, pv.at(lane.layer, GROUPS[ST]["units"][-1] + 1))
                    elif b < CACHE_SLOTS:
                        sp.wait_ge(pv.sem, pv.at(lane.layer, GROUPS[FIRST_S - 2]["units"][-1] + 1))
                    else:
                        sp.wait_ge(pv.sem, pv.at(lane.layer, GROUPS[FIRST_S + b - CACHE_SLOTS]["units"][-1] + 1))
                    sp.dma_start(raw_ckv[s][:], io["cache_mla_ckv"][L, b].rearrange("(t p) c -> p t c", p=P))\
                        .then_inc(mlc_in[s].sem, 16)
                    for half in HALVES:
                        sp.dma_start(raw_kr[s][:, :, half],
                                     io["cache_mla_krope"][L, b].rearrange("(t p) c -> p t c", p=P))\
                            .then_inc(mlc_in[s].sem, 16)

                for x_ in loads[:len(PAIRS) - 2]:
                    load(x_)
                    if x_ == ("in", S_Q):
                        rope_table(1, 1)
                    elif x_ == ("in", CV_H):
                        rope_table(0, 4)
                load(("uq", 0))
                load(("ukv", 0))
                sp.wait_ge(z_done.sem, z_done.at(lane.layer, NIN))
                for dst, name in ((sk_c, "cache_swa_k"), (sv_c, "cache_swa_v")):
                    sp.dma_start(dst[:], io[name][L].rearrange("b s h d -> (b s) (h d)")
                                 .rearrange("(t p) c -> p t c", p=P)).then_inc(swc_in.sem, 16)
                when = {("gate", i): gi for gi, i in GATE_AT.items()}
                when.update({("next", i): gi for gi, i in NEXT_AT.items()})
                when.update({("uq", 0): -2, ("ukv", 0): -3})
                todo = [(-1 if b < 2 else ST + 0.5 if b == 2 else FIRST_S - 1.5 if b < CACHE_SLOTS
                         else FIRST_S + b - CACHE_SLOTS + 0.5, cache, b) for b in range(NB)]
                for x_ in [x for x in loads if x[0] in ("gate", "next") or x in (("out", 0), ("out", 1))]:
                    slot = plan[x_][0]
                    before = [y for y in loads[:loads.index(x_)] if plan[y][0] == slot][-1]
                    todo.append((when[before], load, x_))
                for _, do, what in sorted(todo, key=lambda e: e[0]):
                    do(what)
                sp.wait_ge(x_out.sem, x_out.at(lane.layer, 0))
                sp.wait_ge(hi_h.sem, hi_h.at(lane.layer, 2 * NBLK + 1))
                for i in range(2):
                    sp.dma_start(x[:, 4 * i:4 * i + 4, :], xT[:, 4 * i:4 * i + 4, :]).then_inc(x_in[i].sem, 16)
                load(("out", 2))
                load(("out", 3))
                if last:
                    return
                load_vectors(L + 1)
                sp.dma_start(tab[:], io["c_rope"][0]).then_inc(tab_in.sem, 16)
                for k in range(KD):
                    sp.wait_ge(z_dve.sem, z_dve.at(lane.layer, NIN + k + 1))
                    sp.dma_start(xT[:, k, :], x[:, k, :]).then_inc(x_out.sem, 16)
                    if k in (3, 5):
                        load(("after", (5 - k) // 2))

            with sp.Fori(0, DEPTH - 1) as L:
                layer(L, False)
            layer(DEPTH - 1, True)
            for t in range(TILES):
                sp.wait_ge(s_ya.sem, t + 1)
                sp.wait_ge(s_yv.sem, t + 1)
                dst = (io["y_sample"].rearrange("b t d -> (b t) d") if t == ST
                       else io["y_prompt"][0, tile(t), :])
                sp.dma_start(dst, tok[:, t, :]).then_inc(s_out.sem, 16)
            sp.wait_ge(s_out.sem, 16 * TILES)
            sp.wait_ge(outs.sem, outs.at(DEPTH, 0))
            sp.wait_ge(x_out.sem, x_out.at(DEPTH - 1, 0))

        @block.gpsimd
        def _(pool):
            pool.memset(ones[:], 1.0).then_inc(s_cst.sem, 1)
            pool.memset(mhalf[:], -0.5).then_inc(s_cst.sem, 1)
            pool.memset(qrs[:], 0.0).then_inc(s_cst.sem, 1)
            pool.wait_ge(s_cst.sem, 4)

            def x_rstd(lane, before):
                for k in range(1, KD - 1):
                    pool.wait_ge(sq_x.sem, sq_x.at(lane.layer, k + 1))
                    lane.link(pool.tensor_tensor(mix[:, 0, :], mix[:, 0, :], mix[:, k, :], ALU.add), acc_x)
                pool.wait_ge(mean_x.sem, mean_x.at(lane.layer, 1))
                if before:
                    pool.wait_ge(bc_x.sem, bc_x.at(lane.layer, NBLK))
                pool.tensor_tensor(rstd[:], mean[:], mhalf[:], ALU.pow).then_inc(rstd_x.sem, 1)

            def layer(L, last):
                lane = Lane(pool, L)
                pool.wait_ge(z_act.sem, z_act.at(lane.layer, 2 * Q_LAT + 2))
                pool.tensor_tensor(mix[:, 1, :], mix[:, 1, :], mix[:, 5, :], ALU.add).then_inc(lat_acc.sem, 1)
                for i in range(2):
                    pool.wait_ge(lat_mean.sem, lat_mean.at(lane.layer, i + 1))
                    pool.tensor_tensor(rstdl[:, i, :], meanl[:, i, :], mhalf[:], ALU.pow).then_inc(lat_rstd.sem, 1)
                x_rstd(lane, True)

            x_rstd(Lane(pool, -1), False)
            with pool.Fori(0, DEPTH - 1) as L:
                layer(L, False)
            layer(DEPTH - 1, True)

        @block.tensor
        def _(pe):
            def x_sums(lane, k):
                if k == 0:
                    pe.wait_ge(acc_x.sem, acc_x.at(lane.layer, KD - 2))
                else:
                    pe.wait_ge(sq_x.sem, sq_x.at(lane.layer, KD))
                for t in range(TILES):
                    mm = pe.matmul(psum[:, 6, t:t + 1], mix[:, k, tile(t)], ones[:],
                                   start=(k == 0 and t == 0), stop=(k == KD - 1 and t == TILES - 1))
                if k:
                    mm.then_inc(sum_x.sem, 1)

            def turn_vectors(lane):
                pe.wait_ge(vec_in.sem, vec_in.at(lane.layer, 16 * 7))
                pe.matmul(psum[:, 7, 0:V_ROWS], vrows[:], ident[0:V_ROWS, 0:V_ROWS], start=True, stop=True)
                for j in range(2):
                    mm = pe.transpose(psum[:, 7, 64 + 16 * j:80 + 16 * j], ccrow[:, tile(j)], ident[0:16, 0:16])
                mm.then_inc(small_T.sem, 1)

            def x_spread(lane, final=False):
                for n in range(NBLK):
                    if n == 0:
                        pe.wait_ge(rstd_x.sem, rstd_x.at(lane.layer, 0))
                    elif n == 1 and not final:
                        pe.wait_ge(small_v.sem, small_v.at(lane.layer, 0))
                    elif n == 2:
                        pe.wait_ge(scaled_x.sem, scaled_x.at(lane.layer, 2))
                    for i in range(3):
                        mm = pe.matmul(psum[:, 6 + n % 2, tile(i)],
                                       rstd[:, 3 * n + i:3 * n + i + 1].broadcast_to([P, P]),
                                       ident[:], start=True, stop=True)
                    mm.then_inc(bc_x.sem, 1)

            pe.wait_ge(s_const.sem, 32)
            pe.wait_ge(s_cst.sem, 4)
            bank = 0
            for t in range(TILES):
                pe.wait_ge(s_tok[min(t // 4, 2)].sem, 16)
                for half in range(2):
                    n = 2 * t + half
                    if t >= 2:
                        pe.wait_ge((s_xa, s_xv)[half].sem, t - 1)
                    for k in range(4):
                        mm = pe.transpose(psum[:, n % 4, tile(k)], tok[:, t, tile(4 * half + k)], ident[:])
                    mm.then_inc(s_xT.sem, 1)
            pe.wait_ge(s_cs.sem, 3)
            for k in range(KD):
                mm = pe.transpose(psum[:, 5, 16 * k:16 * k + 1 + NB], csil[:, tile(k)], ident[0:1 + NB, 0:1 + NB])
            mm = pe.transpose(psum[:, 5, 256:256 + KD], frow[:], ident[0:KD, 0:KD])
            mm.then_inc(s_cT.sem, 1)
            pe.wait_ge(s_cT.sem, 3)

            before = Lane(pe, -1)
            turn_vectors(before)
            for k in range(KD):
                if k % 2 == 0:
                    pe.wait_ge(s_modw[k // 2].sem, 32)
                if k == 0:
                    pe.wait_ge(s_xa.sem, TILES)
                    pe.wait_ge(s_xv.sem, TILES)
                for i in range(4):
                    mm = pe.matmul(psum[0:1 + NB, i, :], cT[:, k, :], modw[:, k, 512 * i:512 * i + 512],
                                   start=(k == 0), stop=(k == KD - 1))
                    if k == KD - 1:
                        mm.then_inc(s_row.sem, 1)
                if k == 5:
                    x_sums(before, 0)
                    x_sums(before, KD - 1)
            for i in range(2 * KD):
                if i % 4 == 0:
                    pe.wait_ge(s_rowc.sem, i // 4 + 1)
                mm = pe.matmul(psum[:, 4, i * (1 + NB):(i + 1) * (1 + NB)], modrow0[:, tile(i)],
                               ident[0:1 + NB, 0:1 + NB], start=True, stop=True)
            mm.then_inc(s_mod.sem, 1)
            pe.sem_inc(z_done.sem, 1)

            def layer(L, last):
                lane = Lane(pe, L)
                plan = plans[last][1]

                def modulation(kind, i, sig):
                    s, count = plan[(kind, i)]
                    pe.wait_ge(w_in[s].sem, w_in[s].at(lane.layer, count))
                    for k in range(KD):
                        mm = pe.matmul(psum[0:1 + NB, 7, 0:256], cT[:, k, :], raw[:, s, k, :],
                                       start=(k == 0), stop=(k == KD - 1))
                    mm.then_inc(sig.sem, 1)

                def chunk(c, s):
                    pe.wait_ge(lo_w.sem, lo_w.at(lane.layer, c + 1))
                    pe.wait_ge(z_dve.sem, z_dve.at(lane.layer, c - 1))
                    for n in range(NBLK):
                        for k in range(KD):
                            for i, (w, h) in enumerate(((w_hi, h_hi), (w_lo, h_hi), (w_hi, h_lo))):
                                mm = pe.matmul(psum[:, 3 * s + n, 0:BLK], w[s][:, k, :], h[:, k, blk(n)],
                                               start=(k == 0 and i == 0), stop=(k == KD - 1 and i == 2))
                    mm.then_inc(z_done.sem, 1)

                def first_chunks(c, base):
                    pe.wait_ge(lo_w.sem, lo_w.at(lane.layer, c + 2))
                    pe.wait_ge(z_dve.sem, z_dve.at(lane.layer, c))

                    def part(s, n, half):
                        for k in range(4 * half, 4 * half + 4):
                            for i, (w, h) in enumerate(((w_hi, h_hi), (w_lo, h_hi), (w_hi, h_lo))):
                                mm = pe.matmul(psum[:, 3 * s + n, 0:BLK], w[s][:, k, :], h[:, k, blk(n)],
                                               start=(k == 0 and i == 0), stop=(k == KD - 1 and i == 2))
                        return mm

                    for n in range(NBLK - 1):
                        for half in range(2):
                            pe.wait_ge(lo_h.sem, lo_h.at(lane.layer, base + 2 * n + half + 1))
                            part(0, n, half)
                            part(1, n, half)
                    for half in range(2):
                        pe.wait_ge(lo_h.sem, lo_h.at(lane.layer, base + 2 * (NBLK - 1) + half + 1))
                        mm = part(0, NBLK - 1, half)
                    mm.then_inc(z_done.sem, 1)
                    part(1, NBLK - 1, 0)
                    part(1, NBLK - 1, 1).then_inc(z_done.sem, 1)

                def chunks(first, end):
                    with pe.Fori(first, end, 2) as c:
                        chunk(c, 0)
                        chunk(c + 1, 1)

                x_spread(lane)
                first_chunks(0, 0)
                chunks(2, 2 * SPLIT_AFTER)

                pe.wait_ge(z_act.sem, z_act.at(lane.layer, 2 * Q_LAT + 2))
                pe.wait_ge(scaled_x.sem, scaled_x.at(lane.layer, 2 * NBLK))
                pe.wait_ge(lat_acc.sem, lat_acc.at(lane.layer, 1))
                for i in range(2):
                    for t in range(TILES):
                        mm = pe.matmul(psum[:, 6, 16 * i + t:16 * i + t + 1], mix[:, i, tile(t)], ones[:],
                                       start=True, stop=True)
                mm.then_inc(lat_sum.sem, 1)
                pe.wait_ge(z_dve.sem, z_dve.at(lane.layer, 2 * SK_SV + 2))
                for n in range(3):
                    if n:
                        pe.wait_ge(svt_c.sem, svt_c.at(lane.layer, n))
                    for i in range(4 if n < 2 else 1):
                        mm = pe.transpose(psum[:, 7, tile(i)], svT[:, tile(4 * n + i)], ident[:])
                    mm.then_inc(svt_T.sem, 1)
                chunks(2 * SPLIT_AFTER, 2 * SPLIT_AFTER + 2)
                pe.wait_ge(lat_mean.sem, lat_mean.at(lane.layer, 2))
                pe.wait_ge(svt_c.sem, svt_c.at(lane.layer, 3))
                for m in range(2 * NBLK):
                    i, n = divmod(m, NBLK)
                    pe.wait_ge(lat_rstd.sem, lat_rstd.at(lane.layer, i + 1))
                    if m >= 2:
                        pe.wait_ge(lat_ok.sem, lat_ok.at(lane.layer, m - 1))
                    for t in range(3):
                        mm = pe.matmul(psum[:, 6 + m % 2, tile(t)],
                                       rstdl[:, i, 3 * n + t:3 * n + t + 1].broadcast_to([P, P]), ident[:],
                                       start=True, stop=True)
                    mm.then_inc(lat_bc.sem, 1)
                chunks(2 * SPLIT_AFTER + 2, NIN)

                def turned(n, parts):
                    if n < 2:
                        pe.wait_ge(z_dve.sem, z_dve.at(lane.layer, NIN))
                    else:
                        pe.wait_ge(turn_c.sem, turn_c.at(lane.layer, n - 1))
                    for out, in_, k in parts:
                        mm = pe.transpose(psum[0:out[0], 4 + n % 2, out[1]:out[1] + k], in_, ident[0:k, 0:k])
                    mm.then_inc(turn_T.sem, 1)

                pe.wait_ge(lat_ok.sem, lat_ok.at(lane.layer, 2 * NBLK))
                pe.wait_ge(svt_c.sem, svt_c.at(lane.layer, 3))
                for n in range(3):
                    turned(n, [((P, P * i), ckvT[:, tile(4 * n + i)], P) for i in range(4 if n < 2 else 1)])
                for i in range(2):
                    turned(3 + i, [((P, 0), skT[:, tile(ST - 1 + i)], P)]
                           + [((P, P + 64 * t), krT[0:64, tile(6 * i + t)], 64) for t in range(6 - 3 * i)])
                turned(5, [((2 + 2 * NB, P * j), state[:, j, :], P) for j in range(2)])
                pe.wait_ge(w_in[plan[("ukv", 0)][0]].sem, w_in[plan[("ukv", 0)][0]].at(lane.layer, plan[("ukv", 0)][1]))
                turned(6, [((P, P * h), w_ukv[:, h, 0:P], P) for h in range(HEADS)])

                s_uq, count = plan[("uq", 0)]
                pe.wait_ge(w_in[s_uq].sem, w_in[s_uq].at(lane.layer, count))
                for k in range(2):
                    turned(7 + k, [((P, P * h), w_uq[:, k, tile(h)], P) for h in range(HEADS)])

                def q_rope(m):
                    n, j = divmod(m, 2)
                    if m >= 2:
                        pe.wait_ge(roped.sem, roped.at(lane.layer, 4 + m - 1))
                    for k in range(2):
                        w = w_uq[:, k, HEADS * P + P * j:HEADS * P + P * j + P]
                        mm = pe.matmul(psum[:, m % 2, 0:BLK], w, cq[:, k, blk(n)], start=(k == 0), stop=(k == 1))
                    mm.then_inc(qr_mm.sem, 1)

                def q_latent(m):
                    n, h = divmod(m, HEADS)
                    if m >= 2:
                        pe.wait_ge(qa_c.sem, qa_c.at(lane.layer, m - 1))
                    for k in range(2):
                        mm = pe.matmul(psum[:, 4 + m % 2, 0:BLK], mq[:, k, h, :], cq[:, k, blk(n)],
                                       start=(k == 0), stop=(k == 1))
                    mm.then_inc(qa_mm.sem, 1)

                q_rope(0)
                q_rope(1)
                pe.wait_ge(turn_c.sem, turn_c.at(lane.layer, 9))
                for k in range(2):
                    for h in range(HEADS):
                        mm = pe.matmul(psum[:, 6 + k, tile(h)], w_uqT[:, h, tile(k)], w_ukT[:, h, :], start=True, stop=True)
                    mm.then_inc(mq_mm.sem, 1)
                pe.wait_ge(mq_c.sem, mq_c.at(lane.layer, 2))
                for n in range(NBLK):
                    if n:
                        q_rope(2 * n)
                        q_rope(2 * n + 1)
                    for h in range(HEADS):
                        q_latent(HEADS * n + h)

                bank7 = [mq_c, 2]
                turns = [0]
                turned_for = {}
                summed = {"swa": 0, "mla": 0}

                def free_bank7():
                    pe.wait_ge(bank7[0].sem, bank7[0].at(lane.layer, bank7[1]))

                def cache(gi, part):
                    g = GROUPS[gi]
                    if g["kind"] == "swa_s":
                        pe.wait_ge(swc_in.sem, swc_in.at(lane.layer, 32))
                        src = sk_c
                    else:
                        s = g["idx"] % CACHE_SLOTS
                        pe.wait_ge(mlc_in[s].sem, mlc_in[s].at(lane.layer, 48 * (g["idx"] // CACHE_SLOTS + 1)))
                        src = (raw_ckv, raw_kr)[part][s]
                    free_bank7()
                    for i in range(4):
                        mm = pe.transpose(psum[:, 7, tile(i)], src[:, i, :], ident[:])
                    mm.then_inc(ct_T.sem, 1)
                    turns[0] += 1
                    turned_for[gi] = turns[0]
                    bank7[:] = [ct_c, turns[0]]

                def scores(j):
                    g = GROUP_OF[j]
                    gi, t, i = GROUPS.index(g), g["idx"], g["jobs"].index(j)
                    if j >= 2:
                        pe.wait_ge(expd.sem, expd.at(lane.layer, j - 1))
                    else:
                        pe.wait_ge(roped.sem, roped.at(lane.layer, 4 + 2 * NBLK))
                    out = psum[:, 2 * (j % 2):2 * (j % 2) + 2, :].rearrange("p a b -> p (a b)")
                    if g["kind"] == "swa_p":
                        ks, w = g["keys"], P * len(g["keys"])
                        for h in range(HEADS):
                            half = HALVES[h // 2]
                            pe.matmul(out[:, 256 * h:256 * h + w], sqT[half, h % 2, tile(t)],
                                      skT[half, ks[0] * P:(t + 1) * P], start=True, stop=False)
                            mm = pe.matmul(out[:, 256 * h:256 * h + w], half_rows[0:2, :], band_mask[0:2, 256 - w:256],
                                           start=False, stop=True)
                    elif g["kind"] == "swa_s":
                        half = HALVES[i // 2]
                        if i == 0:
                            pe.wait_ge(ct_c.sem, ct_c.at(lane.layer, turned_for[gi]))
                        for a, b, keys in ((0, 512, skT_c[half, :]), (512, 640, skT[half, SEQ:NTOK])):
                            pe.matmul(out[:, a:b], sqT[half, i % 2, tile(ST)], keys, start=True, stop=False)
                            mm = pe.matmul(out[:, a:b], own8, block_mask[:, a:b], start=False, stop=True)
                    elif g["kind"] == "mla_p":
                        w = (t + 1) * P
                        if t < SPLIT_FROM:
                            half = HALVES[i % 2]
                            pe.wait_ge(qa_c.sem, qa_c.at(lane.layer, HEADS * NBLK))
                            pe.matmul(out[:, 0:w], qa[:, i, tile(t)], ckvT[:, 0:w], start=True, stop=False)
                            pe.matmul(out[:, 0:w], qr[half, i // 2, tile(t)], krT[half, 0:w], start=False, stop=False)
                        elif i == 0:
                            pe.wait_ge(key_lo.sem, key_lo.at(lane.layer, 2))
                            pe.wait_ge(q_st.sem, q_st.at(lane.layer, t - SPLIT_FROM + 1))
                        for a in range(0, w if t >= SPLIT_FROM else 0, 512):
                            b = min(a + 512, w)
                            for n, (q, k) in enumerate(((qa_hi[t % 2][:, i, :], ckv_hi), (qa_hi[t % 2][:, i, :], ckv_lo),
                                                        (qa_lo[t % 2][:, i, :], ckv_hi),
                                                        (qst[t % 2][:, i % 2, i // 2, :], kr_hi),
                                                        (qst[t % 2][:, i % 2, i // 2, :], kr_lo))):
                                pe.matmul(out[:, a:b], q, k[:, a:b], start=(n == 0), stop=(n == 4 and b < w))
                        mm = pe.matmul(out[:, w - CH:w], half_rows[0:1, :], band_mask[0:1, 256 - CH:256],
                                       start=False, stop=True)
                    else:
                        pe.wait_ge(ct_c.sem, ct_c.at(lane.layer, turned_for[gi]))
                        pe.wait_ge(qas_ok.sem, qas_ok.at(lane.layer, 2))
                        for a, e, kc, kr_ in ((0, 512, ckvT_c[t % 2][:], krT_c[t % 2][:]),
                                              (512, 640, ckvT[:, SEQ:NTOK], krT[:, SEQ:NTOK])):
                            pe.matmul(out[0:64, a:e], qas[:, t, :], kc, start=True, stop=False)
                            mm = pe.matmul(out[0:64, a:e], qrs[:, t, :], kr_, start=False, stop=(a == 0))
                        mm = pe.matmul(out[0:64, 512:640], own64[:, 64 * t:64 * t + 64], block_mask[:, 512:640],
                                       start=False, stop=True)
                    mm.then_inc(score.sem, 1)

                def turn_probs(n):
                    g = UNIT_OF[n]
                    i = g["units"].index(n)
                    if n >= 2:
                        pe.wait_ge(pt_c[COPIER[n - 2]].sem, pt_c[COPIER[n - 2]].at(lane.layer, COPIES[n - 2]))
                    else:
                        pe.wait_ge(qa_c.sem, qa_c.at(lane.layer, HEADS * NBLK))
                    if i == 0:
                        pe.wait_ge(p_ok.sem, p_ok.at(lane.layer, g["jobs"][-1] + 1))
                    out = psum[:, 4 + n % 2, :]
                    if g["kind"] == "mla_s":
                        for k in range(5):
                            mm = pe.matmul(out[:, 64 * k:64 * k + 64], probs(g["jobs"][0])[0:64, tile(k)], ident[0:64, 0:64],
                                           start=True, stop=True)
                    else:
                        for h in range(HEADS):
                            if g["kind"] == "swa_p":
                                pr = probs(g["jobs"][0])[:, 256 * h + P * i:256 * h + P * i + P]
                            else:
                                pr = probs(g["jobs"][h])[:, tile(i)]
                            mm = pe.transpose(out[:, tile(h)], pr, ident[:])
                    mm.then_inc(pt_T.sem, 1)

                def weigh(n):
                    g = UNIT_OF[n]
                    i = g["units"].index(n)
                    gi = GROUPS.index(g)
                    last_one = i == len(g["units"]) - 1
                    if i == 0 and gi:
                        if GROUPS[gi - 1]["kind"][:3] == "swa":
                            pe.wait_ge(swa_ok.sem, swa_ok.at(lane.layer, summed["swa"]))
                        else:
                            pe.wait_ge(ol_c.sem, ol_c.at(lane.layer, summed["mla"]))
                    pe.wait_ge(pt_c[COPIER[n]].sem, pt_c[COPIER[n]].at(lane.layer, COPIES[n]))
                    if g["kind"] == "mla_s":
                        s = g["idx"] % CACHE_SLOTS
                        for k in range(5):
                            v = raw_ckv[s][:, k, :] if k < 4 else ckv[:, ST, :]
                            mm = pe.matmul(psum[:, 6, 0:64], v, pT[:, n % 3, 64 * k:64 * k + 64],
                                           start=(k == 0), stop=(k == 4))
                    else:
                        k = g["keys"][i]
                        if g["kind"] == "mla_p":
                            v = ckv[:, k, :]
                        elif g["kind"] == "swa_p":
                            v = sv[:, k, :]
                        else:
                            v = sv_c[:, k, :] if k < 4 else sv[:, ST, :]
                        mm = pe.matmul(psum[:, 6, :], v, pT[:, n % 3, :], start=(i == 0), stop=last_one)
                    mm.then_inc(pv.sem, 1)
                    if last_one:
                        summed[g["kind"][:3]] += 1

                mla_done = [0]

                def up_values(gi):
                    slot = GROUPS[gi]["idx"] % 2 if GROUPS[gi]["kind"] == "mla_p" else 0
                    pe.wait_ge(ol_c.sem, ol_c.at(lane.layer, gi - ST))
                    free_bank7()
                    for h in range(HEADS):
                        mm = pe.matmul(psum[:, 7, tile(h)], w_uv[:, h, :], oL[:, slot, h, :], start=True, stop=True)
                    mm.then_inc(uv_mm.sem, 1)
                    mla_done[0] += 1
                    bank7[:] = [uv_ok, mla_done[0]]

                rows = 0
                for what, i in STEPS:
                    if what == "scores":
                        scores(i)
                    elif what == "turn":
                        turn_probs(i)
                    elif what == "weigh":
                        weigh(i)
                    elif what == "cache":
                        cache(*i)
                    elif what == "up":
                        up_values(i)
                    elif what == "mod" and (i in GATE_AT or not last):
                        free_bank7()
                        if i in GATE_AT:
                            modulation("gate", GATE_AT[i], gate_mm)
                        else:
                            modulation("next", NEXT_AT[i], next_mm)
                        rows += 1
                        bank7[:] = [row_c, rows]
                    elif what == "modT" and (i in GATE_AT or not last):
                        pe.wait_ge(row_c.sem, row_c.at(lane.layer, rows))
                        free_bank7()
                        for j in range(2):
                            mm = pe.matmul(psum[:, 7, j * (1 + NB):(j + 1) * (1 + NB)], modrow[:, tile(j)],
                                           ident[0:1 + NB, 0:1 + NB], start=True, stop=True)
                        mm.then_inc(row_T.sem, 1)
                        bank7[:] = [gate_c, GATE_AT[i] + 1] if i in GATE_AT else [next_c, NEXT_AT[i] + 1]

                first_chunks(NIN, 2 * NBLK)
                chunks(NIN + 2, NCHUNK - 2)
                chunk(NCHUNK - 2, 0)
                pe.wait_ge(uv_ok.sem, uv_ok.at(lane.layer, TILES))
                if not last:
                    turn_vectors(lane)
                chunk(NCHUNK - 1, 1)
                x_sums(lane, 0)
                x_sums(lane, KD - 1)

            with pe.Fori(0, DEPTH - 1) as L:
                layer(L, False)
            layer(DEPTH - 1, True)

            x_spread(Lane(pe, DEPTH), final=True)
            for t in range(TILES):
                if t % 3 == 0:
                    pe.wait_ge(scaled_x.sem, scaled_x.at(DEPTH, 2 * (t // 3) + 2))
                for half in range(2):
                    if t >= 1:
                        pe.wait_ge((s_ya, s_yv)[half].sem, t)
                    for k in range(4):
                        mm = pe.transpose(psum[:, 2 * half, tile(k)], x[:, 4 * half + k, tile(t)], ident[:])
                    mm.then_inc(s_yT.sem, 1)

        @block.scalar
        def _(act):
            act.wait_ge(s_c.sem, 48)
            act.activation(csil[:], crow[:], ACT.Tanh, scale=0.5).then_inc(s_cs.sem, 1)
            for t in range(TILES):
                act.wait_ge(s_xT.sem, 2 * t + 1)
                act.activation(x[:, 0:4, tile(t)], psum[:, (2 * t) % 4, :].rearrange("p (k t) -> p k t", k=4), ACT.Copy)\
                    .then_inc(s_xa.sem, 1)
            act.wait_ge(s_xa.sem, TILES)
            act.wait_ge(s_xv.sem, TILES)
            act.wait_ge(s_cT.sem, 1)

            def x_square(lane, k):
                lane.link(act.activation(mix[:, k, :], x[:, k, :], ACT.Square), sq_x)

            before = Lane(act, -1, act_before)
            for k in range(KD):
                x_square(before, k)

            def layer(L, last):
                lane = Lane(act, L, act_step)

                def split_w(c):
                    (s, count), src, view = w_views(c, last)
                    act.wait_ge(w_in[s].sem, w_in[s].at(lane.layer, count))
                    lane.link(act.activation(view(w_hi[c % 2]), src, ACT.Copy), hi_w)

                def rotate(src, pick, sig):
                    for i, (a, b) in enumerate(QUADS):
                        ins = act.activation(pick(rot[a:a + 32, :]), src[b:b + 32], ACT.Copy)
                        lane.link(ins, sig if i == 3 else None)

                def chunk(c):
                    pair, j = divmod(c, 2)
                    z = zset(c)
                    act.wait_ge(z_done.sem, z_done.at(lane.layer, c + 1))
                    if pair in (KV_KR, Q_LAT) and (pair, j) != (KV_KR, 1):
                        k = {0: 0, 2: 1, 3: 5}[c]
                        lane.link(act.activation(b3(mix[:, k, :]), z, ACT.Square), z_act)
                    elif (pair, j) in ((KV_KR, 1), (SK_SV, 0), (S_Q, 0), (S_Q, 1)):
                        n = {(KV_KR, 1): 0, (SK_SV, 0): 1, (S_Q, 0): 2, (S_Q, 1): 3}[(pair, j)]
                        if n:
                            act.wait_ge(roped.sem, roped.at(lane.layer, n))
                        rotate(z, b3, z_act)
                    elif pair in (S_G, M_G0, M_G1):
                        k = {S_G: 6, M_G0: 2, M_G1: 4}[pair] + j
                        if pair == M_G1:
                            act.wait_ge(lat_sum.sem, lat_sum.at(lane.layer, 1))
                        lane.link(act.activation(b3(mix[:, k, :]), z, ACT.Tanh, scale=0.5), z_act)
                    elif pair == CV_G:
                        act.wait_ge(z_dve.sem, z_dve.at(lane.layer, 2 * CV_B + 2))
                        dst = (rot, svT)[j]
                        lane.link(act.activation(b3(dst[:]), z, ACT.Tanh, scale=0.5), z_act)

                act.wait_ge(z_done.sem, z_done.at(lane.layer, 0))
                split_w(0)
                split_w(1)
                act.wait_ge(mod_v.sem, mod_v.at(lane.layer, 0))
                for n in range(NBLK):
                    width = BLK if n < NBLK - 1 else SEQ - (NBLK - 1) * BLK
                    cols = slice(n * BLK, n * BLK + width)
                    for half in range(2):
                        ks = slice(4 * half, 4 * half + 4)
                        act.wait_ge(scaled_x.sem, scaled_x.at(lane.layer, 2 * n + half + 1))
                        for k in range(4 * half, 4 * half + 4):
                            lane.link(act.activation(x[:, k, cols], x[:, k, cols], ACT.Identity,
                                                     bias=mod[:, 0, k, 0:1], scale=amul[:, k, 0:1]))
                        if n == NBLK - 1:
                            act.wait_ge(h_smp.sem, h_smp.at(lane.layer, 1))
                        lane.link(act.activation(h_hi[:, ks, blk(n)], x[:, ks, blk(n)], ACT.Copy), hi_h)
                for c in range(NIN):
                    if c + 2 < NIN:
                        act.wait_ge(z_done.sem, z_done.at(lane.layer, c + 1))
                        split_w(c + 2)
                    if c in ACT_CHUNKS:
                        chunk(c)
                    if c == 2 * SPLIT_AFTER - 1:
                        for n in range(3):
                            act.wait_ge(svt_T.sem, svt_T.at(lane.layer, n + 1))
                            w = 4 if n < 2 else 1
                            lane.link(act.activation(sv[:, 4 * n:4 * n + w, :],
                                                     psum[:, 7, 0:P * w].rearrange("p (t c) -> p t c", c=P), ACT.Copy),
                                      svt_c)
                        for dst, src in ((io["swa_v_prompt"][L, 0].rearrange("s h d -> s (h d)"), sv[64:128, ST - 1, :]),
                                         (io["swa_v_sample"][L].rearrange("b t h d -> (b t) (h d)"), sv[:, ST, :])):
                            act.dma_start(dst, src).then_inc(outs.sem, 16)

                act.wait_ge(z_done.sem, z_done.at(lane.layer, NIN))
                for n in range(9):
                    act.wait_ge(turn_T.sem, turn_T.at(lane.layer, n + 1))
                    src = psum[:, 4 + n % 2, :]
                    if n < 3:
                        w = 4 if n < 2 else 1
                        out, in_ = ckv[:, 4 * n:4 * n + w, :], src[:, 0:P * w].rearrange("p (t c) -> p t c", c=P)
                    elif n < 5:
                        w = 6 if n == 3 else 3
                        lane.link(act.activation(sk_tok[:, n - 3, :], src[:, 0:P], ACT.Copy))
                        out, in_ = kr_tok[:, 6 * (n - 3):6 * (n - 3) + w, :], src[:, P:P + 64 * w].rearrange(
                            "p (t c) -> p t c", c=64)
                    elif n == 5:
                        out, in_ = state_tok[:], src[0:2 + 2 * NB, 0:CONVW]
                    else:
                        out, in_ = (w_ukT[:] if n == 6 else w_uqT[:, :, tile(n - 7)]), src[:, :].rearrange(
                            "p (h c) -> p h c", c=P)
                    lane.link(act.activation(out, in_, ACT.Copy), turn_c)
                    stores = []
                    if n == 2:
                        stores = [(io["mla_ckv_prompt"][L, 0].rearrange("(t p) c -> p t c", p=P), ckv[:, 0:ST, :]),
                                  (io["mla_ckv_sample"][L].rearrange("b t c -> (b t) c"), ckv[:, ST, :])]
                    elif n == 4:
                        stores = [(io["mla_krope_prompt"][L, 0].rearrange("(t p) c -> p t c", p=P), kr_tok[:, 0:ST, :]),
                                  (io["mla_krope_sample"][L].rearrange("b t c -> (b t) c"), kr_tok[:, ST, :]),
                                  (io["swa_k_prompt"][L, 0].rearrange("s h d -> s (h d)"), sk_tok[64:128, 0, :]),
                                  (io["swa_k_sample"][L].rearrange("b t h d -> (b t) (h d)"), sk_tok[:, 1, :])]
                    elif n == 5:
                        stores = [(io["conv_state_prompt"][L, 0], state_tok[0:2, :]),
                                  (io["conv_state_sample"][L].rearrange("b t c -> (b t) c"), state_tok[2:, :])]
                    for dst, s in stores:
                        act.dma_start(dst, s).then_inc(outs.sem, 16)
                act.wait_ge(z_dve.sem, z_dve.at(lane.layer, NIN))
                act.wait_ge(conv_ok.sem, conv_ok.at(lane.layer, 1))
                lane.link(act.activation(w_uv[:], w_ukv[:, :, P:256], ACT.Copy), w_uv_ok)
                for n in range(NBLK):
                    for m in (2 * n, 2 * n + 1):
                        act.wait_ge(qr_mm.sem, qr_mm.at(lane.layer, m + 1))
                        act.wait_ge(roped.sem, roped.at(lane.layer, 3 + m))
                        rotate(psum[:, m % 2, 0:BLK], lambda r: r[:, (m % 2) * BLK:(m % 2 + 1) * BLK], qr_rot)
                    for h in range(HEADS):
                        m = HEADS * n + h
                        act.wait_ge(qa_mm.sem, qa_mm.at(lane.layer, m + 1))
                        lane.link(act.activation(qa[:, h, blk(n)], psum[:, 4 + m % 2, 0:BLK], ACT.Copy), qa_c)

                turns = [0]

                def cache_copy(gi, part):
                    g = GROUPS[gi]
                    turns[0] += 1
                    act.wait_ge(ct_T.sem, ct_T.at(lane.layer, turns[0]))
                    if g["kind"] == "swa_s":
                        dst = skT_c
                    else:
                        dst = (ckvT_c, krT_c)[part][g["idx"] % 2]
                        if g["idx"] >= 2:
                            act.wait_ge(score.sem, score.at(lane.layer, g["jobs"][0] - 1))
                        elif g["idx"] == 1:
                            act.wait_ge(pv.sem, pv.at(lane.layer, GROUPS[ST]["units"][-1] + 1))
                    lane.link(act.activation(dst[:], psum[:, 7, :], ACT.Copy), ct_c)

                def exps(j):
                    rows, nh, w, has_sink = job_shape(j)
                    s = slot_of(j)
                    scale = SWA_SCALE if has_sink else MLA_SCALE
                    act.wait_ge(negmax.sem, negmax.at(lane.layer, j + 1))
                    if SLOT_FREE[j] is not None:
                        act.wait_ge(pt_T.sem, pt_T.at(lane.layer, SLOT_FREE[j] + 1))
                    for h in range(nh):
                        ins = act.activation(p_view(j)[:, h, :], s_view(j)[:, h, :], ACT.Exp, bias=nmax[0:rows, s, h:h + 1],
                                             scale=scale, accum_out=psum_p[0:rows, s, h:h + 1])
                        lane.link(ins, expd if h == nh - 1 and not has_sink else None)
                    if has_sink:
                        lane.link(act.activation(esink[:, s, 0:nh], esink[:, s, 0:nh], ACT.Exp), expd)

                def out(g):
                    act.wait_ge(pv.sem, pv.at(lane.layer, g["units"][-1] + 1))
                    if g["kind"] == "mla_p":
                        if g["idx"] >= 2:
                            act.wait_ge(uv_mm.sem, uv_mm.at(lane.layer, g["idx"] - 1))
                        lane.link(act.activation(oL[:, g["idx"] % 2], psum[:, 6, :].rearrange("p (h t) -> p h t", h=HEADS),
                                                 ACT.Copy), ol_c)
                    else:
                        if g["idx"] == 0:
                            act.wait_ge(uv_mm.sem, uv_mm.at(lane.layer, ST - 1))
                        b = g["idx"]
                        lane.link(act.activation(
                            oL[:, 0].rearrange("p (j a) t -> p a j t", a=2)[:, :, :, TS * b:TS * b + TS],
                            psum[:, 6, 0:64].rearrange("p (a j t) -> p a j t", a=2, j=2), ACT.Copy), ol_c)

                def split_keys():
                    act.wait_ge(roped.sem, roped.at(lane.layer, 4 + 2 * NBLK))
                    act.wait_ge(qa_mm.sem, qa_mm.at(lane.layer, HEADS * NBLK))
                    lane.link(act.activation(ckv_hi[:], ckvT[:], ACT.Copy), key_hi)
                    lane.link(act.activation(kr_hi[:], krT[:], ACT.Copy), key_hi)

                def split_q(t):
                    if t - 2 >= SPLIT_FROM:
                        act.wait_ge(score.sem, score.at(lane.layer, GROUPS[ST + 1 + t - 2]["jobs"][-1] + 1))
                    elif t % 2 == 1:
                        act.wait_ge(pv.sem, pv.at(lane.layer, GROUPS[ST - 1]["units"][-1] + 1))
                        act.wait_ge(score.sem, score.at(lane.layer, GROUPS[ST]["jobs"][-1] + 1))
                        act.wait_ge(outs.sem, outs.at(lane.layer, 16 * N_STORES))
                    lane.link(act.activation(qa_hi[t % 2][:], qa[:, :, tile(t)], ACT.Copy))
                    for a, half in enumerate(HALVES):
                        lane.link(act.activation(qst[t % 2][half, a], qr[half, :, tile(t)], ACT.Copy), q_hi if a else None)

                def stack_q(t):
                    act.wait_ge(q_lo.sem, q_lo.at(lane.layer, t - SPLIT_FROM + 1))
                    for a, half in enumerate(HALVES):
                        lane.link(act.activation(qst[t % 2][HALVES[1 - a], a], qr_lo[half].bitcast(F32), ACT.Copy),
                                  q_st if a else None)

                for what, i in STEPS:
                    if what == "split_keys":
                        split_keys()
                    elif what == "split_q":
                        split_q(i)
                    elif what == "stack_q":
                        stack_q(i)
                    elif what == "exp":
                        exps(i)
                    elif what == "cache":
                        cache_copy(*i)
                    elif what == "copy" and COPIER[i] == 0:
                        act.wait_ge(pt_T.sem, pt_T.at(lane.layer, i + 1))
                        if i >= 3:
                            act.wait_ge(pv.sem, pv.at(lane.layer, i - 2))
                        w = 320 if UNIT_OF[i]["kind"] == "mla_s" else 512
                        lane.link(act.activation(pT[:, i % 3, 0:w], psum[:, 4 + i % 2, 0:w], ACT.Copy), pt_c[0])
                    elif what == "split":
                        if i == NIN:
                            act.wait_ge(outs.sem, outs.at(lane.layer, 16 * N_STORES))
                        split_w(i)
                    elif what == "out" and GROUPS[i]["kind"][:3] == "mla":
                        out(GROUPS[i])

                act.wait_ge(uv_mm.sem, uv_mm.at(lane.layer, TILES))
                act.wait_ge(outs.sem, outs.at(lane.layer, 16 * N_STORES))
                act.wait_ge(uv_ok.sem, uv_ok.at(lane.layer, TILES))
                act.wait_ge(qrs_ok.sem, qrs_ok.at(lane.layer, 1))
                for n in range(NBLK):
                    for half in range(2):
                        ks = slice(4 * half, 4 * half + 4)
                        lane.link(act.activation(h_hi[:, ks, blk(n)], mix[:, ks, blk(n)], ACT.Copy), hi_h)
                for c in range(NIN + 2, NCHUNK + 3):
                    if c < NCHUNK:
                        act.wait_ge(z_done.sem, z_done.at(lane.layer, c - 1))
                        split_w(c)
                    k = c - 3 - NIN
                    if k >= 0:
                        if k == 0:
                            act.wait_ge(lo_h.sem, lo_h.at(lane.layer, 4 * NBLK))
                        act.wait_ge(z_dve.sem, z_dve.at(lane.layer, NIN + k + 1))
                        x_square(lane, k)
                assert last or lane.count[act_step.name] == ACT_STEPS

            with act.Fori(0, DEPTH - 1) as L:
                layer(L, False)
            layer(DEPTH - 1, True)

            act.wait_ge(sum_x.sem, sum_x.at(DEPTH, 0))
            for t in range(TILES):
                act.wait_ge(s_yT.sem, 2 * t + 1)
                act.activation(tok[:, t, 0:512], psum[:, 0, :], ACT.Copy).then_inc(s_ya.sem, 1)

        @block.vector
        def _(dve):
            dve.wait_ge(s_const.sem, 32)
            dve.tensor_copy(masks[:], masks_f[:]).then_inc(s_cst.sem, 1)
            dve.wait_ge(s_cst.sem, 4)
            dve.wait_ge(s_cs.sem, 1)
            dve.scalar_tensor_tensor(csil[:], csil[:], 1.0, crow[:], ALU.add, ALU.mult).then_inc(s_cs.sem, 1)
            dve.wait_ge(s_cs.sem, 2)
            dve.tensor_scalar(csil[:], csil[:], 0.5, None, ALU.mult).then_inc(s_cs.sem, 1)
            for t in range(TILES):
                dve.wait_ge(s_xT.sem, 2 * t + 2)
                dve.tensor_copy(x[:, 4:8, tile(t)], psum[:, (2 * t + 1) % 4, :].rearrange("p (k t) -> p k t", k=4))\
                    .then_inc(s_xv.sem, 1)
            dve.wait_ge(s_cT.sem, 1)
            dve.tensor_copy(cT[:], psum[:, 5, 0:P].rearrange("p (k c) -> p k c", k=KD)[:, :, 0:1 + NB])\
                .then_inc(s_cT.sem, 1)
            dve.tensor_copy(fing[:], psum[:, 5, 256:256 + KD]).then_inc(s_cT.sem, 1)
            dve.wait_ge(s_cT.sem, 3)
            def x_mean(lane):
                dve.wait_ge(sum_x.sem, sum_x.at(lane.layer, 1))
                lane.link(dve.tensor_scalar(mean[:], psum[:, 6, 0:TILES], 1.0 / D, EPS, ALU.mult, ALU.add), mean_x)

            def next_vectors(lane):
                dve.wait_ge(small_T.sem, small_T.at(lane.layer, 1))
                lane.link(dve.tensor_copy(vec[:], psum[:, 7, 0:V_ROWS]), small_v)
                lane.link(dve.tensor_copy(convc[:], psum[:, 7, 64:96].rearrange("p (j c) -> p j c", j=2)), small_v)
                dve.wait_ge(vec_in.sem, vec_in.at(lane.layer, 16 * 7))
                lane.link(dve.tensor_scalar(nsink[:], sink[:], -1.0, None, ALU.mult))

            def next_modulation(lane):
                both = mod[:, 0:2].rearrange("p a k c -> p (a k) c")
                lane.link(dve.tensor_tensor(both, both, spread(vec[:, V_BMOD:V_BMOD + 16], 1 + NB), ALU.add))
                lane.link(dve.scalar_tensor_tensor(amul[:], mod[:, 1], 1.0, spread(vec[:, V_G:V_G + KD], 1 + NB),
                                                   ALU.add, ALU.mult), mod_v)

            def x_scale(lane, n, half):
                dve.wait_ge(bc_x.sem, bc_x.at(lane.layer, n + 1))
                xb = x[:, 4 * half:4 * half + 4, blk(n)]
                lane.link(dve.tensor_tensor(xb, xb, psum[:, 6 + n % 2, 0:BLK].unsqueeze(1).broadcast_to([P, 4, BLK]),
                                            ALU.mult), scaled_x)

            before = Lane(dve, -1, dve_before)
            next_vectors(before)
            x_mean(before)
            for i in range(4):
                dve.wait_ge(s_row.sem, i + 1)
                dve.tensor_copy(modrow0[:, 512 * i:512 * i + 512], psum[0:1 + NB, i, :]).then_inc(s_rowc.sem, 1)
            dve.wait_ge(s_mod.sem, 1)
            dve.tensor_copy(mod[:, 0:2].rearrange("p a k c -> p (a k c)"), psum[:, 4, 0:16 * (1 + NB)])\
                .then_inc(s_modc.sem, 1)
            dve.wait_ge(s_modc.sem, 1)
            next_modulation(before)
            dve.sem_inc(z_dve.sem, 1)

            def layer(L, last):
                lane = Lane(dve, L, dve_step)
                tt = lambda *a, sig=None: lane.link(dve.tensor_tensor(*a), sig)
                stt = lambda *a, sig=None: lane.link(dve.scalar_tensor_tensor(*a), sig)
                ts = lambda *a, sig=None: lane.link(dve.tensor_scalar(*a), sig)
                cp = lambda *a, sig=None: lane.link(dve.tensor_copy(*a), sig)

                def split_w(c):
                    _, src, view = w_views(c, last)
                    dve.wait_ge(hi_w.sem, hi_w.at(lane.layer, c + 1))
                    if c >= 2:
                        dve.wait_ge(z_done.sem, z_done.at(lane.layer, c - 1))
                    tt(view(w_lo[c % 2]), src, view(w_hi[c % 2]).bitcast(F32), ALU.subtract, sig=lo_w)

                def rope(out, z, c_, s_, r, sig):
                    tt(out, z, c_, ALU.mult)
                    tt(r, r, s_, ALU.mult)
                    tt(out, out, r, ALU.add, sig=sig)

                def per_sample(ap):
                    return ap[:, SEQ:NTOK].rearrange("p (b t) -> p b t", t=TS)

                split_w(0)
                split_w(1)
                dve.wait_ge(x_out.sem, x_out.at(lane.layer, 0))
                xs = x[:, :, SEQ:NTOK].rearrange("p k (b t) -> p k b t", t=TS)

                def each(ap):
                    return ap.unsqueeze(3).broadcast_to([P, KD, NB, TS])

                def lo(n, half, src, base=0):
                    ks = slice(4 * half, 4 * half + 4)
                    dve.wait_ge(hi_h.sem, hi_h.at(lane.layer, base + 2 * n + half + 1))
                    tt(h_lo[:, ks, blk(n)], src[:, ks, blk(n)], h_hi[:, ks, blk(n)].bitcast(F32), ALU.subtract, sig=lo_h)

                for n in range(NBLK):
                    for half in range(2):
                        x_scale(lane, n, half)
                        if n:
                            lo(n - 1, half, x)
                tt(xs, xs, each(amul[:, :, 1:]), ALU.mult)
                tt(xs, xs, each(mod[:, 0, :, 1:]), ALU.add, sig=h_smp)
                for half in range(2):
                    lo(NBLK - 1, half, x)
                for c in range(NIN):
                    if c + 2 < NIN:
                        split_w(c + 2)
                    pair, j = divmod(c, 2)
                    z = zset(c)
                    dve.wait_ge(z_done.sem, z_done.at(lane.layer, c + 1))
                    if c in ACT_CHUNKS:
                        dve.wait_ge(z_act.sem, z_act.at(lane.layer, ACT_CHUNKS.index(c) + 1))
                    if pair == KV_KR and j == 0:
                        ts(b3(ckvT[:]), z, vec[:, V_KVG:V_KVG + 1], None, ALU.mult, sig=z_dve)
                    elif pair == Q_LAT:
                        ts(b3(cq[:, j, :]), z, vec[:, V_QG + j:V_QG + j + 1], None, ALU.mult, sig=z_dve)
                    elif pair == SK_SV and j == 1:
                        cp(b3(svT[:]), z, sig=z_dve)
                    elif pair in (KV_KR, SK_SV, S_Q):
                        dve.wait_ge(tab_in.sem, tab_in.at(lane.layer, 0 if pair == KV_KR else 16))
                        out = {KV_KR: krT[:], SK_SV: skT[:], S_Q: sqT[:, j, :]}[pair]
                        tt(b3(out), z, b3(tab[:, 0, :]), ALU.mult, sig=z_dve)
                        tt(rot[:], rot[:], tab[:, 1, :], ALU.mult)
                        tt(out, out, rot[:], ALU.add, sig=roped)
                    elif pair in (S_G, M_G0, M_G1):
                        k = {S_G: 6, M_G0: 2, M_G1: 4}[pair] + j
                        stt(b3(mix[:, k, :]), b3(mix[:, k, :]), 1.0, z, ALU.add, ALU.mult, sig=z_dve)
                    elif pair == CV_H:
                        dve.wait_ge(lat_sum.sem, lat_sum.at(lane.layer, 1))
                        cp(b3(mix[:, j, :]), z, sig=z_dve)
                    elif pair == CV_C:
                        up, us = u[:, j, 0:2 + SEQ], u[:, j, 2 + SEQ:].rearrange("p (b t) -> p b t", t=TS + 2)
                        y = mix[:, j, :]
                        if j == 0:
                            dve.wait_ge(svt_T.sem, svt_T.at(lane.layer, 3))
                        lane.link(dve.memset(up[:, 0:2], 0.0))
                        cp(us[:, :, 0:2], convc[:, j, :].rearrange("p (b t) -> p b t", t=2))
                        tt(up[:, 2:2 + 2 * BLK].rearrange("p (n t) -> p n t", t=BLK), z[:, 0:2, :],
                           y[:, 0:2 * BLK].rearrange("p (n t) -> p n t", t=BLK), ALU.mult)
                        tt(up[:, 2 + 2 * BLK:2 + SEQ], z[:, 2, 0:SEQ - 2 * BLK], y[:, 2 * BLK:SEQ], ALU.mult)
                        tt(us[:, :, 2:], z[:, 2, SEQ - 2 * BLK:].rearrange("p (b t) -> p b t", t=TS), per_sample(y),
                           ALU.mult, sig=z_dve)
                        for i in range(3):
                            w = vec[:, V_CONV + 2 * i + j:V_CONV + 2 * i + j + 1]
                            for out, in_ in ((y[:, 0:SEQ], up[:, i:i + SEQ]), (per_sample(y), us[:, :, i:i + TS])):
                                if i == 0:
                                    ts(out, in_, w, None, ALU.mult)
                                else:
                                    stt(out, in_, w, out, ALU.mult, ALU.add)
                        cp(state[:, j, 0:2], up[:, SEQ:SEQ + 2])
                        cp(state[:, j, 2:].rearrange("p (b t) -> p b t", t=2), us[:, :, TS:TS + 2])
                    elif pair == CV_B:
                        tt(b3(mix[:, j, :]), z, b3(mix[:, j, :]), ALU.mult, sig=z_dve)
                    else:
                        r = (rot, svT)[j]
                        stt(b3(r[:]), b3(r[:]), 1.0, z, ALU.add, ALU.mult, sig=z_dve)
                        stt(mix[:, j, :], r[:], 0.5, mix[:, j, :], ALU.mult, ALU.mult, sig=conv_ok if j else None)
                    if c == 2 * SPLIT_AFTER - 1:
                        dve.wait_ge(lat_sum.sem, lat_sum.at(lane.layer, 1))
                        for i, width in enumerate((128, 256)):
                            ts(meanl[:, i, :], psum[:, 6, 16 * i:16 * i + TILES], 1.0 / width, EPS, ALU.mult, ALU.add,
                               sig=lat_mean)
                    if c == 2 * SPLIT_AFTER + 1:
                        for i in range(2):
                            for n in range(NBLK):
                                m = NBLK * i + n
                                dve.wait_ge(lat_bc.sem, lat_bc.at(lane.layer, m + 1))
                                r = psum[:, 6 + m % 2, 0:BLK]
                                if i == 0:
                                    tt(ckvT[:, blk(n)], ckvT[:, blk(n)], r, ALU.mult, sig=lat_ok)
                                else:
                                    tt(cq[:, :, blk(n)], cq[:, :, blk(n)], r.unsqueeze(1).broadcast_to([P, 2, BLK]),
                                       ALU.mult, sig=lat_ok)

                dve.wait_ge(tab_in.sem, tab_in.at(lane.layer, 32))
                dve.wait_ge(z_done.sem, z_done.at(lane.layer, NIN))
                for k in range(2):
                    dve.wait_ge(mq_mm.sem, mq_mm.at(lane.layer, k + 1))
                    cp(mq[:, k], psum[:, 6 + k, :].rearrange("p (h c) -> p h c", h=HEADS), sig=mq_c)
                for m in range(2 * NBLK):
                    n, j = divmod(m, 2)
                    dve.wait_ge(qr_rot.sem, qr_rot.at(lane.layer, m + 1))
                    rope(qr[:, j, blk(n)], psum[:, m % 2, 0:BLK], tab[:, 0, blk(n)], tab[:, 1, blk(n)], rot[:, blk(j)],
                         roped)
                for a, half in enumerate(HALVES):
                    ins = dve.tensor_copy(
                        qrs[half, :, 32 * a:32 * a + 32].rearrange("p b (j t) -> p b j t", j=2),
                        qr[half, :, SEQ:NTOK].rearrange("p j (b t) -> p b j t", t=TS))
                    lane.link(ins, qrs_ok if a else None)
                dve.wait_ge(qa_c.sem, qa_c.at(lane.layer, HEADS * NBLK))
                for a in range(2):
                    cp(qas[:, :, 32 * a:32 * a + 32].rearrange("p b (j t) -> p b j t", j=2),
                       qa[:].rearrange("p (j a) t -> p a j t", a=2)[:, a, :, SEQ:NTOK]
                       .rearrange("p j (b t) -> p b j t", t=TS), sig=qas_ok)

                def maxima(j):
                    rows, nh, w, has_sink = job_shape(j)
                    s = slot_of(j)
                    dve.wait_ge(score.sem, score.at(lane.layer, j + 1))
                    lane.link(dve.tensor_reduce(smax[0:rows, s, 0:nh], s_view(j), AX.X, ALU.max))
                    if not has_sink:
                        ts(nmax[0:rows, s, 0:nh], smax[0:rows, s, 0:nh], -MLA_SCALE, None, ALU.mult, sig=negmax)
                        return
                    h0 = GROUP_OF[j]["jobs"].index(j)
                    stt(nmax[:, s, 0:nh], smax[:, s, 0:nh], -SWA_SCALE, nsink[:, h0:h0 + nh], ALU.mult, ALU.min)
                    tt(esink[:, s, 0:nh], nmax[:, s, 0:nh], sink[:, h0:h0 + nh], ALU.add, sig=negmax)

                def normalise(j):
                    rows, nh, w, has_sink = job_shape(j)
                    s = slot_of(j)
                    dve.wait_ge(expd.sem, expd.at(lane.layer, j + 1))
                    total = psum_p[0:rows, s, 0:nh]
                    if has_sink:
                        tt(total, total, esink[:, s, 0:nh], ALU.add)
                    lane.link(dve.reciprocal(rinv[0:rows, s, 0:nh], total))
                    if nh == 1:
                        ts(p_view(j)[:, 0, :], p_view(j)[:, 0, :], rinv[0:rows, s, 0:1], None, ALU.mult, sig=p_ok)
                    else:
                        tt(p_view(j), p_view(j), spread(rinv[:, s, :], w), ALU.mult, sig=p_ok)

                def gate_mla(t):
                    g = mix[:, 2:6, tile(t)]
                    stt(g, psum[:, 7, :].rearrange("p (h t) -> p h t", h=HEADS), 0.5, g, ALU.mult, ALU.mult, sig=uv_ok)

                def gate_swa(g):
                    dve.wait_ge(pv.sem, pv.at(lane.layer, g["units"][-1] + 1))
                    for kv, half in enumerate(HALVES):
                        out = mix[half, 6:8, tile(g["idx"])]
                        in_ = psum[half, 6, 256 * kv:256 * kv + 256].rearrange("p (g t) -> p g t", g=2)
                        stt(out, in_, 0.5, out, ALU.mult, ALU.mult, sig=swa_ok if kv else None)

                n_uv = turned_rows = 0
                for what, i in STEPS:
                    if what == "split_keys":
                        for m, (k, hi, lo_) in enumerate(((ckvT, ckv_hi, ckv_lo), (krT, kr_hi, kr_lo))):
                            dve.wait_ge(key_hi.sem, key_hi.at(lane.layer, m + 1))
                            tt(lo_[:], k[:], hi[:].bitcast(F32), ALU.subtract, sig=key_lo)
                    elif what == "split_q":
                        dve.wait_ge(q_hi.sem, q_hi.at(lane.layer, i - SPLIT_FROM + 1))
                        if i > SPLIT_FROM:
                            dve.wait_ge(q_st.sem, q_st.at(lane.layer, i - SPLIT_FROM))
                        tt(qa_lo[i % 2][:], qa[:, :, tile(i)], qa_hi[i % 2][:].bitcast(F32), ALU.subtract)
                        for a, half in enumerate(HALVES):
                            tt(qr_lo[half], qr[half, :, tile(i)], qst[i % 2][half, a].bitcast(F32), ALU.subtract,
                               sig=q_lo if a else None)
                    elif what == "maxima":
                        maxima(i)
                    elif what == "norm":
                        normalise(i)
                    elif what == "split":
                        split_w(i)
                    elif what == "copy" and COPIER[i] == 1:
                        dve.wait_ge(pt_T.sem, pt_T.at(lane.layer, i + 1))
                        if i >= 3:
                            dve.wait_ge(pv.sem, pv.at(lane.layer, i - 2))
                        w = 320 if UNIT_OF[i]["kind"] == "mla_s" else 512
                        cp(pT[:, i % 3, 0:w], psum[:, 5, 0:w], sig=pt_c[1])
                    elif what == "out" and GROUPS[i]["kind"][:3] == "swa":
                        gate_swa(GROUPS[i])
                    elif what == "up":
                        n_uv += 1
                        dve.wait_ge(uv_mm.sem, uv_mm.at(lane.layer, n_uv))
                        gate_mla(n_uv - 1)
                    elif what == "mod" and (i in GATE_AT or not last):
                        if i in GATE_AT:
                            dve.wait_ge(gate_mm.sem, gate_mm.at(lane.layer, GATE_AT[i] + 1))
                        else:
                            dve.wait_ge(next_mm.sem, next_mm.at(lane.layer, NEXT_AT[i] + 1))
                        if GATE_AT.get(i) == 0:
                            dve.wait_ge(outs.sem, outs.at(lane.layer, 16 * N_STORES))
                        cp(modrow[:], psum[0:1 + NB, 7, 0:256], sig=row_c)
                    elif what == "modT" and (i in GATE_AT or not last):
                        turned_rows += 1
                        dve.wait_ge(row_T.sem, row_T.at(lane.layer, turned_rows))
                        sums = psum[:, 7, 0:2 * (1 + NB)].rearrange("p (k c) -> p k c", k=2)
                        if i in GATE_AT:
                            m = GATE_AT[i]
                            tt(mod[:, 2, 2 * m:2 * m + 2], sums,
                               spread(vec[:, V_BMOD + 16 + 2 * m:V_BMOD + 18 + 2 * m], 1 + NB), ALU.add, sig=gate_c)
                        else:
                            m = NEXT_AT[i]
                            cp(mod[:, m // 4, 2 * (m % 4):2 * (m % 4) + 2], sums, sig=next_c)

                for n in range(NBLK):
                    for half in range(2):
                        lo(n, half, mix, 2 * NBLK)
                for c in range(NIN, NCHUNK):
                    if c + 2 < NCHUNK:
                        split_w(c + 2)
                    k, z = c - NIN, zset(c)
                    dve.wait_ge(z_done.sem, z_done.at(lane.layer, c + 1))
                    if k % 4 == 0:
                        dve.wait_ge(x_in[k // 4].sem, x_in[k // 4].at(lane.layer, 16))
                    gate = mod[:, 2, k, 0:1]
                    xk = x[:, k, :]
                    two = xk[:, 0:2 * BLK].rearrange("p (n t) -> p n t", t=BLK)
                    stt(two, z[:, 0:2, :], gate, two, ALU.mult, ALU.add)
                    stt(xk[:, 2 * BLK:SEQ], z[:, 2, 0:SEQ - 2 * BLK], gate, xk[:, 2 * BLK:SEQ], ALU.mult, ALU.add)
                    tmp = rot[:, 0:P].rearrange("p (b t) -> p b t", t=TS)
                    tt(tmp, z[:, 2, SEQ - 2 * BLK:].rearrange("p (b t) -> p b t", t=TS), spread(mod[:, 2, k, 1:], TS),
                       ALU.mult)
                    tt(per_sample(xk), per_sample(xk), tmp, ALU.add, sig=z_dve)
                    if c == NCHUNK - 2 and not last:
                        next_vectors(lane)
                        next_modulation(lane)
                x_mean(lane)
                assert last or lane.count[dve_step.name] == DVE_STEPS

            with dve.Fori(0, DEPTH - 1) as L:
                layer(L, False)
            layer(DEPTH - 1, True)

            for n in range(NBLK):
                dve.wait_ge(bc_x.sem, bc_x.at(DEPTH, n + 1))
                for k in range(KD):
                    ins = dve.scalar_tensor_tensor(x[:, k, blk(n)], x[:, k, blk(n)], fing[:, k:k + 1],
                                                   psum[:, 6 + n % 2, 0:BLK], ALU.mult, ALU.mult)
                    if k % 4 == 3:
                        ins.then_inc(scaled_x.sem, 1)
            dve.wait_ge(sum_x.sem, sum_x.at(DEPTH, 0))
            for t in range(TILES):
                dve.wait_ge(s_yT.sem, 2 * t + 2)
                dve.tensor_copy(tok[:, t, 512:1024], psum[:, 2, :]).then_inc(s_yv.sem, 1)


_OUTS = [("y_prompt", (1, 1024, 1024)), ("y_sample", (8, 16, 1024)),
         ("conv_state_prompt", (2, 1, 2, 256)), ("conv_state_sample", (2, 8, 2, 256)),
         ("mla_ckv_prompt", (2, 1, 1024, 128)), ("mla_ckv_sample", (2, 8, 16, 128)),
         ("mla_krope_prompt", (2, 1, 1024, 64)), ("mla_krope_sample", (2, 8, 16, 64)),
         ("swa_k_prompt", (2, 1, 64, 2, 64)), ("swa_k_sample", (2, 8, 16, 2, 64)),
         ("swa_v_prompt", (2, 1, 64, 2, 64)), ("swa_v_sample", (2, 8, 16, 2, 64))]
_INS = ["x_prompt", "x_sample", "c_prompt", "c_sample", "cache_conv", "cache_mla_ckv", "cache_mla_krope",
        "cache_swa_k", "cache_swa_v", "norm_g", "w_mod", "b_mod", "w_in", "conv_w", "q_norm_g", "kv_norm_g",
        "w_uq", "w_ukv", "swa_sink", "w_out", "final_norm_g"]


def constants():
    masks = np.zeros((8, 1664), np.float32)
    for b in range(8):
        masks[b, 16 * b:16 * b + 16] = 1
        masks[b, 1152 + 64 * b:1152 + 64 * b + 64] = 1
        own = np.zeros(640, bool)
        own[64 * b:64 * b + 64] = True
        own[512 + 16 * b:512 + 16 * b + 16] = True
        masks[b, 128:768] = np.where(own, 0, NEG)
    masks[0, 768:832] = 1
    masks[1, 832:896] = 1
    masks[0, 896:896 + 64] = NEG
    masks[0, 896 + 192:1152] = NEG
    masks[1, 896:896 + 128] = NEG
    pos = np.concatenate([np.arange(1024), np.tile(512 + np.arange(16), 8)]).astype(np.float32)
    rope = np.zeros((2, 128, 2, 1152), np.float32)
    for i, theta in enumerate((10000.0, 150000.0)):
        inv = np.float32(theta) ** (-np.arange(32, dtype=np.float32) / np.float32(32))
        ang = (pos[None, :] * inv[:, None]).astype(np.float32)
        cos, sin = np.cos(ang), np.sin(ang)
        rope[i, :, 0] = np.tile(cos, (4, 1))
        rope[i, :, 1] = np.concatenate([-sin, sin, -sin, sin])
    return {"c_ident": np.eye(128, dtype=np.float32), "c_masks": masks,
            "c_rope": rope}


def kernel(**inputs):
    import concourse.bacc as bacc
    from concourse.bass_utils import run_bass_kernel_spmd

    nc = bacc.Bacc("TRN2", target_bir_lowering=False, num_devices=1)
    arrays, io = {}, {}
    named = {n: np.ascontiguousarray(inputs[n]) for n in _INS}
    named.update(constants())
    for name, a in named.items():
        arrays[f"in_{name}"] = a
        io[name] = nc.dram_tensor(f"in_{name}", a.shape, mybir.dt.from_np(a.dtype), kind="ExternalInput").ap()
    for name, shape in _OUTS:
        io[name] = nc.dram_tensor(f"out_{name}", shape, F32, kind="ExternalOutput").ap()
    build(nc, io)
    r = run_bass_kernel_spmd(nc, [arrays], core_ids=[0])
    return tuple(r.results[0][f"out_{name}"] for name, _ in _OUTS)
```
